# Optimizing a Trainium2 kernel written in Bass

```python
import functools
import jax, jax.numpy as jnp
from jax import lax
import numpy as np

D_MODEL = 1024
BATCH = 1
SEQ = 512
DEPTH = 2
DEC_BATCH = 8
DEC_SEQ = 8
PAST_LEN = 256
PAGE_SIZE = 128

N_HEADS = 8
N_KV_HEADS = 4
HEAD_DIM = 64
ROT_DIM = HEAD_DIM // 4
ROPE_THETA = 500000.0
IDX_HEADS = 4
IDX_DIM = 64
IDX_ROT_DIM = IDX_DIM // 4
TOPK_MAX = 256
Q_BLOCK = 128
GLA_HEADS = 4
GLA_DK = 64
GLA_DV = 128
GLA_GATE_RANK = 16
GLA_TAU = 16.0
GLA_CHUNK = 64
D_FF = ((8 * D_MODEL + 3 * 256 - 1) // (3 * 256)) * 256
EPS = 1e-6

ATTN_W = N_HEADS * HEAD_DIM
KV_W = N_KV_HEADS * HEAD_DIM
GLA_K_W = GLA_HEADS * GLA_DK
GLA_V_W = GLA_HEADS * GLA_DV
IN_SPLITS = (ATTN_W, KV_W, KV_W, IDX_HEADS * IDX_DIM, IDX_DIM, IDX_HEADS,
             GLA_K_W, GLA_K_W, GLA_V_W, GLA_GATE_RANK, GLA_V_W, D_MODEL, D_MODEL)
N_IN = sum(IN_SPLITS)

kernel_name = 'hybrid_dsa_gla_decode_step'

def rms_norm(x, g):
    x32 = x.astype(jnp.float32)
    y = x32 * lax.rsqrt(jnp.mean(x32 * x32, axis=-1, keepdims=True) + EPS)
    return (y * g.astype(jnp.float32)).astype(x.dtype)

def partial_rope(x, pos, rot_dim):
    half = rot_dim // 2
    inv = jnp.power(ROPE_THETA, -jnp.arange(half, dtype=jnp.float32) * 2.0 / rot_dim)
    ang = pos.astype(jnp.float32)[:, None] * inv[None, :]
    cos = jnp.cos(ang)[None, :, None, :]
    sin = jnp.sin(ang)[None, :, None, :]
    xr = x[..., :rot_dim].astype(jnp.float32)
    x1, x2 = xr[..., :half], xr[..., half:]
    rot = jnp.concatenate([x1 * cos - x2 * sin, x2 * cos + x1 * sin], axis=-1).astype(x.dtype)
    return jnp.concatenate([rot, x[..., rot_dim:]], axis=-1)

def project_inputs(xn, pos, w_in, q_g, k_g, kidx_g, gla_wa2, gla_ba):
    B, T, _ = xn.shape
    h = xn @ w_in
    offs = np.cumsum(IN_SPLITS)[:-1].tolist()
    q, k, v, qi, ki, wi, gq, gk, gv, ga, gr, gate_a, gate_b = jnp.split(h, offs, axis=-1)
    q = partial_rope(rms_norm(q.reshape(B, T, N_HEADS, HEAD_DIM), q_g), pos, ROT_DIM)
    k = partial_rope(rms_norm(k.reshape(B, T, N_KV_HEADS, HEAD_DIM), k_g), pos, ROT_DIM)
    v = v.reshape(B, T, N_KV_HEADS, HEAD_DIM)
    qi = partial_rope(qi.reshape(B, T, IDX_HEADS, IDX_DIM), pos, IDX_ROT_DIM)
    ki = partial_rope(rms_norm(ki, kidx_g)[:, :, None, :], pos, IDX_ROT_DIM)[:, :, 0, :]
    wi = wi * (IDX_HEADS ** -0.5 * IDX_DIM ** -0.5)
    gq = gq.reshape(B, T, GLA_HEADS, GLA_DK) * GLA_DK ** -0.5
    gk = gk.reshape(B, T, GLA_HEADS, GLA_DK)
    gv = gv.reshape(B, T, GLA_HEADS, GLA_DV)
    log_a = jax.nn.log_sigmoid((ga @ gla_wa2 + gla_ba).astype(jnp.float32)) / GLA_TAU
    log_a = log_a.reshape(B, T, GLA_HEADS, GLA_DK)
    return q, k, v, qi, ki, wi, gq, gk, gv, log_a, gr, gate_a, gate_b

def gather_rows(k_all, v_all, idx):
    take = jax.vmap(lambda a, i: a[i])
    return take(k_all, idx), take(v_all, idx)

def gather_paged(cache_k, cache_v, layer, page_table, k_new, v_new, idx):
    ps = cache_k.shape[2]
    past_len = page_table.shape[1] * ps
    t_new = k_new.shape[1]
    is_past = (idx < past_len)[..., None, None]
    pidx = jnp.minimum(idx, past_len - 1)
    page = jax.vmap(lambda pt, i: pt[i])(page_table, pidx // ps)
    off = pidx % ps
    nidx = jnp.clip(idx - past_len, 0, t_new - 1)
    take = jax.vmap(lambda a, i: a[i])
    k_sel = jnp.where(is_past, cache_k[layer, page, off], take(k_new, nidx))
    v_sel = jnp.where(is_past, cache_v[layer, page, off], take(v_new, nidx))
    return k_sel, v_sel

def dsa_attention(q, qi, wi, q_pos, ki_all, topk, gather_kv):
    B, T = q.shape[:2]
    L = ki_all.shape[1]
    qb = min(Q_BLOCK, T)
    nb = -(-T // qb)
    pad = nb * qb - T

    def blocks(a):
        a = jnp.pad(a, [(0, 0), (0, pad)] + [(0, 0)] * (a.ndim - 2))
        return jnp.moveaxis(a.reshape((B, nb, qb) + a.shape[2:]), 1, 0)

    pos_b = jnp.pad(q_pos, (0, pad), mode='edge').reshape(nb, qb)
    k_pos = jnp.arange(L, dtype=jnp.int32)
    ki32 = ki_all.astype(jnp.float32)

    def one_block(args):
        qblk, qiblk, wiblk, pb = args
        s = jnp.einsum('bqhd,bsd->bqhs', qiblk.astype(jnp.float32), ki32)
        score = jnp.einsum('bqh,bqhs->bqs', wiblk.astype(jnp.float32), jax.nn.relu(s))
        causal = k_pos[None, :] <= pb[:, None]
        score = jnp.where(causal[None], score, -jnp.inf)
        _, idx = lax.top_k(score, topk)
        valid = idx <= pb[None, :, None]
        k_sel, v_sel = gather_kv(idx)
        qg = qblk.reshape(B, qb, N_KV_HEADS, N_HEADS // N_KV_HEADS, HEAD_DIM).astype(jnp.float32)
        logits = jnp.einsum('bqhgd,bqkhd->bqhgk', qg, k_sel.astype(jnp.float32)) * HEAD_DIM ** -0.5
        logits = jnp.where(valid[:, :, None, None, :], logits, -jnp.inf)
        p = jax.nn.softmax(logits, axis=-1)
        o = jnp.einsum('bqhgk,bqkhd->bqhgd', p, v_sel.astype(jnp.float32))
        return o.reshape(B, qb, ATTN_W).astype(q.dtype)

    out = lax.map(one_block, (blocks(q), blocks(qi), blocks(wi), pos_b))
    return jnp.moveaxis(out, 0, 1).reshape(B, nb * qb, ATTN_W)[:, :T]

def gla_recurrence(q, k, v, log_a, s0):
    B, T, H, _ = q.shape
    c = min(GLA_CHUNK, T)
    nc = -(-T // c)
    pad = nc * c - T

    def chunks(a):
        a = jnp.pad(a.astype(jnp.float32), [(0, 0), (0, pad), (0, 0), (0, 0)])
        return a.reshape(B, nc, c, H, a.shape[-1]).transpose(1, 0, 3, 2, 4)

    causal = jnp.tril(jnp.ones((c, c), dtype=bool))

    def step(S, inp):
        qc, kc, vc, lac = inp
        b = jnp.cumsum(lac, axis=2)
        o = jnp.einsum('bhtd,bhde->bhte', qc * jnp.exp(b), S)
        diff = b[:, :, :, None, :] - b[:, :, None, :, :]
        decay = jnp.exp(jnp.where(causal[:, :, None], diff, -jnp.inf))
        attn = jnp.einsum('bhtd,bhsd,bhtsd->bhts', qc, kc, decay)
        o = o + jnp.einsum('bhts,bhse->bhte', attn, vc)
        b_last = b[:, :, -1:, :]
        S = jnp.exp(b_last[:, :, 0, :])[..., None] * S + jnp.einsum(
            'bhsd,bhse->bhde', kc * jnp.exp(b_last - b), vc)
        return S, o

    S, o = lax.scan(step, s0.astype(jnp.float32), (chunks(q), chunks(k), chunks(v), chunks(log_a)))
    o = o.transpose(1, 0, 3, 2, 4).reshape(B, nc * c, H, GLA_DV)[:, :T]
    return o.astype(q.dtype), S.astype(s0.dtype)

def merge_and_ffn(x, attn_o, gla_o, gr, gate_a, gate_b, gla_on_g, w_oa, w_ob, w_o,
                  norm2_g, w_gu, w_down):
    B, T, _ = x.shape
    g_out = rms_norm(gla_o, gla_on_g).reshape(B, T, GLA_V_W) * jax.nn.silu(gr)
    merged = jax.nn.sigmoid(gate_a) * (attn_o @ w_oa) + jax.nn.sigmoid(gate_b) * (g_out @ w_ob)
    x = x + merged @ w_o
    hn = rms_norm(x, norm2_g)
    gt, up = jnp.split(hn @ w_gu, 2, axis=-1)
    return x + (jax.nn.silu(gt) * up) @ w_down

def setup_inputs(seed: int = 0) -> dict:
    key = jax.random.key(seed)
    ks = jax.random.split(key, 24)
    f32 = jnp.float32
    n_pages = PAST_LEN // PAGE_SIZE
    n_used = DEC_BATCH * n_pages
    n_pool = (5 * n_used + 3) // 4

    def nrm(k, shape, scale):
        return jax.random.normal(k, shape, f32) * scale

    page_table = jax.random.permutation(ks[0], n_pool)[:n_used].reshape(DEC_BATCH, n_pages).astype(jnp.int32)
    return {
        'x_prompt': nrm(ks[1], (BATCH, SEQ, D_MODEL), 1.0),
        'x_sample': nrm(ks[2], (DEC_BATCH, DEC_SEQ, D_MODEL), 1.0),
        'cache_k': nrm(ks[3], (DEPTH, n_pool, PAGE_SIZE, N_KV_HEADS, HEAD_DIM), 1.0),
        'cache_v': nrm(ks[4], (DEPTH, n_pool, PAGE_SIZE, N_KV_HEADS, HEAD_DIM), 1.0),
        'cache_kidx': nrm(ks[5], (DEPTH, n_pool, PAGE_SIZE, IDX_DIM), 1.0),
        'state_gla': nrm(ks[6], (DEPTH, DEC_BATCH, GLA_HEADS, GLA_DK, GLA_DV), 0.3),
        'page_table': page_table,
        'norm1_g': 1.0 + nrm(ks[7], (DEPTH, D_MODEL), 0.02),
        'w_in': nrm(ks[8], (DEPTH, D_MODEL, N_IN), D_MODEL ** -0.5),
        'q_norm_g': 1.0 + nrm(ks[9], (DEPTH, HEAD_DIM), 0.02),
        'k_norm_g': 1.0 + nrm(ks[10], (DEPTH, HEAD_DIM), 0.02),
        'kidx_norm_g': 1.0 + nrm(ks[11], (DEPTH, IDX_DIM), 0.02),
        'gla_wa2': nrm(ks[12], (DEPTH, GLA_GATE_RANK, GLA_K_W), GLA_GATE_RANK ** -0.5),
        'gla_ba': nrm(ks[13], (DEPTH, GLA_K_W), 0.02),
        'gla_onorm_g': 1.0 + nrm(ks[14], (DEPTH, GLA_DV), 0.02),
        'w_oa': nrm(ks[15], (DEPTH, ATTN_W, D_MODEL), ATTN_W ** -0.5),
        'w_ob': nrm(ks[16], (DEPTH, GLA_V_W, D_MODEL), GLA_V_W ** -0.5),
        'w_o': nrm(ks[17], (DEPTH, D_MODEL, D_MODEL), D_MODEL ** -0.5),
        'norm2_g': 1.0 + nrm(ks[18], (DEPTH, D_MODEL), 0.02),
        'w_ffn_gu': nrm(ks[19], (DEPTH, D_MODEL, 2 * D_FF), D_MODEL ** -0.5),
        'w_ffn_down': nrm(ks[20], (DEPTH, D_FF, D_MODEL), D_FF ** -0.5),
    }

def reference(x_prompt, x_sample, cache_k, cache_v, cache_kidx, state_gla, page_table,
              norm1_g, w_in, q_norm_g, k_norm_g, kidx_norm_g, gla_wa2, gla_ba, gla_onorm_g,
              w_oa, w_ob, w_o, norm2_g, w_ffn_gu, w_ffn_down):
    B, S, _ = x_prompt.shape
    Bd, Td, _ = x_sample.shape
    ps = cache_k.shape[2]
    past_len = page_table.shape[1] * ps
    pos_p = jnp.arange(S, dtype=jnp.int32)
    pos_s = past_len + jnp.arange(Td, dtype=jnp.int32)
    topk_p = min(TOPK_MAX, S // 4)
    topk_s = min(TOPK_MAX, (past_len + Td) // 4)

    hp, hs = x_prompt, x_sample
    nk_p, nv_p, nki_p, ns_p = [], [], [], []
    nk_s, nv_s, nki_s, ns_s = [], [], [], []
    for l in range(DEPTH):
        proj = functools.partial(project_inputs, w_in=w_in[l], q_g=q_norm_g[l], k_g=k_norm_g[l],
                                 kidx_g=kidx_norm_g[l], gla_wa2=gla_wa2[l], gla_ba=gla_ba[l])
        tail = functools.partial(merge_and_ffn, gla_on_g=gla_onorm_g[l], w_oa=w_oa[l], w_ob=w_ob[l],
                                 w_o=w_o[l], norm2_g=norm2_g[l], w_gu=w_ffn_gu[l], w_down=w_ffn_down[l])

        q, k, v, qi, ki, wi, gq, gk, gv, la, gr, ga, gb = proj(rms_norm(hp, norm1_g[l]), pos_p)
        attn_o = dsa_attention(q, qi, wi, pos_p, ki, topk_p, functools.partial(gather_rows, k, v))
        gla_o, s_fin = gla_recurrence(gq, gk, gv, la,
                                      jnp.zeros((B, GLA_HEADS, GLA_DK, GLA_DV), hp.dtype))
        hp = tail(hp, attn_o, gla_o, gr, ga, gb)
        nk_p.append(k); nv_p.append(v); nki_p.append(ki); ns_p.append(s_fin)

        q, k, v, qi, ki, wi, gq, gk, gv, la, gr, ga, gb = proj(rms_norm(hs, norm1_g[l]), pos_s)
        ki_all = jnp.concatenate(
            [cache_kidx[l, page_table].reshape(Bd, past_len, IDX_DIM).astype(ki.dtype), ki], axis=1)
        gather = functools.partial(gather_paged, cache_k, cache_v, l, page_table, k, v)
        attn_o = dsa_attention(q, qi, wi, pos_s, ki_all, topk_s, gather)
        gla_o, s_new = gla_recurrence(gq, gk, gv, la, state_gla[l])
        hs = tail(hs, attn_o, gla_o, gr, ga, gb)
        nk_s.append(k); nv_s.append(v); nki_s.append(ki); ns_s.append(s_new)

    y_prompt, y_sample = hp, hs
    new_k_prompt, new_v_prompt = jnp.stack(nk_p), jnp.stack(nv_p)
    new_kidx_prompt, new_gla_prompt = jnp.stack(nki_p), jnp.stack(ns_p)
    new_k_sample, new_v_sample = jnp.stack(nk_s), jnp.stack(nv_s)
    new_kidx_sample, new_gla_sample = jnp.stack(nki_s), jnp.stack(ns_s)
    return (y_prompt, y_sample, new_k_prompt, new_v_prompt, new_kidx_prompt, new_gla_prompt,
            new_k_sample, new_v_sample, new_kidx_sample, new_gla_sample)


_drawn_inputs = setup_inputs


def setup_inputs(seed=0):
    import zlib

    import numpy as np

    out = dict(_drawn_inputs(seed))
    spreads = {}
    factors = {'q_norm_g': 8.0, 'gla_ba': 6.086, 'gla_onorm_g': 4.442}
    for name, (base, spread) in spreads.items():
        noise = np.random.default_rng([zlib.crc32(name.encode()), seed]).standard_normal(out[name].shape)
        drawn = base * np.exp(spread * noise) if base else spread * noise
        out[name] = __import__('jax').numpy.asarray(drawn.astype(out[name].dtype))
    for name, factor in factors.items():
        out[name] = (out[name] * factor).astype(out[name].dtype)
    return out
```

```python
from contextlib import ExitStack

import numpy as np

import concourse.bass as bass
from concourse import mybir

F32 = mybir.dt.float32
F32R = mybir.dt.float32r
BF16 = mybir.dt.bfloat16
I32 = mybir.dt.int32
U32 = mybir.dt.uint32
ALU = mybir.AluOpType
ACT = mybir.ActivationFunctionType
AX_X = mybir.AxisListType.X

P = 128
DEPTH = 2
D_MODEL = 1024
SEQ = 512
DEC_BATCH = 8
DEC_SEQ = 8
NS = DEC_BATCH * DEC_SEQ
NT = SEQ + NS
NTILE = 5
PAGE = 128
N_PAGES = 2
PAST = PAGE * N_PAGES
N_POOL = 20
N_HEADS = 8
N_KV = 4
HD = 64
ROT = HD // 4
HALF_ROT = ROT // 2
THETA = 500000.0
IDX_HEADS = 4
ID = 64
TOPK_PROMPT = SEQ // 4
TOPK_SAMPLE = (PAST + DEC_SEQ) // 4
GH = 4
DK = 64
DV = 128
RANK = 16
TAU = 16.0
CHUNK = 32
D_FF = 2816
EPS = 1e-6
KD = D_MODEL // P
HALF = NT // 2
ATTN_W, KV_W, IDX_W = N_HEADS * HD, N_KV * HD, IDX_HEADS * ID
GK_W, GV_W = GH * DK, GH * DV
SPLITS = (ATTN_W, KV_W, KV_W, IDX_W, ID, IDX_HEADS, GK_W, GK_W, GV_W, RANK, GV_W, D_MODEL, D_MODEL)
OFFS = [sum(SPLITS[:i]) for i in range(len(SPLITS))]
O_Q, O_K, O_V, O_QI, O_KI, O_WI, O_GQ, O_GK, O_GV, O_GA, O_GR, O_GTA, O_GTB = OFFS
N_IN = sum(SPLITS)
MISC_KI = 32
MISC_WI = MISC_KI + ID
NEW_KEYS = PAST + NS
PAD_TOP = -TOPK_SAMPLE % 8
SAMPLE_W = NEW_KEYS + PAD_TOP
MASKED = -1e30
TAKEN = -3e38
IDX_SCALE = IDX_HEADS ** -0.5 * ID ** -0.5
FF_TILES = D_FF // P
FF_PARTS = (8, 8, 6)
N_CHUNK = SEQ // CHUNK
RAW_RING = 3


def tile_rows(t):
    return P if t < 4 else NS


def token_slice(t):
    return slice(t * P, t * P + tile_rows(t))


def bcast(ap, axis, n):
    dims = [list(d) for d in ap.ap]
    dims.insert(axis, [0, n])
    return bass.AP(ap.tensor, ap.offset, dims)


CONSTS = {}


def const_layout():
    at = 0
    for name, w in (("ident", P), ("chunk_sum", P), ("sample_sum", NS), ("tri", P), ("own_new", NS),
                    ("cos", NTILE * ROT), ("sin", NTILE * ROT), ("batch_rows", DEC_BATCH),
                    ("head_rows", IDX_HEADS), ("spread", 2 * P), ("gather", 2 * NS), ("repeat", 8 * NS)):
        CONSTS[name] = (at, at + w)
        at += w
    return at


CONST_W = const_layout()
KEPT_W = CONSTS["repeat"][0]


def const_array():
    c = np.zeros((P, CONST_W), np.float32)

    def put(name, a):
        lo, hi = CONSTS[name]
        a = a.reshape(a.shape[0], -1)
        assert a.shape[1] == hi - lo
        c[:a.shape[0], lo:hi] = a

    i = np.arange(P)
    put("ident", np.eye(P, dtype=np.float32))
    put("chunk_sum", ((i[:, None] // CHUNK == i[None] // CHUNK) & (i[:, None] <= i[None])) / np.float32(TAU))
    s = np.arange(NS)
    put("sample_sum", ((s[:, None] // DEC_SEQ == s[None] // DEC_SEQ) & (s[:, None] <= s[None])) / np.float32(TAU))
    put("tri", np.where(i[None] <= i[:, None], 0, MASKED).astype(np.float32))
    put("own_new", np.where((s[:, None] // DEC_SEQ == s[None] // DEC_SEQ) & (s[None] <= s[:, None]), 0,
                            MASKED).astype(np.float32))
    inv = np.power(np.float32(THETA), -np.arange(HALF_ROT, dtype=np.float32) * np.float32(2.0) / np.float32(ROT))
    pos = np.zeros((P, NTILE), np.float32)
    pos[:, :4] = i[:, None] + P * np.arange(4)[None]
    pos[:NS, 4] = PAST + s % DEC_SEQ
    ang = pos[:, :, None] * inv.astype(np.float32)[None, None]
    cos, sin = np.cos(ang).astype(np.float32), np.sin(ang).astype(np.float32)
    put("cos", np.concatenate([cos, cos], -1))
    put("sin", np.concatenate([-sin, sin], -1))
    put("batch_rows", (s[:, None] // DEC_SEQ == np.arange(DEC_BATCH)[None]).astype(np.float32))
    rb, rh, rt = i // 32, i // 8 % 4, i % 8
    put("head_rows", (rh[:, None] == np.arange(IDX_HEADS)[None]).astype(np.float32))
    sp = np.stack([(s[:, None] == (g * 4 + rb) * 8 + rt) for g in range(2)], 1).astype(np.float32)
    put("spread", sp)
    put("gather", np.ascontiguousarray(sp.transpose(2, 1, 0)))
    put("repeat", np.stack([(s[:, None] == b * 8 + s[None] % 8) for b in range(DEC_BATCH)], 1).astype(np.float32))
    return c


def make_panels():
    out = []
    for kind, off, n in (("q", O_Q, 4), ("k", O_K, 2), ("v", O_V, 2), ("qi", O_QI, 2)):
        out += [(kind, i, [("w_in", 0, KD, off + i * P, P, 0)]) for i in range(n)]
    out.append(("misc", 0, [("w_in", 0, KD, O_GA, MISC_KI, 0), ("w_in", 0, KD, O_KI, P - MISC_KI, MISC_KI)]))
    for kind, off, n in (("gq", O_GQ, 2), ("gk", O_GK, 2), ("gv", O_GV, 4), ("gr", O_GR, 4),
                         ("gta", O_GTA, 8), ("gtb", O_GTB, 8)):
        out += [(kind, i, [("w_in", 0, KD, off + i * P, P, 0)]) for i in range(n)]
    for j in range(KD):
        out.append(("oab", j, [("w_oa", 0, 4, j * P, P, 0), ("w_ob", 0, 4, j * P, P, 4 * P)]))
    for j in range(KD):
        out.append(("o", j, [("w_o", 0, KD, j * P, P, 0)]))
    first = 0
    for part, n in enumerate(FF_PARTS):
        for i in range(first, first + n):
            out.append(("gate", (part, i), [("w_ffn_gu", 0, KD, i * P, P, 0)]))
            out.append(("up", (part, i), [("w_ffn_gu", 0, KD, D_FF + i * P, P, 0)]))
        for m in range(KD):
            out.append(("down", (part, m), [("w_ffn_down", first * P, n, m * P, P, 0)]))
        first += n
    return out


PANELS = make_panels()
N_PANELS = len(PANELS)
assert N_PANELS % RAW_RING == 0
STAGED = ("q", "k", "v", "qi", "misc", "gv")
RAW_READY = []
_count = [0] * RAW_RING
for _p, (_, _, _parts) in enumerate(PANELS):
    _count[_p % RAW_RING] += len(_parts)
    RAW_READY.append(_count[_p % RAW_RING])
SMALL_LOADS = 8


class Plan:

    def __init__(self):
        self.steps = []
        self.uses = {}
        self.per_bank = [0] * 6
        self.slot_keys = []
        self.groups = {}
        n = 0
        for p, (kind, idx, parts) in enumerate(PANELS):
            self.groups[p] = list(range(n, n + (2 if kind == "oab" else 1)))
            n += len(self.groups[p])
        self.n_groups = n
        self.stage_use = {}
        self.stage_release = []
        self.gate_tmp_use = {}
        self.gate_tmp_release = []
        self.split_use = {}
        self.build()

    def open(self, key, bank):
        self.uses[key] = (bank, self.per_bank[bank])
        self.per_bank[bank] += 1

    def stage(self, key, release):
        self.stage_use[key] = len(self.stage_release)
        self.stage_release.append(release)

    def gate_tmp(self, key, release):
        self.gate_tmp_use[key] = len(self.gate_tmp_release)
        self.gate_tmp_release.append(release)

    def split(self, key):
        self.split_use[key] = len(self.split_use)

    def add(self, *step):
        self.steps.append(step)

    def panel(self, p):
        kind, idx, _ = PANELS[p]
        for g in self.groups[p]:
            self.open(("g", g), 4 + g % 2)
        self.add("panel", p)
        g = self.groups[p][0]
        if kind == "gr":
            self.gate_tmp(("gr", idx), ("bank_free", ("g", g)))
        if kind == "gate":
            self.gate_tmp(("gate", idx), ("bank_free", ("g", g)))
        if kind in STAGED:
            self.stage(("row", p), ("bank_ready", ("rowY", p)))
        if kind == "oab":
            self.split(("merge", idx))
        if kind == "up":
            self.split(("ff", idx))

    def stat(self, norm, kt):
        if kt == 0:
            self.open(("stat", norm, 0), 0)
            self.open(("stat", norm, 1), 1)
        last = kt == KD - 1
        self.stage(("stat", norm, kt), ("bank_ready", ("stat", norm, 1)) if last else ("stage_read", self.n_read + 1))
        self.n_read += not last
        self.add("stat", norm, kt)

    def norm(self, norm):
        self.add("norm", norm)
        for kt in range(KD):
            self.split(("norm", norm, kt))

    def row(self, p, m):
        self.open(("rowX", p), 2 * (m % 2))
        self.open(("rowY", p), 2 * (m % 2) + 1)
        self.add("row", p)

    def build(self):
        self.n_read = 0
        self.open(("gains",), 2)
        self.add("gains")
        for kt in range(KD):
            self.stat(1, kt)
        self.norm(1)
        m = 0
        first_gq = next(p for p, x in enumerate(PANELS) if x[0] == "gq")
        first_gv = first_gq + 4
        first_gr = first_gv + 4
        first_gta = first_gr + 4
        first_gtb = first_gta + 8
        first_oab = first_gtb + 8
        extra = {}

        def at(p, *step):
            extra.setdefault(p, []).append(step)

        for t in range(NTILE):
            at(first_gq + t, "qknorm", t)
            at(first_gq + t + 2, "qkT", t)
        at(first_gq + 1, "z")
        at(first_gq + 2, "decay")
        at(first_gq + 4, "gexp")
        at(first_gv + 3, "qiz")
        for j in range(1, 4):
            at(first_gr + j - 1, "index", j)
        for g in range(2):
            at(first_gr + 1 + g, "kidx", g)
        at(first_gr + 3, "sindex")
        for c in range(N_CHUNK):
            if c % 4 == 0:
                at(first_gr + 1 + c // 2, "intra", c // 4)
            at(first_gr + 1 + c // 2, "chunk", c)
        at(first_gr + 9, "intra", 4)
        for r in range(4):
            at(first_gr + 9 + r // 2, "sround", r)
        at(first_gr + 10, "sgla_out")
        rounds = [("s", r) for r in range((TOPK_SAMPLE + PAD_TOP) // 8)]
        rounds += [(j, r) for j in (1, 2, 3) for r in range(TOPK_PROMPT // 8)]
        for p in range(first_gr + 5, first_oab):
            for _ in range(2 if p < first_gtb else 6):
                if rounds:
                    at(p, "topk", *rounds.pop(0))
        assert not rounds
        for h in range(GH):
            at(first_gtb + 1 + h, "gnorm", h)
        at(first_gtb + 4, "qz")
        for p in range(first_gtb + 8):
            self.panel(p)
            if p and PANELS[p - 1][0] in STAGED:
                self.row(p - 1, m)
                m += 1
            for step in extra.get(p, []):
                self.extra_step(step)
        for h in range(GH):
            self.add("gout", h)
            self.split(("gout", h))
        for i in range(4):
            self.add("sample", i)
            for b in (2 * i, 2 * i + 1):
                self.open(("kcT", b), 2)
                if b == 2 * i:
                    self.open(("slog", i), i % 2)
            self.open(("spT", i), 2)
            if i == 0:
                self.open(("so",), 3)
        self.add("sample_out")
        for j in range(4):
            for h in range(N_HEADS):
                self.add("attn", j, h)
            self.add("attn_out", j)
        order = [(j, h) for j in range(4) for h in range(N_HEADS)]
        self.attn_order = order
        for n, (j, h) in enumerate(order):
            if n == 0:
                self.open(("log", j, h), 0)
            if n + 1 < len(order):
                self.open(("log",) + order[n + 1], (n + 1) % 2)
            self.open(("pT", j, h), 2)
            if h == 0:
                self.open(("o", j), 3)
            if h == N_HEADS - 1:
                self.open(("oT", j), 2)
        for p in range(first_oab, N_PANELS):
            self.panel(p)
            kind, idx, _ = PANELS[p]
            if kind == "o" and idx > 0:
                self.stat(2, idx - 1)
            if kind == "o" and idx == KD - 1:
                self.stat(2, idx)
                self.norm(2)

    def extra_step(self, step):
        kind = step[0]
        if kind == "z":
            for i, b in ((0, 2), (1, 3), (2, 1)):
                self.open(("z", i), b)
        if kind == "decay":
            for i, b in ((0, 0), (1, 1), (2, 2)):
                self.open(("b", i), b)
        if kind == "qkT":
            for i, b in (("q", 0), ("ik", 1), ("ki", 3)):
                self.open((i, step[1]), b)
        if kind == "index":
            for h in range(IDX_HEADS):
                self.open(("index", step[1], h), 2 + h % 2)
                self.gate_tmp(("index", step[1], h), ("index_added", 4 * (step[1] - 1) + h + 1))
        if kind == "kidx":
            g = step[1]
            self.open(("kidxT", 2 * g), 3)
            self.open(("kidxT", 2 * g + 1), 3)
            self.open(("sscore", g), 2)
        if kind == "qiz":
            self.open(("wi", 0), 3)
            self.open(("wi", 1), 2)
        if kind == "sindex":
            self.open(("ssum",), 3)
        if kind == "intra":
            t = step[1]
            self.open(("kT", t), 3)
            self.open(("inE", t), 3)
            self.open(("inO", t), 2)
            self.open(("oE", t), 0)
            self.open(("oO", t), 1)
        if kind == "chunk":
            self.open(("kv", step[1]), 2)
        if kind == "sround":
            self.open(("skv", step[1]), 2)
        if kind == "gnorm":
            self.open(("gn", step[1], 0), 0)
            self.open(("gn", step[1], 1), 1)
            self.stage(("gn", step[1]), ("bank_ready", ("gn", step[1], 1)))
            self.gate_tmp(("gn", step[1]), ("gnorm_done", step[1] + 1))
        self.add(*step)


def build(nc, A, depth=DEPTH):
    plan = Plan()
    uses = plan.uses

    ctx = ExitStack()
    with ctx:
        base = 192
        cursor = [base]

        def region(nbytes):
            at = cursor[0]
            cursor[0] += (nbytes + 31) // 32 * 32
            return at

        def at(name, shape, dt, offset):
            return nc.alloc_sbuf_tensor_at(name, shape, dt, offset=offset)

        def sb(name, shape, dt=F32):
            n = int(np.prod(shape[1:])) * (2 if dt == BF16 else 4)
            return at(name, shape, dt, region(n))

        cst = sb("cst", [P, KEPT_W])
        x_t = sb("x_t", [P, KD, NT])
        in_hi = sb("in_hi", [P, KD, NT], F32R)
        in_lo = sb("in_lo", [P, KD, NT], F32R)
        w_raw = sb("w_raw", [P, RAW_RING, KD * P])
        w_hi = sb("w_hi", [P, 2, KD * P], F32R)
        w_lo = sb("w_lo", [P, 2, KD * P], F32R)
        tmp = sb("tmp", [P, 2, NT])
        stage = sb("stage", [P, 2, NT])
        gate_tmp = sb("gate_tmp", [P, 2, NT])
        ones = sb("ones", [P, P])
        ident_b = sb("ident_b", [P, P], BF16)
        tri_b = sb("tri_b", [P, P], BF16)
        repeat_b = sb("repeat_b", [NS, DEC_BATCH, NS], BF16)
        eps_t = sb("eps_t", [P, 1])
        pages = sb("pages", [1, DEC_BATCH * N_PAGES], I32)
        gain_rows = sb("gain_rows", [2 * KD + 1, P])
        gains = sb("gains", [P, 2 * KD + 1])
        qk_g = sb("qk_g", [P, 3, HD])
        wa2 = sb("wa2", [RANK, GK_W])
        ba = sb("ba", [1, GK_W])
        ff = region(2 * KD * NT * 4)
        mid_hi = at("mid_hi", [P, KD, NT], F32R, ff)
        mid_lo = at("mid_lo", [P, KD, NT], F32R, ff + KD * NT * 4)
        gate_a = at("gate_a", [P, KD, NT], F32, ff)
        gla_r = at("gla_r", [P, GH, NT], F32, ff + KD * NT * 4)
        gla_o = at("gla_o", [P, GH, NT], F32, ff + (KD + GH) * NT * 4)
        x_rows = at("x_rows", [P, NTILE, D_MODEL], F32, ff)
        repeat_f = at("repeat_f", [P, CONST_W - KEPT_W], F32, ff + NTILE * D_MODEL * 4)
        q_rows = at("q_rows", [P, NTILE, 13 * HD], F32, ff)
        la = at("la", [P, NTILE, GK_W], F32, ff + 16640)
        ga_t = at("ga_t", [RANK, NT], F32, ff + 21760)
        d_t = at("d_t", [P, 2, NT], F32, ff + 24064)
        e_t = at("e_t", [P, 2, NT], F32, ff + 28672)
        sq_rows = at("sq_rows", [P, 13, HD], F32, ff + 33280)
        kidx = at("kidx", [P, DEC_BATCH, N_PAGES, ID], F32, ff)
        kidx_t = at("kidx_t", [ID, 2, 2 * PAST], F32, ff + 4096)
        qiz = at("qiz", [ID, DEC_BATCH, 32], F32, ff + 8192)
        s_heads = at("s_heads", [P, 2, NEW_KEYS], F32, ff + 9216)
        kv_rows = sb("kv_rows", [P, NTILE, 2 * KV_W])
        q_t = sb("q_t", [P, 4, NT])
        k_t = sb("k_t", [P, 2, NT])
        mask_b = sb("mask_b", [P, 3, SEQ], BF16)
        mask_s = sb("mask_s", [NS, NEW_KEYS], BF16)
        wi_rows = sb("wi_rows", [P, NTILE, IDX_HEADS])
        ar = region(0)
        off = [ar]

        def sub(name, shape, dt=F32):
            t = at(name, shape, dt, off[0])
            off[0] += (int(np.prod(shape[1:])) * (2 if dt == BF16 else 4) + 31) // 32 * 32
            return t

        gq = sub("gq", [P, 2, NT])
        gk = sub("gk", [P, 2, NT])
        gk_rows = sub("gk_rows", [P, 2, GK_W])
        gv_rows = sub("gv_rows", [P, NTILE, GV_W])
        state = sub("state", [P, 2, DV])
        state_in = sub("state_in", [P, 2, DV])
        state_add = sub("state_add", [P, 2, DV])
        s_state = sub("s_state", [P, 2, 2, 2, DV])
        s_state_in = sub("s_state_in", [P, 2, 2, DV])
        s_state_add = sub("s_state_add", [P, 2, 2, DV])
        gk_one = sub("gk_one", [NS, 2, GK_W])
        g_attn = sub("g_attn", [P, GH, P])
        qi_t = sub("qi_t", [P, 2, NT])
        ki_t = sub("ki_t", [P, NT])
        scores = sub("scores", [P, 2 * P + 3 * P + 4 * P])
        rstd = at("rstd", [P, NT], F32, off[0] - 4608)
        scores_s = sub("scores_s", [NS, SAMPLE_W])
        end1 = off[0]
        off[0] = ar
        gate_b = sub("gate_b", [P, KD, NT])
        qz = sub("qz", [P, DEC_BATCH, 2, NS])
        k_pages = sub("k_pages", [P, 4, N_PAGES, KV_W])
        v_pages = sub("v_pages", [P, 4, N_PAGES, KV_W])
        p_t = sub("p_t", [P, 2, SEQ])
        pT_t = sub("pT_t", [P, 2, 4, P])
        k_past = sub("k_past", [P, 2, 2, PAST])
        o_rows = sub("o_rows", [P, ATTN_W])
        cursor[0] = max(off[0], end1)
        small = lambda name, w, rows=P: sb(name, [rows, w])
        sums = small("sums", 16)
        top8 = small("top8", 8)
        top8s = small("top8s", 8)
        b_ref = sb("b_ref", [P, 2, 24])
        b_end = sb("b_end", [P, 2, 24])
        e_ref = sb("e_ref", [P, 2, 24])
        e_end = sb("e_end", [P, 2, 24])
        e_add = sb("e_add", [P, 2, 24])
        wi_s = sb("wi_s", [P, 2])
        wi_tmp = sb("wi_tmp", [P, 2, IDX_HEADS])
        rope1 = sb("rope1", [P, 13, ROT])
        rope2 = sb("rope2", [P, 13, ROT])
        neg_max = sb("neg_max", [P, 2, N_HEADS])
        p_sum = sb("p_sum", [P, 2, N_HEADS])
        p_inv = sb("p_inv", [P, N_HEADS])
        neg_max_s = sb("neg_max_s", [P, 4])
        p_sum_s = sb("p_sum_s", [P, 4])
        p_inv_s = sb("p_inv_s", [P, 4])
        assert cursor[0] <= nc.sbuf_usable_end, cursor[0]

        aux = nc.alloc_psum_tensor("aux", [P, 4, 512], F32)
        prod = nc.alloc_psum_tensor("prod", [P, 4, 512], F32)

        def const(name, rows=P):
            lo, hi = CONSTS[name]
            return cst[0:rows, lo:hi]

        def slot(g):
            s = g % 2
            return prod[:, 2 * s:2 * s + 2, 0:HALF]

        def halves(ap):
            return ap.rearrange("p (h n) -> p h n", h=2)

        def semaphore(name):
            return ctx.enter_context(nc.semaphore(name))

        x_loaded = semaphore("x_loaded")
        x_turned = semaphore("x_turned")
        once = semaphore("once")
        y_turned = semaphore("y_turned")
        y_ready = semaphore("y_ready")
        y_stored = semaphore("y_stored")
        x_filled = semaphore("x_filled")
        opened_layer = semaphore("opened_layer")
        bank_ready = [semaphore(f"bank{i}_ready") for i in range(6)]
        bank_free = [semaphore(f"bank{i}_free") for i in range(6)]
        raw_ready = [semaphore(f"raw{i}_ready") for i in range(RAW_RING)]
        w_hi_done = semaphore("w_hi_done")
        w_lo_done = semaphore("w_lo_done")
        staged = semaphore("staged")
        stage_read = semaphore("stage_read")
        gated = semaphore("gated")
        index_added = semaphore("index_added")
        split_src = semaphore("split_src")
        split_hi = semaphore("split_hi")
        split_lo = semaphore("split_lo")
        x_added = semaphore("x_added")
        dve_step = semaphore("dve_step")
        rows_sq = semaphore("rows_sq")
        rows_ss = semaphore("rows_ss")
        rows_std = semaphore("rows_std")
        rows_done = semaphore("rows_done")
        ln_done = semaphore("ln_done")
        ga_done = semaphore("ga_done")
        decay_done = semaphore("decay_done")
        exps_done = semaphore("exps_done")
        gqk_done = semaphore("gqk_done")
        qiz_done = semaphore("qiz_done")
        state_done = semaphore("state_done")
        s_in_done = semaphore("s_in_done")
        s_out_done = semaphore("s_out_done")
        gnorm_done = semaphore("gnorm_done")
        masks_done = semaphore("masks_done")
        qz_done = semaphore("qz_done")
        max_done = semaphore("max_done")
        pv_done = semaphore("pv_done")
        p_scaled = semaphore("p_scaled")
        attn_hi = semaphore("attn_hi")
        kc_free = semaphore("kc_free")
        small_ready = semaphore("small_ready")
        kidx_ready = semaphore("kidx_ready")
        s_state_ready = [semaphore(f"s_state{i}_ready") for i in range(2)]
        kv_ready = [semaphore(f"pages{i}_ready") for i in range(4)]
        stored = semaphore("stored")
        s_stored = semaphore("s_stored")
        state_stored = semaphore("state_stored")
        sample_intra = semaphore("sample_intra")
        z_abs = semaphore("z_abs")
        z_exp = semaphore("z_exp")
        arrived = semaphore("arrived")
        layer_sems = range(bank_ready[0].num, arrived.num + 1)

        free_of, of_bank = {}, [0, 0]
        for p, (kind, idx, _) in enumerate(PANELS):
            for g in plan.groups[p]:
                if kind == "o":
                    free_of["g", g] = (x_added, idx + 1)
                elif kind in STAGED:
                    free_of["g", g] = (staged, plan.stage_use["row", p] + 1)
                elif kind == "down":
                    free_of["g", g] = (x_added, KD + idx[0] * KD + idx[1] + 1)
                else:
                    of_bank[g % 2] += 1
                    free_of["g", g] = (bank_free[4 + g % 2], of_bank[g % 2])
        for key, (bank, use) in uses.items():
            if bank < 4:
                free_of[key] = (bank_free[bank], use + 1)

        def ready(key):
            return bank_ready[uses[key][0]]

        def filled(key):
            return uses[key][1] + 1

        def free(key):
            return free_of[key][0]

        def emptied(key):
            return free_of[key][1]

        def opened(key):
            return uses[key][1]

        def pv_used(n):
            j, h = ORDER[n]
            return (pv_done, j * (N_HEADS - 1) + h + 1) if h < N_HEADS - 1 else (ready(("o", j)), filled(("o", j)))

        def counter():
            counts = {}

            def turn(sem):
                counts[sem.num] = counts.get(sem.num, 0) + 1
                return counts[sem.num]
            return turn

        def release(what, key):
            if what == "bank_ready":
                return ready(key), filled(key)
            if what == "bank_free":
                return free(key), emptied(key)
            return {"stage_read": stage_read, "index_added": index_added, "gnorm_done": gnorm_done}[what], key

        def layers(e, body):
            with e.Fori(0, depth) as layer:
                body(layer)
                if e is not nc.sync:
                    e.sem_inc(arrived, 1)
                    e.wait_ge(opened_layer, layer + 1)
                    e.wait_ge(once, 1)

        def of_layer(name, layer):
            return A[name][bass.ds(layer, 1)]

        HEAD_TILE = [(h // 4 * 2 + h % 2, h % 4 // 2) for h in range(N_HEADS)]
        ORDER = plan.attn_order
        last_gtb = max(plan.groups[max(p for p, x in enumerate(PANELS) if x[0] == "gtb")])
        misc_panel = next(p for p, x in enumerate(PANELS) if x[0] == "misc")
        gv_panels = [p for p, x in enumerate(PANELS) if x[0] == "gv"]
        gtb_panels = [p for p, x in enumerate(PANELS) if x[0] == "gtb"]
        gate_panel = [min(p for p, x in enumerate(PANELS) if x[0] == k) for k in ("gta", "gtb")]
        gqk_group = {(x[0], x[1]): plan.groups[p][0] for p, x in enumerate(PANELS) if x[0] in ("gq", "gk")}
        plan_src, gated_no = {}, {}
        for key in plan.split_use:
            if key[0] in ("norm", "merge"):
                plan_src[key] = len(plan_src) + 1
        for key in plan.gate_tmp_use:
            if key[0] in ("gr", "gate"):
                gated_no[key] = len(gated_no) + 1
        score_cols = {1: (0, 2 * P), 2: (2 * P, 5 * P), 3: (5 * P, 9 * P)}
        ident = const("ident")

        block = ctx.enter_context(nc.Block())

        @block.sync
        def _(e):
            e.dma_start(cst[:], A["consts"][:, 0:KEPT_W]).then_inc(x_loaded, 16)
            e.dma_start(repeat_f[:], A["consts"][:, KEPT_W:CONST_W]).then_inc(x_loaded, 16)
            for t in range(NTILE):
                src = A["x_prompt"][0, t * P:(t + 1) * P, :] if t < 4 else A["x_sample"].rearrange("b s d -> (b s) d")
                e.dma_start(x_rows[0:tile_rows(t), t, :], src).then_inc(x_loaded, 16)
            e.dma_start(pages[:], A["page_table"].rearrange("b n -> (b n)").unsqueeze(0)).then_inc(x_loaded, 16)
            e.wait_ge(x_loaded, 16 * (3 + NTILE))

            def load_state(layer, r):
                for b2 in range(2):
                    for h2 in range(2):
                        src = of_layer("state_gla", layer)[:, 2 * r + b2, h2:GH:2].rearrange("a g k v -> k (a g) v")
                        e.dma_start(s_state[h2 * DK:(h2 + 1) * DK, r % 2, b2, :, :], src).then_inc(s_state_ready[r % 2], 16)

            def body(layer):
                def store(dst, src, sig):
                    e.dma_start(dst, src).then_inc(sig, 16)

                def load_panel(p):
                    if p >= RAW_RING:
                        e.wait_ge(w_lo_done, p - RAW_RING + 1)
                    for name, row, nk, col, w, place in PANELS[p][2]:
                        src = of_layer(name, layer)[:, row:row + nk * P, col:col + w].rearrange(
                            "a (k p) n -> p (a k) n", p=P)
                        if w == P:
                            dst = w_raw[:, p % RAW_RING, place:place + nk * P].rearrange("p (k n) -> p k n", n=P)
                        else:
                            dst = w_raw[:, p % RAW_RING, :].rearrange("p (k n) -> p k n", n=P)[:, :, place:place + w]
                        e.dma_start(dst, src).then_inc(raw_ready[p % RAW_RING], 16)

                def page(b, n):
                    i = b * N_PAGES + n
                    return e.value_load(pages[0:1, i:i + 1], min_val=0, max_val=N_POOL - 1)

                def load_pages(b):
                    for n in range(N_PAGES):
                        r = page(b, n)
                        for name, dst in (("cache_k", k_pages), ("cache_v", v_pages)):
                            src = A[name].rearrange("l n s h d -> (l n) s (h d)")[bass.ds(layer * N_POOL + r, 1)]
                            e.dma_start(dst[:, b % 4, n, :], src.rearrange("a s f -> (a s) f")).then_inc(kv_ready[b % 4], 16)

                for p in range(RAW_RING):
                    load_panel(p)
                for n, name in ((0, "norm1_g"), (1, "norm2_g")):
                    e.dma_start(gain_rows[n * KD:(n + 1) * KD, :], of_layer(name, layer).rearrange("a (k p) -> (a k) p", p=P)).then_inc(small_ready, 16)
                e.dma_start(gain_rows[2 * KD:2 * KD + 1, :], of_layer("gla_onorm_g", layer)).then_inc(small_ready, 16)
                for n, name in enumerate(("q_norm_g", "k_norm_g", "kidx_norm_g")):
                    row = of_layer(name, layer)
                    e.dma_start(qk_g[:, n, :], row.partition_broadcast(P).rearrange("p a n -> p (a n)")).then_inc(small_ready, 16)
                e.dma_start(wa2[:], of_layer("gla_wa2", layer).rearrange("a r n -> (a r) n")).then_inc(small_ready, 16)
                e.dma_start(ba[:], of_layer("gla_ba", layer)).then_inc(small_ready, 16)
                for step in plan.steps:
                    kind = step[0]
                    if kind == "panel" and step[1] + RAW_RING < N_PANELS:
                        load_panel(step[1] + RAW_RING)
                    if kind == "qkT":
                        t = step[1]
                        n = tile_rows(t)
                        e.wait_ge(rows_done, t + 1)
                        for name, src in (("k", kv_rows[0:n, t, 0:KV_W]), ("v", kv_rows[0:n, t, KV_W:2 * KV_W]),
                                          ("kidx", q_rows[0:n, t, 12 * HD:13 * HD])):
                            if t < 4:
                                dst = of_layer(f"new_{name}_prompt", layer)[:, 0, t * P:(t + 1) * P]
                                dst = dst.rearrange("a s h d -> (a s) (h d)") if name != "kidx" else \
                                    dst.rearrange("a s d -> (a s) d")
                            else:
                                dst = of_layer(f"new_{name}_sample", layer)
                                dst = dst.rearrange("a b s h d -> (a b s) (h d)") if name != "kidx" else \
                                    dst.rearrange("a b s d -> (a b s) d")
                            e.dma_start(dst, src).then_inc(stored, 16)
                    if kind == "qkT" and step[1] == NTILE - 1:
                        e.wait_ge(stored, 16 * 3 * NTILE)
                        e.wait_ge(ready(("ki", 4)), filled(("ki", 4)))
                        for b in range(DEC_BATCH):
                            for n in range(N_PAGES):
                                r = page(b, n)
                                src = A["cache_kidx"].rearrange("l n s d -> (l n) s d")[
                                    bass.ds(layer * N_POOL + r, 1)].rearrange("a s d -> (a s) d")
                                e.dma_start(kidx[:, b, n, :], src).then_inc(kidx_ready, 16)
                    if kind == "intra" and step[1] == 3:
                        for r in range(2):
                            load_state(layer, r)
                    if kind == "intra" and step[1] == 4:
                        e.wait_ge(state_done, N_CHUNK)
                        for h2 in range(2):
                            dst = of_layer("new_gla_prompt", layer)[:, 0, h2:GH:2].rearrange("a g k v -> k (a g) v")
                            e.dma_start(dst, state[h2 * DK:(h2 + 1) * DK, :, :]).then_inc(state_stored, 16)
                    if kind == "sround":
                        r = step[1]
                        e.wait_ge(s_out_done, r + 1)
                        for b2 in range(2):
                            for h2 in range(2):
                                dst = of_layer("new_gla_sample", layer)[:, 2 * r + b2, h2:GH:2].rearrange(
                                    "a g k v -> k (a g) v")
                                e.dma_start(dst, s_state[h2 * DK:(h2 + 1) * DK, r % 2, b2, :, :]).then_inc(s_stored, 16)
                        if r < 2:
                            e.wait_ge(s_stored, 16 * 4 * (r + 1))
                            load_state(layer, r + 2)
                    if kind == "panel" and step[1] == gtb_panels[2]:
                        e.wait_ge(ready(("g", plan.groups[gtb_panels[1]][0])), filled(("g", plan.groups[gtb_panels[1]][0])))
                        e.wait_ge(state_stored, 16 * 2)
                        e.wait_ge(s_stored, 16 * 2 * DEC_BATCH)
                        for b in range(4):
                            load_pages(b)
                    if kind == "sample" and step[1] < 2:
                        i = step[1]
                        e.wait_ge(kc_free, 2 * i + 2)
                        for b in (2 * i + 4, 2 * i + 5):
                            load_pages(b)

                e.wait_ge(stored, 16 * 3 * NTILE)
                e.wait_ge(s_stored, 16 * 2 * DEC_BATCH)
                e.wait_ge(state_stored, 16 * 2)
                e.wait_ge(arrived, 3)
                e.sem_clear(layer_sems)
                e.sem_inc(opened_layer, 1)

            layers(e, body)
            for t in range(NTILE):
                e.wait_ge(y_ready, 2 * (t + 1))
                dst = A["y_prompt"][0, t * P:(t + 1) * P, :] if t < 4 else A["y_sample"].rearrange("b s d -> (b s) d")
                e.dma_start(dst, x_rows[0:tile_rows(t), t, :]).then_inc(y_stored, 16)
            e.wait_ge(y_stored, 16 * NTILE)

        @block.tensor
        def _(e):
            e.wait_ge(x_loaded, 16 * (3 + NTILE))
            for kt in range(KD):
                if kt >= 2:
                    e.wait_ge(x_filled, kt - 1)
                for t in range(NTILE):
                    n = tile_rows(t)
                    out = aux[:, 2 * (kt % 2) + t // 4, (t % 4) * P:(t % 4) * P + n]
                    ins = e.transpose(out, x_rows[0:n, t, kt * P:(kt + 1) * P], ident[0:n, 0:n])
                ins.then_inc(x_turned, 1)
            e.wait_ge(x_filled, KD)

            def body(layer):
                def panel(p):
                    kind, idx, parts = PANELS[p]
                    slot_w = p % 2
                    e.wait_ge(w_lo_done, p + 1)
                    for n, g in enumerate(plan.groups[p]):
                        if g >= 2:
                            e.wait_ge(free(("g", g - 2)), emptied(("g", g - 2)))
                        if kind in ("oab", "down"):
                            ks = list(range(4 * n, 4 * n + 4)) if kind == "oab" else list(range(FF_PARTS[idx[0]]))
                        else:
                            ks = list(range(KD))
                        if kind in ("o", "down"):
                            hi, lo = mid_hi, mid_lo
                        else:
                            hi, lo = in_hi, in_lo
                        if kind == "oab" and idx == 0 and n == 0:
                            e.wait_ge(free(("so",)), emptied(("so",)))
                            for j in range(4):
                                e.wait_ge(free(("oT", j)), emptied(("oT", j)))
                        for k in ks:
                            if kind in ("q",) and idx == 0:
                                e.wait_ge(split_lo, plan.split_use["norm", 1, k] + 1)
                            if kind == "oab" and idx == 0 and n == 1:
                                e.wait_ge(split_lo, plan.split_use["gout", k - 4] + 1)
                            if kind == "o" and idx == 0:
                                e.wait_ge(split_lo, plan.split_use["merge", k] + 1)
                            if kind == "gate" and idx == (0, 0):
                                e.wait_ge(split_lo, plan.split_use["norm", 2, k] + 1)
                            if kind == "down" and idx[1] == 0:
                                e.wait_ge(split_lo, plan.split_use["ff", (idx[0], sum(FF_PARTS[:idx[0]]) + k)] + 1)
                            for w, parts_in in ((w_hi, (hi, lo)), (w_lo, (hi,))):
                                for a in parts_in:
                                    for h in range(2):
                                        first = k == ks[0] and w is w_hi and a is hi
                                        last = k == ks[-1] and w is w_lo
                                        ins = e.matmul(slot(g)[:, h, :], w[:, slot_w, k * P:(k + 1) * P],
                                                       a[:, k, h * HALF:(h + 1) * HALF], start=first, stop=last)
                        ins.then_inc(ready(("g", g)), 1)

                def logits(n):
                    j, h = ORDER[n]
                    L = (j + 1) * P
                    tile, half = HEAD_TILE[h]
                    rows = slice(64 * half, 64 * half + 64)
                    key = ("log", j, h)
                    e.wait_ge(free(key), opened(key))
                    out = aux[:, uses[key][0], 0:L]
                    mask = tri_b[:] if j == 0 else mask_b[:, j - 1, 0:L]
                    if n == 0:
                        e.wait_ge(masks_done, 4)
                    e.matmul(out, ident_b[:], mask, start=True, stop=False)
                    ins = e.matmul(out, q_t[rows, tile, j * P:(j + 1) * P], k_t[rows, h // 4, 0:L],
                                   start=False, stop=True)
                    ins.then_inc(ready(key), 1)

                for step in plan.steps:
                    kind = step[0]
                    if kind == "panel":
                        panel(step[1])
                    elif kind == "gains":
                        e.wait_ge(small_ready, 16 * SMALL_LOADS)
                        e.wait_ge(free(("gains",)), opened(("gains",)))
                        ins = e.transpose(aux[:, 2, 0:2 * KD + 1], gain_rows[:], ident[0:2 * KD + 1, 0:2 * KD + 1])
                        ins.then_inc(ready(("gains",)), 1)
                    elif kind == "stat":
                        _, norm, kt = step
                        use = plan.stage_use["stat", norm, kt]
                        e.wait_ge(staged, use + 1)
                        if kt == 0:
                            for h in range(2):
                                e.wait_ge(free(("stat", norm, h)), opened(("stat", norm, h)))
                        for h in range(2):
                            ins = e.matmul(aux[:, h, 0:HALF], ones[:], stage[:, use % 2, h * HALF:(h + 1) * HALF],
                                           start=(kt == 0), stop=(kt == KD - 1))
                            if kt == KD - 1:
                                ins.then_inc(ready(("stat", norm, h)), 1)
                        if kt < KD - 1:
                            ins.then_inc(stage_read, 1)
                    elif kind == "row":
                        p = step[1]
                        use = plan.stage_use["row", p]
                        e.wait_ge(staged, use + 1)
                        e.wait_ge(free(("rowX", p)), opened(("rowX", p)))
                        bx, by = uses["rowX", p][0], uses["rowY", p][0]
                        for t in range(4):
                            ins = e.transpose(aux[:, bx, t * P:(t + 1) * P], stage[:, use % 2, t * P:(t + 1) * P], ident)
                        ins.then_inc(ready(("rowX", p)), 1)
                        e.wait_ge(free(("rowY", p)), opened(("rowY", p)))
                        ins = e.transpose(aux[0:NS, by, 0:P], stage[:, use % 2, SEQ:NT], ident)
                        ins.then_inc(ready(("rowY", p)), 1)
                    elif kind == "z":
                        e.wait_ge(small_ready, 16 * SMALL_LOADS)
                        e.wait_ge(ga_done, 1)
                        for i in range(3):
                            e.wait_ge(free(("z", i)), opened(("z", i)))
                            for t in range(2 * i, min(2 * i + 2, NTILE)):
                                n = tile_rows(t)
                                out = aux[0:n, uses["z", i][0], (t % 2) * GK_W:(t % 2 + 1) * GK_W]
                                e.matmul(out, ga_t[:, token_slice(t)], wa2[:], start=True, stop=False)
                                ins = e.matmul(out, ones[0:1, 0:n], ba[:], start=False, stop=True)
                            ins.then_inc(ready(("z", i)), 1)
                    elif kind == "decay":
                        for i in range(3):
                            e.wait_ge(free(("z", i)), emptied(("z", i)))
                        for hp in range(2):
                            e.wait_ge(free(("b", hp)), opened(("b", hp)))
                            for t in range(4):
                                ins = e.matmul(aux[:, hp, t * P:(t + 1) * P], la[:, t, hp * P:(hp + 1) * P],
                                               const("chunk_sum"), start=True, stop=True)
                            ins.then_inc(ready(("b", hp)), 1)
                        e.wait_ge(free(("b", 2)), opened(("b", 2)))
                        for hp in range(2):
                            ins = e.matmul(aux[:, 2, hp * NS:(hp + 1) * NS], la[0:NS, 4, hp * P:(hp + 1) * P],
                                           const("sample_sum", NS), start=True, stop=True)
                        ins.then_inc(ready(("b", 2)), 1)
                    elif kind == "qkT":
                        t = step[1]
                        n = tile_rows(t)
                        idn = ident[0:n, 0:n]
                        e.wait_ge(rows_done, t + 1)
                        e.wait_ge(free(("q", t)), opened(("q", t)))
                        for m in range(4):
                            ins = e.transpose(aux[:, 0, m * P:m * P + n], q_rows[0:n, t, m * P:(m + 1) * P], idn)
                        ins.then_inc(ready(("q", t)), 1)
                        e.wait_ge(free(("ik", t)), opened(("ik", t)))
                        for m in range(2):
                            e.transpose(aux[:, 1, m * P:m * P + n], q_rows[0:n, t, (4 + m) * P:(5 + m) * P], idn)
                        for m in range(2):
                            ins = e.transpose(aux[:, 1, (2 + m) * P:(2 + m) * P + n],
                                              kv_rows[0:n, t, m * P:(m + 1) * P], idn)
                        ins.then_inc(ready(("ik", t)), 1)
                        e.wait_ge(free(("ki", t)), opened(("ki", t)))
                        e.transpose(aux[0:ID, 3, 0:n], q_rows[0:n, t, 12 * HD:13 * HD], idn)
                        ins = e.matmul(aux[ID:2 * ID, 3, 0:n], q_rows[0:n, t, 12 * HD:13 * HD], idn,
                                       start=True, stop=True)
                        ins.then_inc(ready(("ki", t)), 1)
                    elif kind == "index":
                        j = step[1]
                        L = (j + 1) * P
                        e.wait_ge(free(("ik", 4)), emptied(("ik", 4)))
                        e.wait_ge(free(("ki", 4)), emptied(("ki", 4)))
                        for h in range(IDX_HEADS):
                            rows = slice(64 * (h % 2), 64 * (h % 2) + 64)
                            key = ("index", j, h)
                            e.wait_ge(free(key), opened(key))
                            ins = e.matmul(aux[:, uses[key][0], 0:L], qi_t[rows, h // 2, j * P:(j + 1) * P],
                                           ki_t[rows, 0:L], start=True, stop=True)
                            ins.then_inc(ready(key), 1)
                    elif kind == "qiz":
                        for g in range(2):
                            e.wait_ge(free(("wi", g)), opened(("wi", g)))
                            bank = uses["wi", g][0]
                            ins = e.matmul(aux[:, bank, 0:IDX_HEADS],
                                           const("spread", NS)[:, g * P:(g + 1) * P], wi_rows[0:NS, 4, :],
                                           start=True, stop=True)
                            ins.then_inc(ready(("wi", g)), 1)
                    elif kind == "kidx":
                        g = step[1]
                        e.wait_ge(kidx_ready, 16 * DEC_BATCH * N_PAGES)
                        e.wait_ge(qiz_done, 1)
                        for u in range(2):
                            key = ("kidxT", 2 * g + u)
                            e.wait_ge(free(key), opened(key))
                            for k in range(4):
                                b = 4 * g + 2 * u + k // 2
                                ins = e.transpose(aux[0:ID, 3, k * P:(k + 1) * P], kidx[:, b, k % 2, :], ident)
                            ins.then_inc(ready(key), 1)
                        for u in range(2):
                            e.wait_ge(free(("kidxT", 2 * g + u)), emptied(("kidxT", 2 * g + u)))
                            if u == 0:
                                e.wait_ge(free(("sscore", g)), opened(("sscore", g)))
                            for k in range(2):
                                b = 4 * g + 2 * u + k
                                out = aux[32 * (b % 4):32 * (b % 4) + 32, 2, :]
                                e.matmul(out[:, 0:PAST], qiz[:, b, :], kidx_t[:, u, k * PAST:(k + 1) * PAST],
                                         start=True, stop=True)
                                ins = e.matmul(out[:, PAST:NEW_KEYS], qiz[:, b, :], ki_t[0:ID, SEQ:NT],
                                               start=True, stop=True)
                        ins.then_inc(ready(("sscore", g)), 1)
                    elif kind == "sindex":
                        e.wait_ge(free(("ssum",)), opened(("ssum",)))
                        for g in range(2):
                            e.wait_ge(free(("sscore", g)), emptied(("sscore", g)))
                            ins = e.matmul(aux[0:NS, 3, 0:NEW_KEYS], const("gather")[:, g * NS:(g + 1) * NS],
                                           s_heads[:, g, :], start=(g == 0), stop=(g == 1))
                        ins.then_inc(ready(("ssum",)), 1)
                    elif kind == "intra":
                        t = step[1]
                        n = tile_rows(t)
                        tok = token_slice(t)
                        e.wait_ge(gqk_done, 1)
                        e.wait_ge(free(("rowY", gv_panels[-1])), emptied(("rowY", gv_panels[-1])))
                        e.wait_ge(free(("kT", t)), opened(("kT", t)))
                        for hp in range(2):
                            ins = e.transpose(aux[0:n, 3, hp * P:(hp + 1) * P], gk[:, hp, tok], ident)
                        ins.then_inc(ready(("kT", t)), 1)
                        for par, key in enumerate((("inE", t), ("inO", t))):
                            e.wait_ge(free(key), opened(key))
                            rows = slice(64 * par, 64 * par + 64)
                            for hp in range(2):
                                ins = e.matmul(aux[0:n, uses[key][0], hp * P:hp * P + n], gk[rows, hp, tok],
                                               gq[rows, hp, tok], start=True, stop=True)
                            ins.then_inc(ready(key), 1)
                        for par, key in enumerate((("oE", t), ("oO", t))):
                            e.wait_ge(free(key), opened(key))
                            e.wait_ge(free((("inE", t), ("inO", t))[par]), emptied((("inE", t), ("inO", t))[par]))
                            for hp in range(2):
                                h = 2 * hp + par
                                ins = e.matmul(aux[:, par, hp * P:hp * P + n], gv_rows[0:n, t, h * DV:(h + 1) * DV],
                                               g_attn[0:n, h, 0:n], start=(hp == 0), stop=False,
                                               skip_group_check=True)
                        if t == 4:
                            ins.then_inc(sample_intra, 1)
                    elif kind == "chunk":
                        c = step[1]
                        t = c // 4
                        if c > 0:
                            e.wait_ge(state_done, c)
                            for par in range(2):
                                rows = slice(64 * par, 64 * par + 64)
                                for hp in range(2):
                                    ins = e.matmul(aux[:, par, hp * P + c % 4 * CHUNK:hp * P + (c % 4 + 1) * CHUNK],
                                                   state_in[rows, hp, :], gq[rows, hp, c * CHUNK:(c + 1) * CHUNK],
                                                   start=False, stop=(c % 4 == 3), skip_group_check=True)
                                if c % 4 == 3:
                                    ins.then_inc(ready((("oE", t), ("oO", t))[par]), 1)
                        e.wait_ge(free(("kT", t)), emptied(("kT", t)))
                        e.wait_ge(free(("kv", c)), opened(("kv", c)))
                        rows = slice(c % 4 * CHUNK, (c % 4 + 1) * CHUNK)
                        for h in range(GH):
                            ins = e.matmul(aux[64 * (h % 2):64 * (h % 2) + 64, 2, h // 2 * DV:(h // 2 + 1) * DV],
                                           gk_rows[rows, t % 2, h * DK:(h + 1) * DK],
                                           gv_rows[rows, t, h * DV:(h + 1) * DV], start=True, stop=True,
                                           tile_position=(c % 4 * CHUNK, 64 * (h % 2)))
                        ins.then_inc(ready(("kv", c)), 1)
                    elif kind == "sround":
                        r = step[1]
                        e.wait_ge(s_in_done, r + 1)
                        if r == 0:
                            e.wait_ge(sample_intra, 1)
                        for par in range(2):
                            rows = slice(64 * par, 64 * par + 64)
                            for b2 in range(2):
                                for hp in range(2):
                                    b = 2 * r + b2
                                    cols = slice(hp * P + b * DEC_SEQ, hp * P + (b + 1) * DEC_SEQ)
                                    ins = e.matmul(aux[:, par, cols], s_state_in[rows, b2, hp, :],
                                                   gq[rows, hp, SEQ + b * DEC_SEQ:SEQ + (b + 1) * DEC_SEQ],
                                                   start=False, stop=(r == 3), skip_group_check=True)
                            if r == 3:
                                ins.then_inc(ready((("oE", 4), ("oO", 4))[par]), 1)
                        e.wait_ge(free(("skv", r)), opened(("skv", r)))
                        for b2 in range(2):
                            for h in range(GH):
                                c0 = (b2 * 2 + h // 2) * DV
                                ins = e.matmul(aux[64 * (h % 2):64 * (h % 2) + 64, 2, c0:c0 + DV],
                                               gk_one[:, b2, h * DK:(h + 1) * DK], gv_rows[0:NS, 4, h * DV:(h + 1) * DV],
                                               start=True, stop=True)
                        ins.then_inc(ready(("skv", r)), 1)
                    elif kind == "gnorm":
                        h = step[1]
                        use = plan.stage_use["gn", h]
                        e.wait_ge(staged, use + 1)
                        for k in range(2):
                            e.wait_ge(free(("gn", h, k)), opened(("gn", h, k)))
                            ins = e.matmul(aux[:, k, 0:HALF], ones[:], stage[:, use % 2, k * HALF:(k + 1) * HALF],
                                           start=True, stop=True)
                            ins.then_inc(ready(("gn", h, k)), 1)
                    elif kind == "sample":
                        i = step[1]
                        bank = uses["slog", i][0]
                        if i == 0:
                            e.wait_ge(masks_done, 4)
                            e.wait_ge(qz_done, 1)
                        for b in (2 * i, 2 * i + 1):
                            e.wait_ge(kv_ready[b % 4], 16 * 4 * (b // 4 + 1))
                            e.wait_ge(free(("kcT", b)), opened(("kcT", b)))
                            for pair in range(2):
                                for n in range(N_PAGES):
                                    c0 = pair * PAST + n * PAGE
                                    ins = e.transpose(aux[:, 2, c0:c0 + PAGE],
                                                      k_pages[:, b % 4, n, pair * P:(pair + 1) * P], ident)
                            ins.then_inc(ready(("kcT", b)), 1)
                            if b == 2 * i:
                                e.wait_ge(free(("slog", i)), opened(("slog", i)))
                            out = aux[64 * (b % 2):64 * (b % 2) + 64, bank, :]
                            e.matmul(out[:, 0:NEW_KEYS], repeat_b[:, b, :], mask_s[:], start=True, stop=False,
                                     skip_group_check=True)
                            e.wait_ge(free(("kcT", b)), emptied(("kcT", b)))
                            for pair in range(2):
                                e.matmul(out[:, 0:PAST], qz[:, b, pair, :], k_past[:, b % 2, pair, :],
                                         start=False, stop=False, skip_group_check=True)
                                ins = e.matmul(out[:, PAST:NEW_KEYS], qz[:, b, pair, :], k_t[:, pair, SEQ:NT],
                                               start=False, stop=(pair == 1), skip_group_check=True)
                        ins.then_inc(ready(("slog", i)), 1)
                        e.wait_ge(p_scaled, i + 1)
                        e.wait_ge(free(("spT", i)), opened(("spT", i)))
                        for s in range(2):
                            e.transpose(aux[:, 2, s * P:(s + 1) * P], p_t[:, i % 2, s * P:(s + 1) * P], ident)
                        ins = e.transpose(aux[0:NS, 2, 2 * P:3 * P], p_t[:, i % 2, PAST:NEW_KEYS], ident)
                        ins.then_inc(ready(("spT", i)), 1)
                        if i == 0:
                            e.wait_ge(free(("so",)), opened(("so",)))
                        e.wait_ge(free(("spT", i)), emptied(("spT", i)))
                        for b in (2 * i, 2 * i + 1):
                            for pair in range(2):
                                out = aux[:, 3, (b * 2 + pair) * 32:(b * 2 + pair + 1) * 32]
                                cols = slice(64 * (b % 2) + 32 * pair, 64 * (b % 2) + 32 * pair + 32)
                                for s in range(2):
                                    e.matmul(out, v_pages[:, b % 4, s, pair * P:(pair + 1) * P],
                                             pT_t[:, i % 2, s, cols], start=(s == 0), stop=False)
                                ins = e.matmul(out, kv_rows[0:NS, 4, KV_W + pair * P:KV_W + (pair + 1) * P],
                                               pT_t[0:NS, i % 2, 2, cols], start=False, stop=True)
                            if b == DEC_BATCH - 1:
                                ins.then_inc(ready(("so",)), 1)
                            else:
                                ins.then_inc(kc_free, 1)
                    elif kind == "attn":
                        _, j, h = step
                        n = j * N_HEADS + h
                        if n == 0:
                            logits(0)
                        if n + 1 < len(ORDER):
                            logits(n + 1)
                        e.wait_ge(free(("log", j, h)), emptied(("log", j, h)))
                        e.wait_ge(free(("pT", j, h)), opened(("pT", j, h)))
                        for s in range(j + 1):
                            ins = e.transpose(aux[:, 2, s * P:(s + 1) * P], p_t[:, n % 2, s * P:(s + 1) * P], ident)
                        ins.then_inc(ready(("pT", j, h)), 1)
                        if h == 0:
                            e.wait_ge(free(("o", j)), opened(("o", j)))
                        e.wait_ge(free(("pT", j, h)), emptied(("pT", j, h)))
                        kv = h // 2
                        for s in range(j + 1):
                            ins = e.matmul(aux[:, 3, h * HD:(h + 1) * HD], pT_t[:, n % 2, s, :],
                                           kv_rows[:, s, KV_W + kv * HD:KV_W + (kv + 1) * HD],
                                           start=(s == 0), stop=(s == j))
                        if h < N_HEADS - 1:
                            ins.then_inc(pv_done, 1)
                        else:
                            ins.then_inc(ready(("o", j)), 1)
                    elif kind == "attn_out":
                        j = step[1]
                        e.wait_ge(free(("o", j)), emptied(("o", j)))
                        e.wait_ge(free(("oT", j)), opened(("oT", j)))
                        for m in range(4):
                            ins = e.transpose(aux[:, 2, m * P:(m + 1) * P], o_rows[:, m * P:(m + 1) * P], ident)
                        ins.then_inc(ready(("oT", j)), 1)

            layers(e, body)
            for t in range(NTILE):
                if t >= 2:
                    e.wait_ge(y_ready, 2 * (t - 1))
                n = tile_rows(t)
                for kt in range(KD):
                    ins = e.transpose(aux[0:n, 2 * (t % 2) + kt // 4, kt % 4 * P:(kt % 4 + 1) * P],
                                      x_t[:, kt, token_slice(t)], ident)
                ins.then_inc(y_turned, 1)

        @block.scalar
        def _(e):
            e.wait_ge(x_filled, KD)

            def body(layer):
                def copy_w(p):
                    e.wait_ge(raw_ready[p % RAW_RING], 16 * RAW_READY[p])
                    if p >= 2:
                        e.wait_ge(ready(("g", plan.groups[p - 2][-1])), filled(("g", plan.groups[p - 2][-1])))
                    n = sum(part[2] for part in PANELS[p][2]) * P if PANELS[p][0] != "misc" else KD * P
                    e.activation(w_hi[:, p % 2, 0:n], w_raw[:, p % RAW_RING, 0:n], ACT.Copy).then_inc(w_hi_done, 1)

                def exp_head(n):
                    j, h = ORDER[n]
                    L = (j + 1) * P
                    key = ("log", j, h)
                    e.wait_ge(max_done, 4 + n + 1)
                    if n >= 2:
                        e.wait_ge(ready(("pT",) + ORDER[n - 2]), filled(("pT",) + ORDER[n - 2]))
                    e.activation(p_t[:, n % 2, 0:L], aux[:, uses[key][0], 0:L], ACT.Exp, bias=neg_max[:, j % 2, h:h + 1], accum_out=p_sum[:, j % 2, h:h + 1]).then_inc(free(key), 1)

                def stage_slot(key):
                    use = plan.stage_use[key]
                    if use >= 2:
                        e.wait_ge(*release(*plan.stage_release[use - 2]))
                    return stage[:, use % 2, :]

                def gate_slot(key):
                    use = plan.gate_tmp_use[key]
                    if use >= 2:
                        e.wait_ge(*release(*plan.gate_tmp_release[use - 2]))
                    return gate_tmp[:, use % 2, :]

                copy_w(0)
                for step in plan.steps:
                    kind = step[0]
                    if kind == "panel":
                        p = step[1]
                        if p + 1 < N_PANELS:
                            copy_w(p + 1)
                        kind_p, idx, _ = PANELS[p]
                        g = plan.groups[p][0]
                        key = ("g", g)
                        src = slot(g)
                        if kind_p in STAGED:
                            dst = stage_slot(("row", p))
                            e.wait_ge(ready(key), filled(key))
                            if kind_p == "misc":
                                e.activation(halves(ga_t[:]), src[0:RANK], ACT.Copy).then_inc(ga_done, 1)
                            e.activation(halves(dst), src, ACT.Copy).then_inc(staged, 1)
                        elif kind_p == "gq":
                            e.wait_ge(ready(key), filled(key))
                            e.activation(halves(gq[:, idx, :]), src, ACT.Copy, scale=DK ** -0.5).then_inc(free(key), 1)
                        elif kind_p == "gk":
                            e.wait_ge(ready(key), filled(key))
                            e.activation(halves(gk[:, idx, :]), src, ACT.Copy).then_inc(free(key), 1)
                        elif kind_p == "gr":
                            dst = gate_slot(("gr", idx))
                            e.wait_ge(ready(key), filled(key))
                            e.activation(halves(dst), src, ACT.Sigmoid).then_inc(gated, 1)
                        elif kind_p == "gta":
                            e.wait_ge(ready(key), filled(key))
                            e.activation(halves(gate_a[:, idx, :]), src, ACT.Sigmoid).then_inc(free(key), 1)
                        elif kind_p == "gtb":
                            e.wait_ge(ready(key), filled(key))
                            e.activation(halves(gate_b[:, idx, :]), src, ACT.Sigmoid).then_inc(free(key), 1)
                        elif kind_p == "oab":
                            e.wait_ge(split_src, plan_src["merge", idx])
                            e.activation(mid_hi[:, idx, :], tmp[:, plan.split_use["merge", idx] % 2, :], ACT.Copy).then_inc(split_hi, 1)
                        elif kind_p == "gate":
                            dst = gate_slot(("gate", idx))
                            e.wait_ge(ready(key), filled(key))
                            e.activation(halves(dst), src, ACT.Sigmoid).then_inc(gated, 1)
                        elif kind_p == "up":
                            e.wait_ge(free(key), emptied(key))
                            part, i = idx
                            u = plan.split_use["ff", idx]
                            e.activation(mid_hi[:, i - sum(FF_PARTS[:part]), :], tmp[:, u % 2, :], ACT.Copy).then_inc(split_hi, 1)
                    elif kind == "stat":
                        _, norm, kt = step
                        dst = stage_slot(("stat", norm, kt))
                        if norm == 2:
                            e.wait_ge(x_added, kt + 1)
                        e.activation(dst, x_t[:, kt, :], ACT.Square).then_inc(staged, 1)
                    elif kind == "norm":
                        norm = step[1]
                        for h in range(2):
                            key = ("stat", norm, h)
                            e.wait_ge(ready(key), filled(key))
                            e.activation(rstd[:, h * HALF:(h + 1) * HALF], aux[:, h, 0:HALF], ACT.Sqrt, bias=eps_t[:], scale=1.0 / D_MODEL).then_inc(free(key), 1)
                        for kt in range(KD):
                            e.wait_ge(split_src, plan_src["norm", norm, kt])
                            e.activation(in_hi[:, kt, :], tmp[:, plan.split_use["norm", norm, kt] % 2, :], ACT.Copy).then_inc(split_hi, 1)
                    elif kind == "qknorm":
                        t = step[1]
                        n = tile_rows(t)
                        e.wait_ge(free(("rowX", misc_panel)), emptied(("rowX", misc_panel)))
                        e.wait_ge(free(("rowY", misc_panel)), emptied(("rowY", misc_panel)))
                        if t > 0:
                            e.wait_ge(rows_ss, t)
                        q3 = q_rows[0:n, t, :].rearrange("p (h d) -> p h d", d=HD)
                        e.activation(sq_rows[0:n, 0:8, :], q3[:, 0:8, :], ACT.Square)
                        e.activation(sq_rows[0:n, 8:12, :], kv_rows[0:n, t, 0:KV_W].rearrange("p (h d) -> p h d", d=HD), ACT.Square)
                        e.activation(sq_rows[0:n, 12, :], q3[:, 12, :], ACT.Square).then_inc(rows_sq, 1)
                        e.wait_ge(rows_ss, t + 1)
                        e.activation(sums[0:n, 0:13], sums[0:n, 0:13], ACT.Sqrt, bias=eps_t[0:n, :], scale=1.0 / HD).then_inc(rows_std, 1)
                    elif kind == "qkT":
                        t = step[1]
                        n = tile_rows(t)
                        e.wait_ge(ready(("q", t)), filled(("q", t)))
                        e.activation(q_t[:, :, token_slice(t)], aux[:, 0, :].rearrange("p (m n) -> p m n", m=4)[:, :, 0:n], ACT.Copy, scale=HD ** -0.5).then_inc(free(("q", t)), 1)
                        e.wait_ge(ready(("ki", t)), filled(("ki", t)))
                        e.activation(ki_t[:, token_slice(t)], aux[:, 3, 0:n], ACT.Copy).then_inc(free(("ki", t)), 1)
                    elif kind == "z":
                        def la_rows(i):
                            n = tile_rows(2 * i)
                            tiles = min(2, NTILE - 2 * i)
                            return la[0:n, 2 * i:2 * i + tiles, :].rearrange("p t n -> p (t n)"), n, tiles
                        for i in range(3):
                            dst, n, tiles = la_rows(i)
                            e.wait_ge(ready(("z", i)), filled(("z", i)))
                            e.activation(dst, aux[0:n, uses["z", i][0], 0:tiles * GK_W], ACT.Abs).then_inc(z_abs, 1)
                        e.wait_ge(z_abs, 3)
                        for i in range(3):
                            dst = la_rows(i)[0]
                            e.activation(dst, dst, ACT.Exp, scale=-1.0).then_inc(z_exp, 1)
                        e.wait_ge(z_exp, 3)
                        for i in range(3):
                            dst = la_rows(i)[0]
                            e.activation(dst, dst, ACT.Ln, bias=1.0).then_inc(ln_done, 1)
                    elif kind == "decay":
                        e.wait_ge(decay_done, 1)
                        e.activation(e_t[:], d_t[:], ACT.Exp)
                        e.activation(d_t[:], d_t[:], ACT.Exp, scale=-1.0)
                        e.activation(e_ref[:], b_ref[:], ACT.Exp)
                        e.activation(e_end[:], b_end[:], ACT.Exp)
                        e.activation(e_add[:], e_add[:], ACT.Exp).then_inc(exps_done, 1)
                    elif kind == "index":
                        j = step[1]
                        L = (j + 1) * P
                        for h in range(IDX_HEADS):
                            key = ("index", j, h)
                            dst = gate_slot(key)
                            e.wait_ge(ready(key), filled(key))
                            e.activation(dst[:, 0:L], aux[:, uses[key][0], 0:L], ACT.Relu, scale=IDX_SCALE).then_inc(free(key), 1)
                    elif kind == "kidx":
                        g = step[1]
                        if g:
                            e.wait_ge(ready(("sscore", g - 1)), filled(("sscore", g - 1)))
                        for u in range(2):
                            key = ("kidxT", 2 * g + u)
                            e.wait_ge(ready(key), filled(key))
                            e.activation(kidx_t[:, u, :], aux[0:ID, 3, :], ACT.Copy).then_inc(free(key), 1)
                    elif (kind == "chunk" and step[1] % 4 == 3) or kind == "sgla_out":
                        t = step[1] // 4 if kind == "chunk" else 4
                        n = tile_rows(t)
                        for par, key in enumerate((("oE", t), ("oO", t))):
                            e.wait_ge(ready(key), filled(key))
                            e.activation(gla_o[:, par::2, token_slice(t)], aux[:, par, 0:2 * P].rearrange("p (g n) -> p g n", g=2)[:, :, 0:n], ACT.Copy).then_inc(free(key), 1)
                    elif kind == "gnorm":
                        h = step[1]
                        dst = stage_slot(("gn", h))
                        for par in range(2):
                            e.wait_ge(free((("oE", 4), ("oO", 4))[par]), emptied((("oE", 4), ("oO", 4))[par]))
                        e.activation(dst, gla_o[:, h, :], ACT.Square).then_inc(staged, 1)
                        root = gate_slot(("gn", h))
                        for k in range(2):
                            key = ("gn", h, k)
                            e.wait_ge(ready(key), filled(key))
                            e.activation(root[:, k * HALF:(k + 1) * HALF], aux[:, k, 0:HALF], ACT.Sqrt, bias=eps_t[:], scale=1.0 / DV).then_inc(free(key), 1)
                    elif kind == "gout":
                        h = step[1]
                        e.wait_ge(gnorm_done, h + 1)
                        e.wait_ge(ready(("g", last_gtb)), filled(("g", last_gtb)))
                        e.activation(in_hi[:, 4 + h, :], gla_o[:, h, :], ACT.Copy).then_inc(split_hi, 1)
                    elif kind == "sample":
                        i = step[1]
                        if i == 0:
                            e.wait_ge(masks_done, 4)
                        for b in (2 * i, 2 * i + 1):
                            if i:
                                e.wait_ge(ready(("slog", i - 1)), filled(("slog", i - 1)))
                            e.wait_ge(ready(("kcT", b)), filled(("kcT", b)))
                            e.activation(k_past[:, b % 2, :, :].rearrange("p a n -> p (a n)"), aux[:, 2, :], ACT.Copy).then_inc(free(("kcT", b)), 1)
                        e.wait_ge(max_done, i + 1)
                        if i >= 2:
                            e.wait_ge(ready(("spT", i - 2)), filled(("spT", i - 2)))
                        e.activation(p_t[:, i % 2, 0:NEW_KEYS], aux[:, uses["slog", i][0], 0:NEW_KEYS], ACT.Exp, bias=neg_max_s[:, i:i + 1], accum_out=p_sum_s[:, i:i + 1]).then_inc(free(("slog", i)), 1)
                    elif kind == "sample_out":
                        e.wait_ge(ready(("so",)), filled(("so",)))
                        for jj in range(4):
                            src = slice(64 * (jj // 2), 64 * (jj // 2) + 64)
                            dst = slice(64 * (jj % 2), 64 * (jj % 2) + 64)
                            for pair in range(2):
                                e.activation(in_hi[dst, jj // 2 + 2 * pair, SEQ:NT].rearrange("p (b t) -> p b t", t=DEC_SEQ), aux[src, 3, :].rearrange("p (b a q t) -> p b a q t", b=8, a=2, q=4)[:, :, pair, jj, :], ACT.Copy).then_inc(attn_hi, 1)
                    elif kind == "attn":
                        _, j, h = step
                        n = j * N_HEADS + h
                        L = (j + 1) * P
                        if n == 0:
                            e.wait_ge(ready(("spT", 3)), filled(("spT", 3)))
                            exp_head(0)
                        if n + 1 < len(ORDER):
                            exp_head(n + 1)
                        if n % 2 == 0:
                            e.wait_ge(ready(("pT", j, h)), filled(("pT", j, h)))
                            if n >= 2:
                                e.wait_ge(*pv_used(n - 2))
                            e.activation(pT_t[:, n % 2, 0:j + 1, :].rearrange("p s n -> p (s n)"), aux[:, 2, 0:L], ACT.Copy).then_inc(free(("pT", j, h)), 1)
                    elif kind == "attn_out":
                        j = step[1]
                        e.wait_ge(ready(("oT", j)), filled(("oT", j)))
                        e.activation(in_hi[:, 0:4, j * P:(j + 1) * P], aux[:, 2, :].rearrange("p (m n) -> p m n", m=4), ACT.Copy).then_inc(attn_hi, 1)

            layers(e, body)

        @block.vector
        def _(e):
            e.memset(ones[:], 1.0).then_inc(once, 1)
            e.memset(eps_t[:], EPS).then_inc(once, 1)
            e.wait_ge(x_loaded, 16 * (3 + NTILE))
            e.tensor_copy(ident_b[:], ident).then_inc(once, 1)
            e.tensor_copy(tri_b[:], const("tri")).then_inc(once, 1)
            e.tensor_copy(repeat_b[:].rearrange("p b n -> p (b n)"), repeat_f[0:NS, :]).then_inc(once, 1)
            for kt in range(KD):
                e.wait_ge(x_turned, kt + 1)
                b0 = 2 * (kt % 2)
                e.tensor_copy(x_t[:, kt, 0:SEQ], aux[:, b0, :])
                e.tensor_copy(x_t[:, kt, SEQ:NT], aux[:, b0 + 1, 0:NS]).then_inc(x_filled, 1)

            def body(layer):
                turn = counter()

                def split_w(p):
                    e.wait_ge(w_hi_done, p + 1)
                    n = sum(part[2] for part in PANELS[p][2]) * P if PANELS[p][0] != "misc" else KD * P
                    e.tensor_tensor(w_lo[:, p % 2, 0:n], w_raw[:, p % RAW_RING, 0:n],
                                        w_hi[:, p % 2, 0:n].bitcast(F32), ALU.subtract).then_inc(w_lo_done, 1)
                    e.wait_ge(w_lo_done, turn(w_lo_done))

                def low_part(key, dst, src, hi):
                    e.wait_ge(split_hi, plan.split_use[key] + 1)
                    e.tensor_tensor(dst, src, hi.bitcast(F32), ALU.subtract).then_inc(split_lo, 1)
                    e.wait_ge(split_lo, turn(split_lo))

                def max_head(n):
                    j, h = ORDER[n]
                    L = (j + 1) * P
                    key = ("log", j, h)
                    e.wait_ge(ready(key), filled(key))
                    e.tensor_reduce(neg_max[:, j % 2, h:h + 1], aux[:, uses[key][0], 0:L], AX_X, ALU.max,
                                        negate=True).then_inc(max_done, 1)
                    e.wait_ge(max_done, turn(max_done))

                split_w(0)
                for step in plan.steps:
                    kind = step[0]
                    if kind == "panel":
                        p = step[1]
                        if p + 1 < N_PANELS:
                            split_w(p + 1)
                        kind_p, idx, _ = PANELS[p]
                        g = plan.groups[p][0]
                        key = ("g", g)
                        src = slot(g)
                        if kind_p in STAGED:
                            pass
                        elif kind_p == "gr":
                            u = plan.gate_tmp_use["gr", idx]
                            e.wait_ge(gated, gated_no["gr", idx])
                            e.tensor_tensor(halves(gla_r[:, idx, :]), src, halves(gate_tmp[:, u % 2, :]), ALU.mult).then_inc(free(key), 1)
                            e.wait_ge(free(key), emptied(key))
                        elif kind_p == "oab":
                            for gate, gg in ((gate_a, g), (gate_b, g + 1)):
                                k2 = ("g", gg)
                                e.wait_ge(free(("g", plan.groups[gate_panel[gate is gate_b] + idx][0])), emptied(("g", plan.groups[gate_panel[gate is gate_b] + idx][0])))
                                e.wait_ge(ready(k2), filled(k2))
                                e.tensor_tensor(halves(gate[:, idx, :]), slot(gg), halves(gate[:, idx, :]),
                                                    ALU.mult).then_inc(free(k2), 1)
                                e.wait_ge(free(k2), emptied(k2))
                            u = plan.split_use["merge", idx] % 2
                            e.wait_ge(free(("g", g)), emptied(("g", g)))
                            e.tensor_tensor(tmp[:, u, :], gate_a[:, idx, :], gate_b[:, idx, :], ALU.add).then_inc(split_src, 1)
                            e.wait_ge(split_src, turn(split_src))
                            low_part(("merge", idx), mid_lo[:, idx, :], tmp[:, u, :], mid_hi[:, idx, :])
                        elif kind_p in ("o", "down"):
                            m = idx if kind_p == "o" else idx[1]
                            e.wait_ge(ready(key), filled(key))
                            e.tensor_tensor(halves(x_t[:, m, :]), src, halves(x_t[:, m, :]), ALU.add).then_inc(free(key), 1)
                            e.wait_ge(free(key), emptied(key))
                        elif kind_p == "gate":
                            u = plan.gate_tmp_use["gate", idx]
                            v = plan.split_use["ff", idx] % 2
                            e.wait_ge(gated, gated_no["gate", idx])
                            e.tensor_tensor(halves(tmp[:, v, :]), src, halves(gate_tmp[:, u % 2, :]), ALU.mult).then_inc(free(key), 1)
                            e.wait_ge(free(key), emptied(key))
                        elif kind_p == "up":
                            part, i = idx
                            v = plan.split_use["ff", idx] % 2
                            e.wait_ge(ready(key), filled(key))
                            e.wait_ge(free(("g", g - 1)), emptied(("g", g - 1)))
                            e.tensor_tensor(halves(tmp[:, v, :]), src, halves(tmp[:, v, :]), ALU.mult).then_inc(free(key), 1)
                            e.wait_ge(free(key), emptied(key))
                            k = i - sum(FF_PARTS[:part])
                            low_part(("ff", idx), mid_lo[:, k, :], tmp[:, v, :], mid_hi[:, k, :])
                    elif kind == "gains":
                        e.wait_ge(ready(("gains",)), filled(("gains",)))
                        e.tensor_copy(gains[:], aux[:, 2, 0:2 * KD + 1]).then_inc(free(("gains",)), 1)
                        e.wait_ge(free(("gains",)), emptied(("gains",)))
                    elif kind == "norm":
                        norm = step[1]
                        for h in range(2):
                            e.wait_ge(free(("stat", norm, h)), emptied(("stat", norm, h)))
                        e.reciprocal(rstd[:], rstd[:]).then_inc(dve_step, 1)
                        e.wait_ge(dve_step, turn(dve_step))
                        e.wait_ge(small_ready, 16 * SMALL_LOADS)
                        for kt in range(KD + 1):
                            if kt < KD:
                                u = plan.split_use["norm", norm, kt] % 2
                                e.scalar_tensor_tensor(out=tmp[:, u, :], in0=x_t[:, kt, :],
                                                           scalar=gains[:, (norm - 1) * KD + kt:(norm - 1) * KD + kt + 1], in1=rstd[:],
                                                           op0=ALU.mult, op1=ALU.mult).then_inc(split_src, 1)
                                e.wait_ge(split_src, turn(split_src))
                            if kt > 0:
                                key = ("norm", norm, kt - 1)
                                low_part(key, in_lo[:, kt - 1, :], tmp[:, plan.split_use[key] % 2, :],
                                         in_hi[:, kt - 1, :])
                    elif kind == "row":
                        p = step[1]
                        kind_p, idx, _ = PANELS[p]
                        bx, by = uses["rowX", p][0], uses["rowY", p][0]
                        if kind_p == "gv":
                            buf, lo, w, src0 = gv_rows, idx * P, P, 0
                        elif kind_p == "q":
                            buf, lo, w, src0 = q_rows, idx * P, P, 0
                        elif kind_p in ("k", "v"):
                            buf, lo, w, src0 = kv_rows, idx * P + (KV_W if kind_p == "v" else 0), P, 0
                        elif kind_p == "qi":
                            buf, lo, w, src0 = q_rows, ATTN_W + idx * P, P, 0
                        else:
                            buf, lo, w, src0 = q_rows, ATTN_W + IDX_W, ID, MISC_KI
                        x3 = aux[:, bx, :].rearrange("p (t n) -> p t n", t=4)
                        if kind_p == "q":
                            at0 = HEAD_TILE[2 * idx][0] * 2 + HEAD_TILE[2 * idx][1]
                            heads = q_rows[:, :, 0:ATTN_W].rearrange("p t (h d) -> p t h d", d=HD)
                            e.wait_ge(ready(("rowX", p)), filled(("rowX", p)))
                            e.tensor_copy(heads[:, 0:4, at0:at0 + 3:2, :],
                                              x3.rearrange("p t (h d) -> p t h d", d=HD)).then_inc(free(("rowX", p)), 1)
                            e.wait_ge(free(("rowX", p)), emptied(("rowX", p)))
                            e.wait_ge(ready(("rowY", p)), filled(("rowY", p)))
                            e.tensor_copy(heads[0:NS, 4, at0:at0 + 3:2, :],
                                              aux[0:NS, by, 0:P].rearrange("p (h d) -> p h d", d=HD)).then_inc(free(("rowY", p)), 1)
                            e.wait_ge(free(("rowY", p)), emptied(("rowY", p)))
                            continue
                        e.wait_ge(ready(("rowX", p)), filled(("rowX", p)))
                        if kind_p == "misc":
                            e.tensor_copy(wi_rows[:, 0:4, :], x3[:, :, MISC_WI:MISC_WI + IDX_HEADS]).then_inc(dve_step, 1)
                            e.wait_ge(dve_step, turn(dve_step))
                        e.tensor_copy(buf[:, 0:4, lo:lo + w], x3[:, :, src0:src0 + w]).then_inc(free(("rowX", p)), 1)
                        e.wait_ge(free(("rowX", p)), emptied(("rowX", p)))
                        e.wait_ge(ready(("rowY", p)), filled(("rowY", p)))
                        if kind_p == "misc":
                            e.tensor_copy(wi_rows[0:NS, 4, :], aux[0:NS, by, MISC_WI:MISC_WI + IDX_HEADS]).then_inc(dve_step, 1)
                            e.wait_ge(dve_step, turn(dve_step))
                        e.tensor_copy(buf[0:NS, 4, lo:lo + w], aux[0:NS, by, src0:src0 + w]).then_inc(free(("rowY", p)), 1)
                        e.wait_ge(free(("rowY", p)), emptied(("rowY", p)))
                    elif kind == "qknorm":
                        t = step[1]
                        n = tile_rows(t)
                        q3 = q_rows[0:n, t, :].rearrange("p (h d) -> p h d", d=HD)
                        k3 = kv_rows[0:n, t, 0:KV_W].rearrange("p (h d) -> p h d", d=HD)
                        e.wait_ge(rows_sq, t + 1)
                        e.tensor_reduce(sums[0:n, 0:13], sq_rows[0:n, :, :], AX_X, ALU.add).then_inc(rows_ss, 1)
                        e.wait_ge(rows_ss, turn(rows_ss))
                        e.wait_ge(rows_std, t + 1)
                        e.reciprocal(sums[0:n, 0:13], sums[0:n, 0:13]).then_inc(dve_step, 1)
                        e.wait_ge(dve_step, turn(dve_step))
                        parts = ((q3[:, 0:8, :], 0, 8, 0), (k3, 8, 4, 1), (q3[:, 12:13, :], 12, 1, 2))
                        for x3, s0, nh, gi in parts:
                            e.tensor_tensor(x3, x3, bcast(sums[0:n, s0:s0 + nh], 2, HD), ALU.mult).then_inc(dve_step, 1)
                            e.wait_ge(dve_step, turn(dve_step))
                        for x3, s0, nh, gi in parts:
                            e.tensor_tensor(x3, x3, bcast(qk_g[0:n, gi, :], 1, nh), ALU.mult).then_inc(dve_step, 1)
                            e.wait_ge(dve_step, turn(dve_step))
                        cos = const("cos")[0:n, t * ROT:(t + 1) * ROT]
                        sin = const("sin")[0:n, t * ROT:(t + 1) * ROT]
                        for last, x3, nh in ((False, q3, 13), (True, k3, 4)):
                            e.tensor_tensor(rope1[0:n, 0:nh, :], x3[:, :, 0:ROT], bcast(cos, 1, nh), ALU.mult).then_inc(dve_step, 1)
                            e.wait_ge(dve_step, turn(dve_step))
                            e.tensor_tensor(rope2[0:n, 0:nh, 0:HALF_ROT], x3[:, :, HALF_ROT:ROT],
                                                bcast(sin[:, 0:HALF_ROT], 1, nh), ALU.mult).then_inc(dve_step, 1)
                            e.wait_ge(dve_step, turn(dve_step))
                            e.tensor_tensor(rope2[0:n, 0:nh, HALF_ROT:ROT], x3[:, :, 0:HALF_ROT],
                                                bcast(sin[:, HALF_ROT:ROT], 1, nh), ALU.mult).then_inc(dve_step, 1)
                            e.wait_ge(dve_step, turn(dve_step))
                            raised = rows_done if last else dve_step
                            e.tensor_tensor(x3[:, :, 0:ROT], rope1[0:n, 0:nh, :], rope2[0:n, 0:nh, :], ALU.add).then_inc(raised, 1)
                            e.wait_ge(raised, turn(raised))
                    elif kind == "qkT":
                        t = step[1]
                        n = tile_rows(t)
                        key = ("ik", t)
                        e.wait_ge(ready(key), filled(key))
                        v = aux[:, 1, :].rearrange("p (m n) -> p m n", m=4)
                        e.tensor_copy(qi_t[:, :, token_slice(t)], v[:, 0:2, 0:n]).then_inc(dve_step, 1)
                        e.wait_ge(dve_step, turn(dve_step))
                        e.tensor_copy(k_t[:, :, token_slice(t)], v[:, 2:4, 0:n]).then_inc(free(key), 1)
                        e.wait_ge(free(key), emptied(key))
                    elif kind == "z":
                        for i in range(3):
                            n = tile_rows(2 * i)
                            tiles = min(2, NTILE - 2 * i)
                            dst = la[0:n, 2 * i:2 * i + tiles, :].rearrange("p t n -> p (t n)")
                            e.wait_ge(ln_done, i + 1)
                            e.scalar_tensor_tensor(out=dst, in0=aux[0:n, uses["z", i][0], 0:tiles * GK_W],
                                                       scalar=0.0, in1=dst, op0=ALU.min, op1=ALU.subtract).then_inc(free(("z", i)), 1)
                            e.wait_ge(free(("z", i)), emptied(("z", i)))
                    elif kind == "decay":
                        for i in range(3):
                            if i < 2:
                                v = aux[:, i, :].rearrange("p (c s) -> p c s", s=CHUNK)
                                ref, end = b_ref[:, i, 0:16], b_end[:, i, 0:16]
                                mid, last = CHUNK // 2 - 1, CHUNK - 1
                                dst = d_t[:, i, 0:SEQ].rearrange("p (c s) -> p c s", s=CHUNK)
                                rb = bcast(ref, 2, CHUNK)
                                e.wait_ge(ready(("b", i)), filled(("b", i)))
                                e.tensor_copy(ref, v[:, :, mid]).then_inc(dve_step, 1)
                                e.wait_ge(dve_step, turn(dve_step))
                                e.tensor_copy(end, v[:, :, last]).then_inc(dve_step, 1)
                                e.wait_ge(dve_step, turn(dve_step))
                                e.tensor_tensor(dst, v, rb, ALU.subtract).then_inc(free(("b", i)), 1)
                                e.wait_ge(free(("b", i)), emptied(("b", i)))
                            else:
                                e.wait_ge(ready(("b", 2)), filled(("b", 2)))
                                for hp in range(2):
                                    v = aux[:, 2, hp * NS:(hp + 1) * NS].rearrange("p (c s) -> p c s", s=DEC_SEQ)
                                    e.tensor_copy(b_ref[:, hp, 16:24], v[:, :, DEC_SEQ // 2 - 1]).then_inc(dve_step, 1)
                                    e.wait_ge(dve_step, turn(dve_step))
                                    e.tensor_copy(b_end[:, hp, 16:24], v[:, :, DEC_SEQ - 1]).then_inc(dve_step, 1)
                                    e.wait_ge(dve_step, turn(dve_step))
                                for hp in range(2):
                                    v = aux[:, 2, hp * NS:(hp + 1) * NS].rearrange("p (c s) -> p c s", s=DEC_SEQ)
                                    dst = d_t[:, hp, SEQ:NT].rearrange("p (c s) -> p c s", s=DEC_SEQ)
                                    rb = bcast(b_ref[:, hp, 16:24], 2, DEC_SEQ)
                                    if hp == 0:
                                        e.tensor_tensor(dst, v, rb, ALU.subtract).then_inc(dve_step, 1)
                                        e.wait_ge(dve_step, turn(dve_step))
                                    else:
                                        e.tensor_tensor(dst, v, rb, ALU.subtract).then_inc(free(("b", 2)), 1)
                                        e.wait_ge(free(("b", 2)), emptied(("b", 2)))
                        e.tensor_tensor(e_add[:], b_end[:], b_ref[:], ALU.subtract).then_inc(decay_done, 1)
                        e.wait_ge(decay_done, turn(decay_done))
                    elif kind == "gexp":
                        e.memset(g_attn[:], 0.0).then_inc(dve_step, 1)
                        e.wait_ge(dve_step, turn(dve_step))
                        e.wait_ge(exps_done, 1)
                        for x, y in ((gq, "gq"), (gk, "gk")):
                            for i in range(2):
                                e.wait_ge(free(("g", gqk_group[y, i])), emptied(("g", gqk_group[y, i])))
                        e.tensor_tensor(gq[:], gq[:], e_t[:], ALU.mult).then_inc(dve_step, 1)
                        e.wait_ge(dve_step, turn(dve_step))
                        e.tensor_tensor(gk[:], gk[:], d_t[:], ALU.mult).then_inc(gqk_done, 1)
                        e.wait_ge(gqk_done, turn(gqk_done))
                    elif kind == "qiz":
                        e.wait_ge(free(("ik", 4)), emptied(("ik", 4)))
                        for h in range(IDX_HEADS):
                            src = qi_t[64 * (h % 2):64 * (h % 2) + 64, h // 2, SEQ:NT]
                            raised = qiz_done if h == IDX_HEADS - 1 else dve_step
                            e.tensor_copy(qiz[:, :, h * DEC_SEQ:(h + 1) * DEC_SEQ],
                                              src.rearrange("p (b t) -> p b t", t=DEC_SEQ)).then_inc(raised, 1)
                            e.wait_ge(raised, turn(raised))
                        for g in range(2):
                            e.wait_ge(ready(("wi", g)), filled(("wi", g)))
                            e.tensor_tensor_reduce(out=wi_tmp[:, g, :], in0=aux[:, uses["wi", g][0], 0:IDX_HEADS],
                                                       in1=const("head_rows"), scale=IDX_SCALE, scalar=0.0,
                                                       op0=ALU.mult, op1=ALU.add, accum_out=wi_s[:, g:g + 1]).then_inc(free(("wi", g)), 1)
                            e.wait_ge(free(("wi", g)), emptied(("wi", g)))
                    elif kind == "kidx":
                        g = step[1]
                        e.wait_ge(ready(("sscore", g)), filled(("sscore", g)))
                        e.wait_ge(free(("wi", g)), emptied(("wi", g)))
                        e.tensor_scalar(s_heads[:, g, :], aux[:, 2, 0:NEW_KEYS], 0.0, wi_s[:, g:g + 1],
                                            ALU.max, ALU.mult).then_inc(free(("sscore", g)), 1)
                        e.wait_ge(free(("sscore", g)), emptied(("sscore", g)))
                    elif kind == "sindex":
                        e.memset(scores_s[:, NEW_KEYS:SAMPLE_W], -MASKED).then_inc(dve_step, 1)
                        e.wait_ge(dve_step, turn(dve_step))
                        e.wait_ge(ready(("ssum",)), filled(("ssum",)))
                        e.tensor_copy(scores_s[:, 0:PAST], aux[0:NS, 3, 0:PAST]).then_inc(dve_step, 1)
                        e.wait_ge(dve_step, turn(dve_step))
                        e.tensor_tensor(scores_s[:, PAST:NEW_KEYS], aux[0:NS, 3, PAST:NEW_KEYS],
                                            const("own_new", NS), ALU.add).then_inc(free(("ssum",)), 1)
                        e.wait_ge(free(("ssum",)), emptied(("ssum",)))
                    elif kind == "index":
                        j = step[1]
                        L = (j + 1) * P
                        lo, hi = score_cols[j]
                        acc = scores[:, lo:hi]
                        for h in range(IDX_HEADS):
                            key = ("index", j, h)
                            src = gate_tmp[:, plan.gate_tmp_use[key] % 2, 0:L]
                            e.wait_ge(free(key), emptied(key))
                            if h == 0:
                                e.tensor_scalar(acc, src, wi_rows[:, j, 0:1], None, ALU.mult).then_inc(index_added, 1)
                                e.wait_ge(index_added, turn(index_added))
                            else:
                                e.scalar_tensor_tensor(out=acc, in0=src, scalar=wi_rows[:, j, h:h + 1], in1=acc,
                                                           op0=ALU.mult, op1=ALU.add).then_inc(index_added, 1)
                                e.wait_ge(index_added, turn(index_added))
                        e.tensor_tensor(acc[:, L - P:L], acc[:, L - P:L], const("tri"), ALU.add).then_inc(dve_step, 1)
                        e.wait_ge(dve_step, turn(dve_step))
                    elif kind == "topk":
                        _, w, r = step
                        if w == "s":
                            buf, t8, out, last = scores_s[:], top8s, mask_s[:], (TOPK_SAMPLE + PAD_TOP) // 8 - 1
                            width = NEW_KEYS
                        else:
                            lo, hi = score_cols[w]
                            buf, t8, last, width = scores[:, lo:hi], top8, TOPK_PROMPT // 8 - 1, (w + 1) * P
                            out = mask_b[:, w - 1, 0:width]
                        e.max(out=t8[0:buf.shape[0], :], in_=buf).then_inc(dve_step, 1)
                        e.wait_ge(dve_step, turn(dve_step))
                        e.match_replace(out=buf, in_to_replace=t8[0:buf.shape[0], :], in_values=buf,
                                            imm_value=TAKEN).then_inc(dve_step, 1)
                        e.wait_ge(dve_step, turn(dve_step))
                        if r == last:
                            e.tensor_scalar(out, buf[:, 0:width], TAKEN / 1.5, MASKED, ALU.is_gt, ALU.mult).then_inc(masks_done, 1)
                            e.wait_ge(masks_done, turn(masks_done))
                    elif kind == "intra":
                        t = step[1]
                        n = tile_rows(t)
                        e.wait_ge(ready(("kT", t)), filled(("kT", t)))
                        e.tensor_copy(gk_rows[0:n, t % 2, :], aux[0:n, 3, 0:GK_W]).then_inc(free(("kT", t)), 1)
                        e.wait_ge(free(("kT", t)), emptied(("kT", t)))
                        if t == 4:
                            e.wait_ge(ready(("inE", t)), filled(("inE", t)))
                            e.memset(g_attn[0:NS, :, :], 0.0).then_inc(dve_step, 1)
                            e.wait_ge(dve_step, turn(dve_step))
                        for par, key in enumerate((("inE", t), ("inO", t))):
                            causal = const("chunk_sum") if t < 4 else const("sample_sum", NS)
                            src = aux[0:n, uses[key][0], 0:2 * P].rearrange("p (g n) -> p g n", g=2)[:, :, 0:n]
                            e.wait_ge(ready(key), filled(key))
                            e.copy_predicated(out=g_attn[0:n, par::2, 0:n], mask=bcast(causal, 1, 2).bitcast(U32),
                                                  data=src).then_inc(free(key), 1)
                            e.wait_ge(free(key), emptied(key))
                    elif kind == "chunk":
                        c = step[1]
                        key = ("kv", c)
                        ps = aux[:, 2, 0:2 * DV].rearrange("p (g n) -> p g n", g=2)
                        e.wait_ge(ready(key), filled(key))
                        if c == 0:
                            e.tensor_tensor(state[:], ps, bcast(e_add[:, :, c], 2, DV), ALU.mult).then_inc(free(key), 1)
                            e.wait_ge(free(key), emptied(key))
                        else:
                            e.tensor_tensor(state_add[:], ps, bcast(e_add[:, :, c], 2, DV), ALU.mult).then_inc(free(key), 1)
                            e.wait_ge(free(key), emptied(key))
                            e.tensor_tensor(state[:], state[:], bcast(e_end[:, :, c], 2, DV), ALU.mult).then_inc(dve_step, 1)
                            e.wait_ge(dve_step, turn(dve_step))
                            raised = state_done if c == N_CHUNK - 1 else dve_step
                            e.tensor_tensor(state[:], state[:], state_add[:], ALU.add).then_inc(raised, 1)
                            e.wait_ge(raised, turn(raised))
                        if c < N_CHUNK - 1:
                            e.tensor_tensor(state_in[:], state[:], bcast(e_ref[:, :, c + 1], 2, DV), ALU.mult).then_inc(state_done, 1)
                            e.wait_ge(state_done, turn(state_done))
                    elif kind == "sround":
                        r = step[1]

                        def per_batch(x):
                            return bcast(x[:, :, 16 + 2 * r:18 + 2 * r].rearrange("p g b -> p b g"), 3, DV)
                        e.wait_ge(s_state_ready[r % 2], 16 * 4 * (r // 2 + 1))
                        if r:
                            e.wait_ge(ready(("skv", r - 1)), filled(("skv", r - 1)))
                        st = s_state[:, r % 2, :, :, :]
                        e.tensor_tensor(s_state_in[:], st, per_batch(e_ref), ALU.mult).then_inc(dve_step, 1)
                        e.wait_ge(dve_step, turn(dve_step))
                        e.tensor_tensor(gk_one[:], bcast(gk_rows[0:NS, 0, :], 1, 2),
                                            bcast(const("batch_rows", NS)[:, 2 * r:2 * r + 2], 2, GK_W), ALU.mult).then_inc(s_in_done, 1)
                        e.wait_ge(s_in_done, turn(s_in_done))
                        e.tensor_tensor(st, st, per_batch(e_end), ALU.mult).then_inc(dve_step, 1)
                        e.wait_ge(dve_step, turn(dve_step))
                        e.wait_ge(ready(("skv", r)), filled(("skv", r)))
                        ps = aux[:, 2, :].rearrange("p (b g n) -> p b g n", b=2, g=2)
                        e.tensor_tensor(s_state_add[:], ps, per_batch(e_add), ALU.mult).then_inc(free(("skv", r)), 1)
                        e.wait_ge(free(("skv", r)), emptied(("skv", r)))
                        e.tensor_tensor(st, st, s_state_add[:], ALU.add).then_inc(s_out_done, 1)
                        e.wait_ge(s_out_done, turn(s_out_done))
                    elif kind == "gnorm":
                        h = step[1]
                        root = gate_tmp[:, plan.gate_tmp_use["gn", h] % 2, :]
                        for k in range(2):
                            e.wait_ge(free(("gn", h, k)), emptied(("gn", h, k)))
                        e.reciprocal(root, root).then_inc(dve_step, 1)
                        e.wait_ge(dve_step, turn(dve_step))
                        e.scalar_tensor_tensor(out=gla_o[:, h, :], in0=gla_o[:, h, :], scalar=gains[:, 2 * KD:2 * KD + 1],
                                                   in1=root, op0=ALU.mult, op1=ALU.mult).then_inc(dve_step, 1)
                        e.wait_ge(dve_step, turn(dve_step))
                        e.tensor_tensor(gla_o[:, h, :], gla_o[:, h, :], gla_r[:, h, :], ALU.mult).then_inc(gnorm_done, 1)
                        e.wait_ge(gnorm_done, turn(gnorm_done))
                    elif kind == "gout":
                        h = step[1]
                        low_part(("gout", h), in_lo[:, 4 + h, :], gla_o[:, h, :], in_hi[:, 4 + h, :])
                    elif kind == "qz":
                        e.wait_ge(state_stored, 16 * 2)
                        e.wait_ge(ready(("g", plan.groups[gtb_panels[1]][0])), filled(("g", plan.groups[gtb_panels[1]][0])))
                        e.memset(qz[:], 0.0).then_inc(dve_step, 1)
                        e.wait_ge(dve_step, turn(dve_step))
                        for h in range(N_HEADS):
                            tile, half = HEAD_TILE[h]
                            rows = slice(64 * half, 64 * half + 64)
                            if h == 0:
                                e.wait_ge(free(("q", 4)), emptied(("q", 4)))
                            raised = qz_done if h == N_HEADS - 1 else dve_step
                            e.tensor_copy(qz[rows, :, h // 4, h * DEC_SEQ:(h + 1) * DEC_SEQ],
                                              q_t[rows, tile, SEQ:NT].rearrange("p (b t) -> p b t", t=DEC_SEQ)).then_inc(raised, 1)
                            e.wait_ge(raised, turn(raised))
                    elif kind == "sample":
                        i = step[1]
                        e.wait_ge(ready(("slog", i)), filled(("slog", i)))
                        e.tensor_reduce(neg_max_s[:, i:i + 1], aux[:, uses["slog", i][0], 0:NEW_KEYS], AX_X,
                                            ALU.max, negate=True).then_inc(max_done, 1)
                        e.wait_ge(max_done, turn(max_done))
                        e.wait_ge(free(("slog", i)), emptied(("slog", i)))
                        e.reciprocal(p_inv_s[:, i:i + 1], p_sum_s[:, i:i + 1]).then_inc(dve_step, 1)
                        e.wait_ge(dve_step, turn(dve_step))
                        e.tensor_scalar(p_t[:, i % 2, 0:NEW_KEYS], p_t[:, i % 2, 0:NEW_KEYS],
                                            p_inv_s[:, i:i + 1], None, ALU.mult).then_inc(p_scaled, 1)
                        e.wait_ge(p_scaled, turn(p_scaled))
                        if i >= 2:
                            e.wait_ge(kc_free, 2 * i - 2)
                        e.wait_ge(ready(("spT", i)), filled(("spT", i)))
                        e.tensor_copy(pT_t[:, i % 2, 0:2, :], aux[:, 2, 0:2 * P].rearrange("p (s n) -> p s n", s=2)).then_inc(dve_step, 1)
                        e.wait_ge(dve_step, turn(dve_step))
                        e.tensor_copy(pT_t[0:NS, i % 2, 2, :], aux[0:NS, 2, 2 * P:3 * P]).then_inc(free(("spT", i)), 1)
                        e.wait_ge(free(("spT", i)), emptied(("spT", i)))
                    elif kind == "sample_out":
                        e.wait_ge(attn_hi, 8)
                        for jj in range(4):
                            src = slice(64 * (jj // 2), 64 * (jj // 2) + 64)
                            dst = slice(64 * (jj % 2), 64 * (jj % 2) + 64)
                            for pair in range(2):
                                kt = jj // 2 + 2 * pair
                                ins = e.tensor_tensor(
                                    in_lo[dst, kt, SEQ:NT].rearrange("p (b t) -> p b t", t=DEC_SEQ),
                                    aux[src, 3, :].rearrange("p (b a q t) -> p b a q t", b=8, a=2, q=4)[:, :, pair, jj, :],
                                    in_hi[dst, kt, SEQ:NT].bitcast(F32).rearrange("p (b t) -> p b t", t=DEC_SEQ),
                                    ALU.subtract)
                        ins.then_inc(free(("so",)), 1)
                        e.wait_ge(free(("so",)), emptied(("so",)))
                    elif kind == "attn":
                        _, j, h = step
                        n = j * N_HEADS + h
                        L = (j + 1) * P
                        if n == 0:
                            max_head(0)
                        if n + 1 < len(ORDER):
                            max_head(n + 1)
                        if n % 2 == 1:
                            if n >= 2:
                                e.wait_ge(*pv_used(n - 2))
                            e.wait_ge(ready(("pT", j, h)), filled(("pT", j, h)))
                            e.tensor_copy(pT_t[:, n % 2, 0:j + 1, :].rearrange("p s n -> p (s n)"), aux[:, 2, 0:L]).then_inc(free(("pT", j, h)), 1)
                            e.wait_ge(free(("pT", j, h)), emptied(("pT", j, h)))
                    elif kind == "attn_out":
                        j = step[1]
                        e.wait_ge(ready(("o", j)), filled(("o", j)))
                        e.reciprocal(p_inv[:], p_sum[:, j % 2, :]).then_inc(dve_step, 1)
                        e.wait_ge(dve_step, turn(dve_step))
                        e.tensor_tensor(o_rows[:].rearrange("p (h d) -> p h d", d=HD),
                                            aux[:, 3, :].rearrange("p (h d) -> p h d", d=HD), bcast(p_inv[:], 2, HD),
                                            ALU.mult).then_inc(free(("o", j)), 1)
                        e.wait_ge(free(("o", j)), emptied(("o", j)))
                        e.wait_ge(attn_hi, 8 + j + 1)
                        e.tensor_tensor(in_lo[:, 0:4, j * P:(j + 1) * P],
                                            aux[:, 2, :].rearrange("p (m n) -> p m n", m=4),
                                            in_hi[:, 0:4, j * P:(j + 1) * P].bitcast(F32), ALU.subtract).then_inc(free(("oT", j)), 1)
                        e.wait_ge(free(("oT", j)), emptied(("oT", j)))

            layers(e, body)
            for t in range(NTILE):
                e.wait_ge(y_turned, t + 1)
                n = tile_rows(t)
                for k in range(2):
                    e.tensor_copy(x_rows[0:n, t, k * 512:(k + 1) * 512],
                                  aux[0:n, 2 * (t % 2) + k, :]).then_inc(y_ready, 1)



_INS = ["x_prompt", "x_sample", "cache_k", "cache_v", "cache_kidx", "state_gla", "page_table", "norm1_g", "w_in",
        "q_norm_g", "k_norm_g", "kidx_norm_g", "gla_wa2", "gla_ba", "gla_onorm_g", "w_oa", "w_ob", "w_o", "norm2_g",
        "w_ffn_gu", "w_ffn_down"]
_OUTS = {
    "y_prompt": (1, SEQ, D_MODEL), "y_sample": (DEC_BATCH, DEC_SEQ, D_MODEL),
    "new_k_prompt": (DEPTH, 1, SEQ, N_KV, HD), "new_v_prompt": (DEPTH, 1, SEQ, N_KV, HD),
    "new_kidx_prompt": (DEPTH, 1, SEQ, ID), "new_gla_prompt": (DEPTH, 1, GH, DK, DV),
    "new_k_sample": (DEPTH, DEC_BATCH, DEC_SEQ, N_KV, HD), "new_v_sample": (DEPTH, DEC_BATCH, DEC_SEQ, N_KV, HD),
    "new_kidx_sample": (DEPTH, DEC_BATCH, DEC_SEQ, ID), "new_gla_sample": (DEPTH, DEC_BATCH, GH, DK, DV),
}

def kernel(**inputs):
    import concourse.bacc as bacc
    from concourse.bass_utils import run_bass_kernel_spmd

    nc = bacc.Bacc("TRN2", target_bir_lowering=False, num_devices=1, dynamic_dma_scratch_size=64)
    arrays, args = {}, {}
    for name in _INS:
        a = np.ascontiguousarray(inputs[name])
        arrays[f"in_{name}"] = a
        args[name] = nc.dram_tensor(f"in_{name}", a.shape, mybir.dt.from_np(a.dtype), kind="ExternalInput").ap()
    consts = const_array()
    arrays["in_consts"] = consts
    args["consts"] = nc.dram_tensor("in_consts", consts.shape, F32, kind="ExternalInput").ap()
    for name, shape in _OUTS.items():
        args[name] = nc.dram_tensor(f"out_{name}", shape, F32, kind="ExternalOutput").ap()
    build(nc, args)
    r = run_bass_kernel_spmd(nc, [arrays], core_ids=[0])
    return tuple(r.results[0][f"out_{name}"] for name in _OUTS)
```

```python
from contextlib import ExitStack

import numpy as np

import concourse.bass as bass
from concourse import mybir

F32 = mybir.dt.float32
F32R = mybir.dt.float32r
BF16 = mybir.dt.bfloat16
I32 = mybir.dt.int32
U32 = mybir.dt.uint32
ALU = mybir.AluOpType
ACT = mybir.ActivationFunctionType
AX_X = mybir.AxisListType.X

P = 128
DEPTH = 2
D_MODEL = 1024
SEQ = 512
DEC_BATCH = 8
DEC_SEQ = 8
NS = DEC_BATCH * DEC_SEQ
NT = SEQ + NS
NTILE = 5
PAGE = 128
N_PAGES = 2
PAST = PAGE * N_PAGES
N_POOL = 20
N_HEADS = 8
N_KV = 4
HD = 64
ROT = HD // 4
HALF_ROT = ROT // 2
THETA = 500000.0
IDX_HEADS = 4
ID = 64
TOPK_PROMPT = SEQ // 4
TOPK_SAMPLE = (PAST + DEC_SEQ) // 4
GH = 4
DK = 64
DV = 128
RANK = 16
TAU = 16.0
CHUNK = 32
D_FF = 2816
EPS = 1e-6
KD = D_MODEL // P
HALF = NT // 2
ATTN_W, KV_W, IDX_W = N_HEADS * HD, N_KV * HD, IDX_HEADS * ID
GK_W, GV_W = GH * DK, GH * DV
SPLITS = (ATTN_W, KV_W, KV_W, IDX_W, ID, IDX_HEADS, GK_W, GK_W, GV_W, RANK, GV_W, D_MODEL, D_MODEL)
OFFS = [sum(SPLITS[:i]) for i in range(len(SPLITS))]
O_Q, O_K, O_V, O_QI, O_KI, O_WI, O_GQ, O_GK, O_GV, O_GA, O_GR, O_GTA, O_GTB = OFFS
N_IN = sum(SPLITS)
MISC_KI = 32
MISC_WI = MISC_KI + ID
NEW_KEYS = PAST + NS
PAD_TOP = -TOPK_SAMPLE % 8
SAMPLE_W = NEW_KEYS + PAD_TOP
MASKED = -1e30
TAKEN = -3e38
IDX_SCALE = IDX_HEADS ** -0.5 * ID ** -0.5
FF_TILES = D_FF // P
FF_PARTS = (8, 8, 6)
N_CHUNK = SEQ // CHUNK
RAW_RING = 3
GLA_PANELS = 10
TOPK_EACH = 2


def tile_rows(t):
    return P if t < 4 else NS


def token_slice(t):
    return slice(t * P, t * P + tile_rows(t))


def bcast(ap, axis, n):
    dims = [list(d) for d in ap.ap]
    dims.insert(axis, [0, n])
    return bass.AP(ap.tensor, ap.offset, dims)


CONSTS = {}


def const_layout():
    at = 0
    for name, w in (("ident", P), ("chunk_sum", P), ("sample_sum", NS), ("tri", P), ("own_new", NS),
                    ("cos", NTILE * ROT), ("sin", NTILE * ROT), ("batch_rows", DEC_BATCH),
                    ("head_rows", IDX_HEADS), ("spread", 2 * P), ("gather", 2 * NS), ("repeat", 8 * NS)):
        CONSTS[name] = (at, at + w)
        at += w
    return at


CONST_W = const_layout()
KEPT_W = CONSTS["repeat"][0]


def const_array():
    c = np.zeros((P, CONST_W), np.float32)

    def put(name, a):
        lo, hi = CONSTS[name]
        a = a.reshape(a.shape[0], -1)
        assert a.shape[1] == hi - lo
        c[:a.shape[0], lo:hi] = a

    i = np.arange(P)
    put("ident", np.eye(P, dtype=np.float32))
    put("chunk_sum", ((i[:, None] // CHUNK == i[None] // CHUNK) & (i[:, None] <= i[None])) / np.float32(TAU))
    s = np.arange(NS)
    put("sample_sum", ((s[:, None] // DEC_SEQ == s[None] // DEC_SEQ) & (s[:, None] <= s[None])) / np.float32(TAU))
    put("tri", np.where(i[None] <= i[:, None], 0, MASKED).astype(np.float32))
    put("own_new", np.where((s[:, None] // DEC_SEQ == s[None] // DEC_SEQ) & (s[None] <= s[:, None]), 0,
                            MASKED).astype(np.float32))
    inv = np.power(np.float32(THETA), -np.arange(HALF_ROT, dtype=np.float32) * np.float32(2.0) / np.float32(ROT))
    pos = np.zeros((P, NTILE), np.float32)
    pos[:, :4] = i[:, None] + P * np.arange(4)[None]
    pos[:NS, 4] = PAST + s % DEC_SEQ
    ang = pos[:, :, None] * inv.astype(np.float32)[None, None]
    cos, sin = np.cos(ang).astype(np.float32), np.sin(ang).astype(np.float32)
    put("cos", np.concatenate([cos, cos], -1))
    put("sin", np.concatenate([-sin, sin], -1))
    put("batch_rows", (s[:, None] // DEC_SEQ == np.arange(DEC_BATCH)[None]).astype(np.float32))
    rb, rh, rt = i // 32, i // 8 % 4, i % 8
    put("head_rows", (rh[:, None] == np.arange(IDX_HEADS)[None]).astype(np.float32))
    sp = np.stack([(s[:, None] == (g * 4 + rb) * 8 + rt) for g in range(2)], 1).astype(np.float32)
    put("spread", sp)
    put("gather", np.ascontiguousarray(sp.transpose(2, 1, 0)))
    put("repeat", np.stack([(s[:, None] == b * 8 + s[None] % 8) for b in range(DEC_BATCH)], 1).astype(np.float32))
    return c


def make_panels():
    out = []
    for kind, off, n in (("q", O_Q, 4), ("k", O_K, 2), ("v", O_V, 2), ("qi", O_QI, 2)):
        out += [(kind, i, [("w_in", 0, KD, off + i * P, P, 0)]) for i in range(n)]
    out.append(("misc", 0, [("w_in", 0, KD, O_GA, MISC_KI, 0), ("w_in", 0, KD, O_KI, P - MISC_KI, MISC_KI)]))
    for kind, off, n in (("gq", O_GQ, 2), ("gk", O_GK, 2), ("gv", O_GV, 4), ("gr", O_GR, 4),
                         ("gta", O_GTA, 8), ("gtb", O_GTB, 8)):
        out += [(kind, i, [("w_in", 0, KD, off + i * P, P, 0)]) for i in range(n)]
    for j in range(KD):
        out.append(("oab", j, [("w_oa", 0, 4, j * P, P, 0), ("w_ob", 0, 4, j * P, P, 4 * P)]))
    for j in range(KD):
        out.append(("o", j, [("w_o", 0, KD, j * P, P, 0)]))
    first = 0
    for part, n in enumerate(FF_PARTS):
        for i in range(first, first + n):
            out.append(("gate", (part, i), [("w_ffn_gu", 0, KD, i * P, P, 0)]))
            out.append(("up", (part, i), [("w_ffn_gu", 0, KD, D_FF + i * P, P, 0)]))
        for m in range(KD):
            out.append(("down", (part, m), [("w_ffn_down", first * P, n, m * P, P, 0)]))
        first += n
    return out


PANELS = make_panels()
N_PANELS = len(PANELS)
assert N_PANELS % RAW_RING == 0
STAGED = ("q", "k", "v", "qi", "misc", "gv")
RAW_READY = []
_count = [0] * RAW_RING
for _p, (_, _, _parts) in enumerate(PANELS):
    _count[_p % RAW_RING] += len(_parts)
    RAW_READY.append(_count[_p % RAW_RING])
SMALL_LOADS = 8


class Plan:

    def __init__(self):
        self.steps = []
        self.uses = {}
        self.per_bank = [0] * 6
        self.slot_keys = []
        self.groups = {}
        n = 0
        for p, (kind, idx, parts) in enumerate(PANELS):
            self.groups[p] = list(range(n, n + (2 if kind == "oab" else 1)))
            n += len(self.groups[p])
        self.n_groups = n
        self.stage_use = {}
        self.stage_release = []
        self.gate_tmp_use = {}
        self.gate_tmp_release = []
        self.split_use = {}
        self.build()

    def open(self, key, bank):
        self.uses[key] = (bank, self.per_bank[bank])
        self.per_bank[bank] += 1

    def stage(self, key, release):
        self.stage_use[key] = len(self.stage_release)
        self.stage_release.append(release)

    def gate_tmp(self, key, release):
        self.gate_tmp_use[key] = len(self.gate_tmp_release)
        self.gate_tmp_release.append(release)

    def split(self, key):
        self.split_use[key] = len(self.split_use)

    def add(self, *step):
        self.steps.append(step)

    def start(self, p):
        for g in self.groups[p]:
            self.open(("g", g), 4 + g % 2)
        self.add("panel", p)

    def finish(self, p):
        kind, idx, _ = PANELS[p]
        g = self.groups[p][0]
        if kind in ("gr", "gate"):
            self.gate_tmp((kind, idx), ("bank_free", ("g", g)))
        if kind in STAGED:
            self.stage(("row", p), ("bank_ready", ("rowY", p)))
        if kind == "oab":
            self.split(("merge", idx))
        if kind == "up":
            self.split(("ff", idx))
        self.add("post", p)

    def panel(self, p):
        self.start(p)
        for i in range(KD):
            self.add("part", p, i)
        self.finish(p)

    def woven(self, panels, items):
        pieces = len(panels) * KD
        done = 0
        for n in range(len(items) + 1):
            while done * max(len(items), 1) < n * pieces:
                p, i = panels[done // KD], done % KD
                if i == 0:
                    self.start(p)
                self.add("part", p, i)
                if i == 0 and PANELS[p - 1][0] in STAGED:
                    self.row(p - 1)
                if i == KD - 1:
                    self.finish(p)
                done += 1
            if n < len(items):
                for step in items[n]:
                    self.extra_step(step)

    def stat(self, norm, kt):
        if kt == 0:
            self.open(("stat", norm, 0), 0)
            self.open(("stat", norm, 1), 1)
        last = kt == KD - 1
        self.stage(("stat", norm, kt), ("bank_ready", ("stat", norm, 1)) if last else ("stage_read", self.n_read + 1))
        self.n_read += not last
        self.add("stat", norm, kt)

    def norm(self, norm):
        self.add("norm", norm)
        for kt in range(KD):
            self.split(("norm", norm, kt))

    def row(self, p):
        m = self.n_row
        self.n_row += 1
        self.open(("rowX", p), 2 * (m % 2))
        self.open(("rowY", p), 2 * (m % 2) + 1)
        self.add("row", p)

    def build(self):
        self.n_read = 0
        self.open(("gains",), 2)
        self.add("gains")
        for kt in range(KD):
            self.stat(1, kt)
        self.norm(1)
        self.n_row = 0
        first = {}
        for p, (kind, _, _) in enumerate(PANELS):
            first.setdefault(kind, p)
        for p in range(first["gq"]):
            self.start(p)
            for i in range(KD):
                self.add("part", p, i)
                if i == 0 and p:
                    self.row(p - 1)
            self.finish(p)
        items = [[], []]
        for t in range(NTILE + 1):
            if t < NTILE:
                items.append([("qknorm", t)])
            if t == 0:
                items.append([("z",)])
            if t == 2:
                items.append([("decay",)])
            if t:
                items.append([("qkT", t - 1)])
        self.woven(range(first["gq"], first["gv"]), items)
        rounds = [(1, r) for r in range(TOPK_PROMPT // 8)]
        rounds += [("s", r) for r in range((TOPK_SAMPLE + PAD_TOP) // 8)]
        rounds += [(j, r) for j in (2, 3) for r in range(TOPK_PROMPT // 8)]

        def topk(n):
            out = []
            for _ in range(n):
                if rounds:
                    out.append(("topk", *rounds.pop(0)))
            return out
        items = [[("gexp",)], [("qiz",)], [("index", 1)], [("index", 2)], topk(2), [("index", 3)], topk(2),
                 [("kidx", 0)], topk(2), [("kidx", 1)], topk(2), [("sindex",)], topk(2)]
        self.woven(range(first["gv"], first["gr"]), items)
        items = [[], [("intra", 0)], [("intra_out", 0)]]
        for c in range(N_CHUNK):
            items.append([("chunk", c)] + topk(TOPK_EACH))
            if c % 4 == 2:
                items.append([("intra", c // 4 + 1)] + topk(1))
            if c % 4 == 3:
                items.append([("intra_out", c // 4 + 1)])
        for r in range(4):
            items.append([("sround", r)] + topk(TOPK_EACH))
        items.append([("sgla_out",)])
        split = first["gr"] + GLA_PANELS
        self.woven(range(first["gr"], split), items)
        items = [[("gnorm", h)] + topk(TOPK_EACH) for h in range(GH)]
        while rounds:
            items.append(topk(2))
        items[-1].append(("qz",))
        items += [[("kcT", 0)], [("kcT", 1)]]
        for i in range(5):
            for b in (2 * i, 2 * i + 1):
                if i < 4:
                    items.append([("slog", b)] + ([("kcT", b + 2)] if b + 2 < DEC_BATCH else []))
                if i > 0:
                    items.append([("spT", i - 1)] if b == 2 * i else [("spv", i - 1)])
        items[-1].append(("sample_out",))
        order = [(j, h) for j in range(4) for h in range(N_HEADS)]
        self.attn_order = order
        for j, h in order:
            if h == 1 and j > 0:
                items.append([("attn_t", j - 1)])
            items.append([("attn", j, h)])
            items.append([("attn_pv", j, h)])
            if h == N_HEADS - 1:
                items[-1].append(("attn_out", j))
        self.woven(range(split, first["oab"]), items)
        self.extra_step(("attn_t", 3))
        for kt in range(KD):
            self.split(("mix", kt))
        self.add("mix")
        for p in range(first["oab"], N_PANELS):
            self.panel(p)
            kind, idx, _ = PANELS[p]
            if kind == "o" and idx > 0:
                self.stat(2, idx - 1)
            if kind == "o" and idx == KD - 1:
                self.stat(2, idx)
                self.norm(2)

    def extra_step(self, step):
        kind = step[0]
        if kind == "z":
            for i, b in ((0, 2), (1, 3), (2, 1)):
                self.open(("z", i), b)
        if kind == "decay":
            for i, b in ((0, 0), (1, 1), (2, 2)):
                self.open(("b", i), b)
        if kind == "qkT":
            for i, b in (("q", 0), ("ik", 1), ("ki", 3)):
                self.open((i, step[1]), b)
        if kind == "index":
            for h in range(IDX_HEADS):
                self.open(("index", step[1], h), 2 + h % 2)
                self.gate_tmp(("index", step[1], h), ("index_added", 4 * (step[1] - 1) + h + 1))
        if kind == "kidx":
            g = step[1]
            self.open(("kidxT", 2 * g), 3)
            self.open(("kidxT", 2 * g + 1), 3)
            self.open(("sscore", g), 2)
        if kind == "qiz":
            self.open(("wi", 0), 3)
            self.open(("wi", 1), 2)
        if kind == "sindex":
            self.open(("ssum",), 3)
        if kind == "intra":
            t = step[1]
            self.open(("kT", t), 3)
            self.open(("inE", t), 3)
            self.open(("inO", t), 2)
        if kind == "intra_out":
            self.open(("oE", step[1]), 0)
            self.open(("oO", step[1]), 1)
        if kind == "chunk":
            self.open(("kv", step[1]), 2)
        if kind == "sround":
            self.open(("skv", step[1]), 2)
        if kind == "kcT":
            self.open(("kcT", step[1]), 1 + step[1] % 2)
        if kind == "slog" and step[1] % 2 == 0:
            self.open(("slog", step[1] // 2), 0)
        if kind == "spT":
            self.open(("spT", step[1]), 2)
        if kind == "spv" and step[1] == 0:
            self.open(("so",), 3)
        if kind == "attn":
            _, j, h = step
            order = self.attn_order
            n = order.index((j, h))
            if n == 0:
                self.open(("log", j, h), 0)
            if n + 1 < len(order):
                self.open(("log",) + order[n + 1], (n + 1) % 2)
            self.open(("pT", j, h), 2)
        if kind == "attn_pv" and step[2] == 0:
            self.open(("o", step[1]), 3)
        if kind == "attn_t":
            self.open(("oT", step[1]), 2)
        if kind == "gnorm":
            self.open(("gn", step[1], 0), 0)
            self.open(("gn", step[1], 1), 1)
            self.stage(("gn", step[1]), ("bank_ready", ("gn", step[1], 1)))
            self.gate_tmp(("gn", step[1]), ("gnorm_done", step[1] + 1))
        self.add(*step)


def build(nc, A, depth=DEPTH):
    plan = Plan()
    uses = plan.uses

    ctx = ExitStack()
    with ctx:
        base = 192
        cursor = [base]

        def region(nbytes):
            at = cursor[0]
            cursor[0] += (nbytes + 31) // 32 * 32
            return at

        def at(name, shape, dt, offset):
            return nc.alloc_sbuf_tensor_at(name, shape, dt, offset=offset)

        def sb(name, shape, dt=F32):
            n = int(np.prod(shape[1:])) * (2 if dt == BF16 else 4)
            return at(name, shape, dt, region(n))

        cst = sb("cst", [P, KEPT_W])
        x_t = sb("x_t", [P, KD, NT])
        in_hi = sb("in_hi", [P, KD, NT], F32R)
        in_lo = sb("in_lo", [P, KD, NT], F32R)
        w_raw = sb("w_raw", [P, RAW_RING, KD * P])
        w_hi = sb("w_hi", [P, 2, KD * P], F32R)
        w_lo = sb("w_lo", [P, 2, KD * P], F32R)
        tmp = sb("tmp", [P, 2, NT])
        stage = sb("stage", [P, 2, NT])
        gate_tmp = sb("gate_tmp", [P, 2, NT])
        ones = sb("ones", [P, P])
        ident_b = sb("ident_b", [P, P], BF16)
        tri_b = sb("tri_b", [P, P], BF16)
        repeat_b = sb("repeat_b", [NS, DEC_BATCH, NS], BF16)
        eps_t = sb("eps_t", [P, 1])
        pages = sb("pages", [1, DEC_BATCH * N_PAGES], I32)
        gain_rows = sb("gain_rows", [2 * KD + 1, P])
        gains = sb("gains", [P, 2 * KD + 1])
        qk_g = sb("qk_g", [P, 3, HD])
        wa2 = sb("wa2", [RANK, GK_W])
        ba = sb("ba", [1, GK_W])
        ff = region(2 * KD * NT * 4)
        mid_hi = at("mid_hi", [P, KD, NT], F32R, ff)
        mid_lo = at("mid_lo", [P, KD, NT], F32R, ff + KD * NT * 4)
        gate_a = at("gate_a", [P, KD, NT], F32, ff)
        gla_r = at("gla_r", [P, GH, NT], F32, ff + KD * NT * 4)
        attn_t = at("attn_t", [P, 4, NT], F32, ff + KD * NT * 4)
        gla_o = at("gla_o", [P, GH, NT], F32, ff + (KD + GH) * NT * 4)
        x_rows = at("x_rows", [P, NTILE, D_MODEL], F32, ff)
        repeat_f = at("repeat_f", [P, CONST_W - KEPT_W], F32, ff + NTILE * D_MODEL * 4)
        q_rows = at("q_rows", [P, NTILE, 13 * HD], F32, ff)
        la = at("la", [P, NTILE, GK_W], F32, ff + 16640)
        ga_t = at("ga_t", [RANK, NT], F32, ff + 21760)
        d_t = at("d_t", [P, 2, NT], F32, ff + 24064)
        e_t = at("e_t", [P, 2, NT], F32, ff + 28672)
        sq_rows = at("sq_rows", [P, 13, HD], F32, ff + 33280)
        kidx = at("kidx", [P, DEC_BATCH, N_PAGES, ID], F32, ff)
        kidx_t = at("kidx_t", [ID, 2, 2 * PAST], F32, ff + 4096)
        qiz = at("qiz", [ID, DEC_BATCH, 32], F32, ff + 8192)
        s_heads = at("s_heads", [P, 2, NEW_KEYS], F32, ff + 9216)
        kv_rows = sb("kv_rows", [P, NTILE, 2 * KV_W])
        q_t = sb("q_t", [P, 4, NT])
        k_t = sb("k_t", [P, 2, NT])
        mask_b = sb("mask_b", [P, 3, SEQ], BF16)
        mask_s = sb("mask_s", [NS, NEW_KEYS], BF16)
        wi_rows = sb("wi_rows", [P, NTILE, IDX_HEADS])
        ar = region(0)
        off = [ar]

        def sub(name, shape, dt=F32):
            t = at(name, shape, dt, off[0])
            off[0] += (int(np.prod(shape[1:])) * (2 if dt == BF16 else 4) + 31) // 32 * 32
            return t

        gq = sub("gq", [P, 2, NT])
        gk = sub("gk", [P, 2, NT])
        gk_rows = sub("gk_rows", [P, 2, GK_W])
        gv_rows = sub("gv_rows", [P, NTILE, GV_W])
        state = sub("state", [P, 2, DV])
        state_in = sub("state_in", [P, 2, DV])
        state_add = sub("state_add", [P, 2, DV])
        s_state = sub("s_state", [P, 2, 2, 2, DV])
        s_state_in = sub("s_state_in", [P, 2, 2, DV])
        s_state_add = sub("s_state_add", [P, 2, 2, DV])
        gk_one = sub("gk_one", [NS, 2, GK_W])
        g_attn = sub("g_attn", [P, GH, P])
        qi_t = sub("qi_t", [P, 2, NT])
        ki_t = sub("ki_t", [P, NT])
        scores = sub("scores", [P, 2 * P + 3 * P + 4 * P])
        rstd = at("rstd", [P, NT], F32, off[0] - 4608)
        scores_s = sub("scores_s", [NS, SAMPLE_W])
        end1 = off[0]
        off[0] = ar
        gate_b = sub("gate_b", [P, KD, NT])
        qz = sub("qz", [P, DEC_BATCH, 2, NS])
        k_pages = sub("k_pages", [P, 4, N_PAGES, KV_W])
        v_pages = sub("v_pages", [P, 4, N_PAGES, KV_W])
        p_t = sub("p_t", [P, 2, SEQ])
        pT_t = sub("pT_t", [P, 2, 4, P])
        k_past = sub("k_past", [P, 2, 2, PAST])
        o_rows = sub("o_rows", [P, ATTN_W])
        cursor[0] = max(off[0], end1)
        small = lambda name, w, rows=P: sb(name, [rows, w])
        sums = small("sums", 16)
        top8 = small("top8", 8)
        top8s = small("top8s", 8)
        b_ref = sb("b_ref", [P, 2, 24])
        b_end = sb("b_end", [P, 2, 24])
        e_ref = sb("e_ref", [P, 2, 24])
        e_end = sb("e_end", [P, 2, 24])
        e_add = sb("e_add", [P, 2, 24])
        wi_s = sb("wi_s", [P, 2])
        wi_tmp = sb("wi_tmp", [P, 2, IDX_HEADS])
        rope1 = sb("rope1", [P, 13, ROT])
        rope2 = sb("rope2", [P, 13, ROT])
        neg_max = sb("neg_max", [P, 2, N_HEADS])
        p_sum = sb("p_sum", [P, 2, N_HEADS])
        p_inv = sb("p_inv", [P, N_HEADS])
        neg_max_s = sb("neg_max_s", [P, 4])
        p_sum_s = sb("p_sum_s", [P, 4])
        p_inv_s = sb("p_inv_s", [P, 4])
        assert cursor[0] <= nc.sbuf_usable_end, cursor[0]

        aux = nc.alloc_psum_tensor("aux", [P, 4, 512], F32)
        prod = nc.alloc_psum_tensor("prod", [P, 4, 512], F32)

        def const(name, rows=P):
            lo, hi = CONSTS[name]
            return cst[0:rows, lo:hi]

        def slot(g):
            s = g % 2
            return prod[:, 2 * s:2 * s + 2, 0:HALF]

        def halves(ap):
            return ap.rearrange("p (h n) -> p h n", h=2)

        def semaphore(name):
            return ctx.enter_context(nc.semaphore(name))

        x_loaded = semaphore("x_loaded")
        x_turned = semaphore("x_turned")
        once = semaphore("once")
        y_turned = semaphore("y_turned")
        y_ready = semaphore("y_ready")
        y_stored = semaphore("y_stored")
        x_filled = semaphore("x_filled")
        opened_layer = semaphore("opened_layer")
        passed = semaphore("passed")
        bank_ready = [semaphore(f"bank{i}_ready") for i in range(6)]
        bank_free = [semaphore(f"bank{i}_free") for i in range(6)]
        raw_ready = [semaphore(f"raw{i}_ready") for i in range(RAW_RING)]
        w_hi_done = semaphore("w_hi_done")
        w_lo_done = semaphore("w_lo_done")
        staged = semaphore("staged")
        stage_read = semaphore("stage_read")
        gated = semaphore("gated")
        index_added = semaphore("index_added")
        split_src = semaphore("split_src")
        split_hi = semaphore("split_hi")
        split_lo = semaphore("split_lo")
        x_added = semaphore("x_added")
        dve_step = semaphore("dve_step")
        rows_sq = semaphore("rows_sq")
        rows_ss = semaphore("rows_ss")
        rows_std = semaphore("rows_std")
        rows_done = semaphore("rows_done")
        ln_done = semaphore("ln_done")
        ga_done = semaphore("ga_done")
        decay_done = semaphore("decay_done")
        exps_done = semaphore("exps_done")
        gqk_done = semaphore("gqk_done")
        qiz_done = semaphore("qiz_done")
        s_in_done = semaphore("s_in_done")
        s_out_done = semaphore("s_out_done")
        gnorm_done = semaphore("gnorm_done")
        masks_done = semaphore("masks_done")
        qz_done = semaphore("qz_done")
        max_done = semaphore("max_done")
        pv_done = semaphore("pv_done")
        p_scaled = semaphore("p_scaled")
        kc_free = semaphore("kc_free")
        small_ready = semaphore("small_ready")
        kidx_ready = semaphore("kidx_ready")
        s_state_ready = [semaphore(f"s_state{i}_ready") for i in range(2)]
        k_ready = [semaphore(f"k_pages{i}_ready") for i in range(4)]
        v_ready = [semaphore(f"v_pages{i}_ready") for i in range(4)]
        stored = semaphore("stored")
        s_stored = semaphore("s_stored")
        state_stored = semaphore("state_stored")
        sample_intra = semaphore("sample_intra")
        gates_done = semaphore("gates_done")
        rstd_done = semaphore("rstd_done")
        gn_root = semaphore("gn_root")
        rows_ln = semaphore("rows_ln")
        state_in_done = semaphore("state_in_done")
        decayed = semaphore("decayed")
        k_past_used = semaphore("k_past_used")
        z_abs = semaphore("z_abs")
        z_exp = semaphore("z_exp")
        arrived = semaphore("arrived")
        layer_sems = range(bank_ready[0].num, arrived.num + 1)

        free_of, of_bank = {}, [0, 0]
        for p, (kind, idx, _) in enumerate(PANELS):
            for g in plan.groups[p]:
                if kind == "o":
                    free_of["g", g] = (x_added, idx + 1)
                elif kind in STAGED:
                    free_of["g", g] = (staged, plan.stage_use["row", p] + 1)
                elif kind == "down":
                    free_of["g", g] = (x_added, KD + idx[0] * KD + idx[1] + 1)
                else:
                    of_bank[g % 2] += 1
                    free_of["g", g] = (bank_free[4 + g % 2], of_bank[g % 2])
        for key, (bank, use) in uses.items():
            if bank < 4:
                free_of[key] = (bank_free[bank], use + 1)

        def ready(key):
            return bank_ready[uses[key][0]]

        def filled(key):
            return uses[key][1] + 1

        def free(key):
            return free_of[key][0]

        def emptied(key):
            return free_of[key][1]

        def opened(key):
            return uses[key][1]

        def pv_used(n):
            j, h = ORDER[n]
            return (pv_done, j * (N_HEADS - 1) + h + 1) if h < N_HEADS - 1 else (ready(("o", j)), filled(("o", j)))

        def counter():
            counts = {}

            def turn(sem):
                counts[sem.num] = counts.get(sem.num, 0) + 1
                return counts[sem.num]
            return turn

        def release(what, key):
            if what == "bank_ready":
                return ready(key), filled(key)
            if what == "bank_free":
                return free(key), emptied(key)
            return {"stage_read": stage_read, "index_added": index_added, "gnorm_done": gnorm_done}[what], key

        def layers(e, body):
            with e.Fori(0, depth) as layer:
                body(layer)
                if e is not nc.sync:
                    e.sem_inc(arrived, 1)
                    e.wait_ge(opened_layer, 1)
                    e.sem_inc(passed, 1)

        def of_layer(name, layer):
            return A[name][bass.ds(layer, 1)]

        HEAD_TILE = [(h // 4 * 2 + h % 2, h % 4 // 2) for h in range(N_HEADS)]
        ORDER = plan.attn_order
        last_gtb = max(plan.groups[max(p for p, x in enumerate(PANELS) if x[0] == "gtb")])
        misc_panel = next(p for p, x in enumerate(PANELS) if x[0] == "misc")
        gv_panels = [p for p, x in enumerate(PANELS) if x[0] == "gv"]
        gtb_panels = [p for p, x in enumerate(PANELS) if x[0] == "gtb"]
        gate_panel = [min(p for p, x in enumerate(PANELS) if x[0] == k) for k in ("gta", "gtb")]
        gate_group = {(x[0], x[1]): ("g", plan.groups[p][0]) for p, x in enumerate(PANELS) if x[0] in ("gta", "gtb")}
        gqk_group = {(x[0], x[1]): plan.groups[p][0] for p, x in enumerate(PANELS) if x[0] in ("gq", "gk")}
        plan_src, gated_no = {}, {}
        for key in plan.split_use:
            if key[0] in ("norm", "merge"):
                plan_src[key] = len(plan_src) + 1
        for key in plan.gate_tmp_use:
            if key[0] in ("gr", "gate"):
                gated_no[key] = len(gated_no) + 1
        score_cols = {1: (0, 2 * P), 2: (2 * P, 5 * P), 3: (5 * P, 9 * P)}
        ident = const("ident")

        block = ctx.enter_context(nc.Block())

        @block.sync
        def _(e):
            e.dma_start(cst[:], A["consts"][:, 0:KEPT_W]).then_inc(x_loaded, 16)
            e.dma_start(repeat_f[:], A["consts"][:, KEPT_W:CONST_W]).then_inc(x_loaded, 16)
            for t in range(NTILE):
                src = A["x_prompt"][0, t * P:(t + 1) * P, :] if t < 4 else A["x_sample"].rearrange("b s d -> (b s) d")
                e.dma_start(x_rows[0:tile_rows(t), t, :], src).then_inc(x_loaded, 16)
            e.dma_start(pages[:], A["page_table"].rearrange("b n -> (b n)").unsqueeze(0)).then_inc(x_loaded, 16)
            e.wait_ge(x_loaded, 16 * (3 + NTILE))

            def load_state(layer, r):
                for b2 in range(2):
                    for h2 in range(2):
                        src = of_layer("state_gla", layer)[:, 2 * r + b2, h2:GH:2].rearrange("a g k v -> k (a g) v")
                        e.dma_start(s_state[h2 * DK:(h2 + 1) * DK, r % 2, b2, :, :], src).then_inc(s_state_ready[r % 2], 16)

            def body(layer):
                def store(dst, src, sig):
                    e.dma_start(dst, src).then_inc(sig, 16)

                def load_panel(p):
                    if p >= RAW_RING:
                        e.wait_ge(w_lo_done, p - RAW_RING + 1)
                    for name, row, nk, col, w, place in PANELS[p][2]:
                        src = of_layer(name, layer)[:, row:row + nk * P, col:col + w].rearrange(
                            "a (k p) n -> p (a k) n", p=P)
                        if w == P:
                            dst = w_raw[:, p % RAW_RING, place:place + nk * P].rearrange("p (k n) -> p k n", n=P)
                        else:
                            dst = w_raw[:, p % RAW_RING, :].rearrange("p (k n) -> p k n", n=P)[:, :, place:place + w]
                        e.dma_start(dst, src).then_inc(raw_ready[p % RAW_RING], 16)

                def page(b, n):
                    i = b * N_PAGES + n
                    return e.value_load(pages[0:1, i:i + 1], min_val=0, max_val=N_POOL - 1)

                def load_pages(b, name, dst, sem):
                    for n in range(N_PAGES):
                        r = page(b, n)
                        src = A[name].rearrange("l n s h d -> (l n) s (h d)")[bass.ds(layer * N_POOL + r, 1)]
                        e.dma_start(dst[:, b % 4, n, :], src.rearrange("a s f -> (a s) f")).then_inc(sem[b % 4], 16)

                for p in range(RAW_RING):
                    load_panel(p)
                for n, name in ((0, "norm1_g"), (1, "norm2_g")):
                    e.dma_start(gain_rows[n * KD:(n + 1) * KD, :], of_layer(name, layer).rearrange("a (k p) -> (a k) p", p=P)).then_inc(small_ready, 16)
                e.dma_start(gain_rows[2 * KD:2 * KD + 1, :], of_layer("gla_onorm_g", layer)).then_inc(small_ready, 16)
                for n, name in enumerate(("q_norm_g", "k_norm_g", "kidx_norm_g")):
                    row = of_layer(name, layer)
                    e.dma_start(qk_g[:, n, :], row.partition_broadcast(P).rearrange("p a n -> p (a n)")).then_inc(small_ready, 16)
                e.dma_start(wa2[:], of_layer("gla_wa2", layer).rearrange("a r n -> (a r) n")).then_inc(small_ready, 16)
                e.dma_start(ba[:], of_layer("gla_ba", layer)).then_inc(small_ready, 16)
                for step in plan.steps:
                    kind = step[0]
                    if kind == "panel" and step[1] + RAW_RING < N_PANELS:
                        load_panel(step[1] + RAW_RING)
                    if kind == "qkT":
                        t = step[1]
                        n = tile_rows(t)
                        e.wait_ge(rows_done, t + 1)
                        for name, src in (("k", kv_rows[0:n, t, 0:KV_W]), ("v", kv_rows[0:n, t, KV_W:2 * KV_W]),
                                          ("kidx", q_rows[0:n, t, 12 * HD:13 * HD])):
                            if t < 4:
                                dst = of_layer(f"new_{name}_prompt", layer)[:, 0, t * P:(t + 1) * P]
                                dst = dst.rearrange("a s h d -> (a s) (h d)") if name != "kidx" else \
                                    dst.rearrange("a s d -> (a s) d")
                            else:
                                dst = of_layer(f"new_{name}_sample", layer)
                                dst = dst.rearrange("a b s h d -> (a b s) (h d)") if name != "kidx" else \
                                    dst.rearrange("a b s d -> (a b s) d")
                            e.dma_start(dst, src).then_inc(stored, 16)
                    if kind == "qkT" and step[1] == NTILE - 1:
                        e.wait_ge(stored, 16 * 3 * NTILE)
                        e.wait_ge(ready(("ki", 4)), filled(("ki", 4)))
                        for b in range(DEC_BATCH):
                            for n in range(N_PAGES):
                                r = page(b, n)
                                src = A["cache_kidx"].rearrange("l n s d -> (l n) s d")[
                                    bass.ds(layer * N_POOL + r, 1)].rearrange("a s d -> (a s) d")
                                e.dma_start(kidx[:, b, n, :], src).then_inc(kidx_ready, 16)
                    if kind == "intra" and step[1] == 3:
                        for r in range(2):
                            load_state(layer, r)
                    if kind == "intra" and step[1] == 4:
                        e.wait_ge(free(("kv", N_CHUNK - 1)), emptied(("kv", N_CHUNK - 1)))
                        for h2 in range(2):
                            dst = of_layer("new_gla_prompt", layer)[:, 0, h2:GH:2].rearrange("a g k v -> k (a g) v")
                            e.dma_start(dst, state[h2 * DK:(h2 + 1) * DK, :, :]).then_inc(state_stored, 16)
                    if kind == "sround":
                        r = step[1]
                        e.wait_ge(s_out_done, r + 1)
                        for b2 in range(2):
                            for h2 in range(2):
                                dst = of_layer("new_gla_sample", layer)[:, 2 * r + b2, h2:GH:2].rearrange(
                                    "a g k v -> k (a g) v")
                                e.dma_start(dst, s_state[h2 * DK:(h2 + 1) * DK, r % 2, b2, :, :]).then_inc(s_stored, 16)
                        if r < 2:
                            e.wait_ge(s_stored, 16 * 4 * (r + 1))
                            load_state(layer, r + 2)
                    if kind == "sgla_out":
                        e.wait_ge(ready(("oO", 4)), filled(("oO", 4)))
                        e.wait_ge(state_stored, 16 * 2)
                        e.wait_ge(s_stored, 16 * 2 * DEC_BATCH)
                        for b in range(4):
                            load_pages(b, "cache_k", k_pages, k_ready)
                            load_pages(b, "cache_v", v_pages, v_ready)
                    if kind == "kcT" and step[1] < 4:
                        b = step[1]
                        e.wait_ge(ready(("kcT", b)), filled(("kcT", b)))
                        load_pages(b + 4, "cache_k", k_pages, k_ready)
                    if kind == "spv" and step[1] < 2:
                        i = step[1]
                        e.wait_ge(kc_free, 2 * i + 2)
                        for b in (2 * i + 4, 2 * i + 5):
                            load_pages(b, "cache_v", v_pages, v_ready)

                e.wait_ge(stored, 16 * 3 * NTILE)
                e.wait_ge(s_stored, 16 * 2 * DEC_BATCH)
                e.wait_ge(state_stored, 16 * 2)
                e.wait_ge(arrived, 4)
                e.sem_clear(layer_sems)
                e.sem_inc(opened_layer, 1)
                e.wait_ge(passed, 4)
                e.sem_clear(range(opened_layer.num, passed.num + 1))

            layers(e, body)
            for t in range(NTILE):
                e.wait_ge(y_ready, 2 * (t + 1))
                dst = A["y_prompt"][0, t * P:(t + 1) * P, :] if t < 4 else A["y_sample"].rearrange("b s d -> (b s) d")
                e.dma_start(dst, x_rows[0:tile_rows(t), t, :]).then_inc(y_stored, 16)
            e.wait_ge(y_stored, 16 * NTILE)

        @block.tensor
        def _(e):
            e.wait_ge(x_loaded, 16 * (3 + NTILE))
            for kt in range(KD):
                if kt >= 2:
                    e.wait_ge(x_filled, kt - 1)
                for t in range(NTILE):
                    n = tile_rows(t)
                    out = aux[:, 2 * (kt % 2) + t // 4, (t % 4) * P:(t % 4) * P + n]
                    ins = e.transpose(out, x_rows[0:n, t, kt * P:(kt + 1) * P], ident[0:n, 0:n])
                ins.then_inc(x_turned, 1)
            e.wait_ge(x_filled, KD)

            def body(layer):
                def part(p, i):
                    kind, idx, parts = PANELS[p]
                    slot_w = p % 2
                    if i == 0:
                        e.wait_ge(w_lo_done, p + 1)
                    n, first_k, last_k = 0, 0, KD - 1
                    if kind == "oab":
                        n, first_k, last_k = i // 4, i // 4 * 4, i // 4 * 4 + 3
                    elif kind == "down":
                        last_k = FF_PARTS[idx[0]] - 1
                        if i > last_k:
                            return
                    g = plan.groups[p][n]
                    hi, lo = (mid_hi, mid_lo) if kind in ("o", "down") else (in_hi, in_lo)
                    for k in (i,):
                        if k == first_k and g >= 2:
                            e.wait_ge(free(("g", g - 2)), emptied(("g", g - 2)))
                        if kind == "q" and idx == 0:
                            e.wait_ge(split_lo, plan.split_use["norm", 1, k] + 1)
                        if kind == "oab" and idx == 0:
                            e.wait_ge(split_lo, plan.split_use["mix", k] + 1)
                        if kind == "o" and idx == 0:
                            e.wait_ge(split_lo, plan.split_use["merge", k] + 1)
                        if kind == "gate" and idx == (0, 0):
                            e.wait_ge(split_lo, plan.split_use["norm", 2, k] + 1)
                        if kind == "down" and idx[1] == 0:
                            e.wait_ge(split_lo, plan.split_use["ff", (idx[0], sum(FF_PARTS[:idx[0]]) + k)] + 1)
                        for w, parts_in in ((w_hi, (hi, lo)), (w_lo, (hi,))):
                            for a in parts_in:
                                for h in range(2):
                                    first = k == first_k and w is w_hi and a is hi
                                    last = k == last_k and w is w_lo
                                    ins = e.matmul(slot(g)[:, h, :], w[:, slot_w, k * P:(k + 1) * P],
                                                   a[:, k, h * HALF:(h + 1) * HALF], start=first, stop=last)
                        if k == last_k:
                            ins.then_inc(ready(("g", g)), 1)

                def logits(n):
                    j, h = ORDER[n]
                    L = (j + 1) * P
                    tile, half = HEAD_TILE[h]
                    rows = slice(64 * half, 64 * half + 64)
                    key = ("log", j, h)
                    e.wait_ge(free(key), opened(key))
                    out = aux[:, uses[key][0], 0:L]
                    mask = tri_b[:] if j == 0 else mask_b[:, j - 1, 0:L]
                    if n == 0:
                        e.wait_ge(masks_done, 4)
                    e.matmul(out, ident_b[:], mask, start=True, stop=False)
                    ins = e.matmul(out, q_t[rows, tile, j * P:(j + 1) * P], k_t[rows, h // 4, 0:L],
                                   start=False, stop=True)
                    ins.then_inc(ready(key), 1)

                for step in plan.steps:
                    kind = step[0]
                    if kind == "part":
                        part(step[1], step[2])
                    elif kind == "gains":
                        e.wait_ge(small_ready, 16 * SMALL_LOADS)
                        e.wait_ge(free(("gains",)), opened(("gains",)))
                        ins = e.transpose(aux[:, 2, 0:2 * KD + 1], gain_rows[:], ident[0:2 * KD + 1, 0:2 * KD + 1])
                        ins.then_inc(ready(("gains",)), 1)
                    elif kind == "stat":
                        _, norm, kt = step
                        use = plan.stage_use["stat", norm, kt]
                        e.wait_ge(staged, use + 1)
                        if kt == 0:
                            for h in range(2):
                                e.wait_ge(free(("stat", norm, h)), opened(("stat", norm, h)))
                        for h in range(2):
                            ins = e.matmul(aux[:, h, 0:HALF], ones[:], stage[:, use % 2, h * HALF:(h + 1) * HALF],
                                           start=(kt == 0), stop=(kt == KD - 1))
                            if kt == KD - 1:
                                ins.then_inc(ready(("stat", norm, h)), 1)
                        if kt < KD - 1:
                            ins.then_inc(stage_read, 1)
                    elif kind == "row":
                        p = step[1]
                        use = plan.stage_use["row", p]
                        e.wait_ge(staged, use + 1)
                        e.wait_ge(free(("rowX", p)), opened(("rowX", p)))
                        bx, by = uses["rowX", p][0], uses["rowY", p][0]
                        for t in range(4):
                            ins = e.transpose(aux[:, bx, t * P:(t + 1) * P], stage[:, use % 2, t * P:(t + 1) * P], ident)
                        ins.then_inc(ready(("rowX", p)), 1)
                        e.wait_ge(free(("rowY", p)), opened(("rowY", p)))
                        ins = e.transpose(aux[0:NS, by, 0:P], stage[:, use % 2, SEQ:NT], ident)
                        ins.then_inc(ready(("rowY", p)), 1)
                    elif kind == "z":
                        e.wait_ge(small_ready, 16 * SMALL_LOADS)
                        e.wait_ge(ga_done, 1)
                        for i in range(3):
                            e.wait_ge(free(("z", i)), opened(("z", i)))
                            for t in range(2 * i, min(2 * i + 2, NTILE)):
                                n = tile_rows(t)
                                out = aux[0:n, uses["z", i][0], (t % 2) * GK_W:(t % 2 + 1) * GK_W]
                                e.matmul(out, ga_t[:, token_slice(t)], wa2[:], start=True, stop=False)
                                ins = e.matmul(out, ones[0:1, 0:n], ba[:], start=False, stop=True)
                            ins.then_inc(ready(("z", i)), 1)
                    elif kind == "decay":
                        for i in range(3):
                            e.wait_ge(free(("z", i)), emptied(("z", i)))
                        for hp in range(2):
                            e.wait_ge(free(("b", hp)), opened(("b", hp)))
                            for t in range(4):
                                ins = e.matmul(aux[:, hp, t * P:(t + 1) * P], la[:, t, hp * P:(hp + 1) * P],
                                               const("chunk_sum"), start=True, stop=True)
                            ins.then_inc(ready(("b", hp)), 1)
                        e.wait_ge(free(("b", 2)), opened(("b", 2)))
                        for hp in range(2):
                            ins = e.matmul(aux[:, 2, hp * NS:(hp + 1) * NS], la[0:NS, 4, hp * P:(hp + 1) * P],
                                           const("sample_sum", NS), start=True, stop=True)
                        ins.then_inc(ready(("b", 2)), 1)
                    elif kind == "qkT":
                        t = step[1]
                        n = tile_rows(t)
                        idn = ident[0:n, 0:n]
                        e.wait_ge(rows_done, t + 1)
                        e.wait_ge(free(("q", t)), opened(("q", t)))
                        for m in range(4):
                            ins = e.transpose(aux[:, 0, m * P:m * P + n], q_rows[0:n, t, m * P:(m + 1) * P], idn)
                        ins.then_inc(ready(("q", t)), 1)
                        e.wait_ge(free(("ik", t)), opened(("ik", t)))
                        for m in range(2):
                            e.transpose(aux[:, 1, m * P:m * P + n], q_rows[0:n, t, (4 + m) * P:(5 + m) * P], idn)
                        for m in range(2):
                            ins = e.transpose(aux[:, 1, (2 + m) * P:(2 + m) * P + n],
                                              kv_rows[0:n, t, m * P:(m + 1) * P], idn)
                        ins.then_inc(ready(("ik", t)), 1)
                        e.wait_ge(free(("ki", t)), opened(("ki", t)))
                        e.transpose(aux[0:ID, 3, 0:n], q_rows[0:n, t, 12 * HD:13 * HD], idn)
                        ins = e.matmul(aux[ID:2 * ID, 3, 0:n], q_rows[0:n, t, 12 * HD:13 * HD], idn,
                                       start=True, stop=True)
                        ins.then_inc(ready(("ki", t)), 1)
                    elif kind == "index":
                        j = step[1]
                        L = (j + 1) * P
                        e.wait_ge(free(("ik", 4)), emptied(("ik", 4)))
                        e.wait_ge(free(("ki", 4)), emptied(("ki", 4)))
                        for h in range(IDX_HEADS):
                            rows = slice(64 * (h % 2), 64 * (h % 2) + 64)
                            key = ("index", j, h)
                            e.wait_ge(free(key), opened(key))
                            ins = e.matmul(aux[:, uses[key][0], 0:L], qi_t[rows, h // 2, j * P:(j + 1) * P],
                                           ki_t[rows, 0:L], start=True, stop=True)
                            ins.then_inc(ready(key), 1)
                    elif kind == "qiz":
                        for g in range(2):
                            e.wait_ge(free(("wi", g)), opened(("wi", g)))
                            bank = uses["wi", g][0]
                            ins = e.matmul(aux[:, bank, 0:IDX_HEADS],
                                           const("spread", NS)[:, g * P:(g + 1) * P], wi_rows[0:NS, 4, :],
                                           start=True, stop=True)
                            ins.then_inc(ready(("wi", g)), 1)
                    elif kind == "kidx":
                        g = step[1]
                        e.wait_ge(kidx_ready, 16 * DEC_BATCH * N_PAGES)
                        e.wait_ge(qiz_done, 1)
                        for u in range(2):
                            key = ("kidxT", 2 * g + u)
                            e.wait_ge(free(key), opened(key))
                            for k in range(4):
                                b = 4 * g + 2 * u + k // 2
                                ins = e.transpose(aux[0:ID, 3, k * P:(k + 1) * P], kidx[:, b, k % 2, :], ident)
                            ins.then_inc(ready(key), 1)
                        for u in range(2):
                            e.wait_ge(free(("kidxT", 2 * g + u)), emptied(("kidxT", 2 * g + u)))
                            if u == 0:
                                e.wait_ge(free(("sscore", g)), opened(("sscore", g)))
                            for k in range(2):
                                b = 4 * g + 2 * u + k
                                out = aux[32 * (b % 4):32 * (b % 4) + 32, 2, :]
                                e.matmul(out[:, 0:PAST], qiz[:, b, :], kidx_t[:, u, k * PAST:(k + 1) * PAST],
                                         start=True, stop=True)
                                ins = e.matmul(out[:, PAST:NEW_KEYS], qiz[:, b, :], ki_t[0:ID, SEQ:NT],
                                               start=True, stop=True)
                        ins.then_inc(ready(("sscore", g)), 1)
                    elif kind == "sindex":
                        e.wait_ge(free(("ssum",)), opened(("ssum",)))
                        for g in range(2):
                            e.wait_ge(free(("sscore", g)), emptied(("sscore", g)))
                            ins = e.matmul(aux[0:NS, 3, 0:NEW_KEYS], const("gather")[:, g * NS:(g + 1) * NS],
                                           s_heads[:, g, :], start=(g == 0), stop=(g == 1))
                        ins.then_inc(ready(("ssum",)), 1)
                    elif kind == "intra":
                        t = step[1]
                        n = tile_rows(t)
                        tok = token_slice(t)
                        e.wait_ge(gqk_done, 1)
                        e.wait_ge(free(("rowY", gv_panels[-1])), emptied(("rowY", gv_panels[-1])))
                        e.wait_ge(free(("kT", t)), opened(("kT", t)))
                        for hp in range(2):
                            ins = e.transpose(aux[0:n, 3, hp * P:(hp + 1) * P], gk[:, hp, tok], ident)
                        ins.then_inc(ready(("kT", t)), 1)
                        for par, key in enumerate((("inE", t), ("inO", t))):
                            e.wait_ge(free(key), opened(key))
                            rows = slice(64 * par, 64 * par + 64)
                            for hp in range(2):
                                ins = e.matmul(aux[0:n, uses[key][0], hp * P:hp * P + n], gk[rows, hp, tok],
                                               gq[rows, hp, tok], start=True, stop=True)
                            ins.then_inc(ready(key), 1)
                    elif kind == "intra_out":
                        t = step[1]
                        n = tile_rows(t)
                        for par, key in enumerate((("oE", t), ("oO", t))):
                            e.wait_ge(free(key), opened(key))
                            e.wait_ge(free((("inE", t), ("inO", t))[par]), emptied((("inE", t), ("inO", t))[par]))
                            for hp in range(2):
                                h = 2 * hp + par
                                ins = e.matmul(aux[:, par, hp * P:hp * P + n], gv_rows[0:n, t, h * DV:(h + 1) * DV],
                                               g_attn[0:n, h, 0:n], start=(hp == 0), stop=False,
                                               skip_group_check=True)
                        if t == 4:
                            ins.then_inc(sample_intra, 1)
                    elif kind == "chunk":
                        c = step[1]
                        t = c // 4
                        if c > 0:
                            e.wait_ge(state_in_done, c)
                            for par in range(2):
                                rows = slice(64 * par, 64 * par + 64)
                                for hp in range(2):
                                    ins = e.matmul(aux[:, par, hp * P + c % 4 * CHUNK:hp * P + (c % 4 + 1) * CHUNK],
                                                   state_in[rows, hp, :], gq[rows, hp, c * CHUNK:(c + 1) * CHUNK],
                                                   start=False, stop=(c % 4 == 3), skip_group_check=True)
                                if c % 4 == 3:
                                    ins.then_inc(ready((("oE", t), ("oO", t))[par]), 1)
                        e.wait_ge(free(("kT", t)), emptied(("kT", t)))
                        e.wait_ge(free(("kv", c)), opened(("kv", c)))
                        rows = slice(c % 4 * CHUNK, (c % 4 + 1) * CHUNK)
                        for h in range(GH):
                            ins = e.matmul(aux[64 * (h % 2):64 * (h % 2) + 64, 2, h // 2 * DV:(h // 2 + 1) * DV],
                                           gk_rows[rows, t % 2, h * DK:(h + 1) * DK],
                                           gv_rows[rows, t, h * DV:(h + 1) * DV], start=True, stop=True,
                                           tile_position=(c % 4 * CHUNK, 64 * (h % 2)))
                        ins.then_inc(ready(("kv", c)), 1)
                    elif kind == "sround":
                        r = step[1]
                        e.wait_ge(s_in_done, r + 1)
                        if r == 0:
                            e.wait_ge(sample_intra, 1)
                        for par in range(2):
                            rows = slice(64 * par, 64 * par + 64)
                            for b2 in range(2):
                                for hp in range(2):
                                    b = 2 * r + b2
                                    cols = slice(hp * P + b * DEC_SEQ, hp * P + (b + 1) * DEC_SEQ)
                                    ins = e.matmul(aux[:, par, cols], s_state_in[rows, b2, hp, :],
                                                   gq[rows, hp, SEQ + b * DEC_SEQ:SEQ + (b + 1) * DEC_SEQ],
                                                   start=False, stop=(r == 3), skip_group_check=True)
                            if r == 3:
                                ins.then_inc(ready((("oE", 4), ("oO", 4))[par]), 1)
                        e.wait_ge(free(("skv", r)), opened(("skv", r)))
                        for b2 in range(2):
                            for h in range(GH):
                                c0 = (b2 * 2 + h // 2) * DV
                                ins = e.matmul(aux[64 * (h % 2):64 * (h % 2) + 64, 2, c0:c0 + DV],
                                               gk_one[:, b2, h * DK:(h + 1) * DK], gv_rows[0:NS, 4, h * DV:(h + 1) * DV],
                                               start=True, stop=True)
                        ins.then_inc(ready(("skv", r)), 1)
                    elif kind == "gnorm":
                        h = step[1]
                        use = plan.stage_use["gn", h]
                        e.wait_ge(staged, use + 1)
                        for k in range(2):
                            e.wait_ge(free(("gn", h, k)), opened(("gn", h, k)))
                            ins = e.matmul(aux[:, k, 0:HALF], ones[:], stage[:, use % 2, k * HALF:(k + 1) * HALF],
                                           start=True, stop=True)
                            ins.then_inc(ready(("gn", h, k)), 1)
                    elif kind == "kcT":
                        b = step[1]
                        e.wait_ge(k_ready[b % 4], 16 * N_PAGES * (b // 4 + 1))
                        e.wait_ge(free(("kcT", b)), opened(("kcT", b)))
                        for pair in range(2):
                            for n in range(N_PAGES):
                                c0 = pair * PAST + n * PAGE
                                ins = e.transpose(aux[:, 1 + b % 2, c0:c0 + PAGE],
                                                  k_pages[:, b % 4, n, pair * P:(pair + 1) * P], ident)
                        ins.then_inc(ready(("kcT", b)), 1)
                    elif kind == "slog":
                        b = step[1]
                        i = b // 2
                        if b == 0:
                            e.wait_ge(masks_done, 4)
                            e.wait_ge(qz_done, 1)
                        if b % 2 == 0:
                            e.wait_ge(free(("slog", i)), opened(("slog", i)))
                        out = aux[64 * (b % 2):64 * (b % 2) + 64, uses["slog", i][0], :]
                        e.matmul(out[:, 0:NEW_KEYS], repeat_b[:, b, :], mask_s[:], start=True, stop=False,
                                 skip_group_check=True)
                        e.wait_ge(free(("kcT", b)), emptied(("kcT", b)))
                        for pair in range(2):
                            e.matmul(out[:, 0:PAST], qz[:, b, pair, :], k_past[:, b % 2, pair, :],
                                     start=False, stop=False, skip_group_check=True)
                            ins = e.matmul(out[:, PAST:NEW_KEYS], qz[:, b, pair, :], k_t[:, pair, SEQ:NT],
                                           start=False, stop=(pair == 1), skip_group_check=True)
                        if b % 2 == 1:
                            ins.then_inc(ready(("slog", i)), 1)
                        else:
                            ins.then_inc(k_past_used, 1)
                    elif kind == "spT":
                        i = step[1]
                        e.wait_ge(p_scaled, i + 1)
                        e.wait_ge(free(("spT", i)), opened(("spT", i)))
                        for s in range(2):
                            e.transpose(aux[:, 2, s * P:(s + 1) * P], p_t[:, i % 2, s * P:(s + 1) * P], ident)
                        ins = e.transpose(aux[0:NS, 2, 2 * P:3 * P], p_t[:, i % 2, PAST:NEW_KEYS], ident)
                        ins.then_inc(ready(("spT", i)), 1)
                    elif kind == "spv":
                        i = step[1]
                        if i == 0:
                            e.wait_ge(free(("so",)), opened(("so",)))
                        e.wait_ge(free(("spT", i)), emptied(("spT", i)))
                        for b in (2 * i, 2 * i + 1):
                            e.wait_ge(v_ready[b % 4], 16 * N_PAGES * (b // 4 + 1))
                            for pair in range(2):
                                out = aux[:, 3, (b * 2 + pair) * 32:(b * 2 + pair + 1) * 32]
                                cols = slice(64 * (b % 2) + 32 * pair, 64 * (b % 2) + 32 * pair + 32)
                                for s in range(2):
                                    e.matmul(out, v_pages[:, b % 4, s, pair * P:(pair + 1) * P],
                                             pT_t[:, i % 2, s, cols], start=(s == 0), stop=False)
                                ins = e.matmul(out, kv_rows[0:NS, 4, KV_W + pair * P:KV_W + (pair + 1) * P],
                                               pT_t[0:NS, i % 2, 2, cols], start=False, stop=True)
                            if b == DEC_BATCH - 1:
                                ins.then_inc(ready(("so",)), 1)
                            else:
                                ins.then_inc(kc_free, 1)
                    elif kind == "attn":
                        _, j, h = step
                        n = j * N_HEADS + h
                        if n == 0:
                            logits(0)
                        if n + 1 < len(ORDER):
                            logits(n + 1)
                        e.wait_ge(free(("log", j, h)), emptied(("log", j, h)))
                        e.wait_ge(free(("pT", j, h)), opened(("pT", j, h)))
                        for s in range(j + 1):
                            ins = e.transpose(aux[:, 2, s * P:(s + 1) * P], p_t[:, n % 2, s * P:(s + 1) * P], ident)
                        ins.then_inc(ready(("pT", j, h)), 1)
                    elif kind == "attn_pv":
                        _, j, h = step
                        n = j * N_HEADS + h
                        if h == 0:
                            e.wait_ge(free(("o", j)), opened(("o", j)))
                        e.wait_ge(free(("pT", j, h)), emptied(("pT", j, h)))
                        kv = h // 2
                        for s in range(j + 1):
                            ins = e.matmul(aux[:, 3, h * HD:(h + 1) * HD], pT_t[:, n % 2, s, :],
                                           kv_rows[:, s, KV_W + kv * HD:KV_W + (kv + 1) * HD],
                                           start=(s == 0), stop=(s == j))
                        if h < N_HEADS - 1:
                            ins.then_inc(pv_done, 1)
                        else:
                            ins.then_inc(ready(("o", j)), 1)
                    elif kind == "attn_t":
                        j = step[1]
                        e.wait_ge(free(("o", j)), emptied(("o", j)))
                        e.wait_ge(free(("oT", j)), opened(("oT", j)))
                        for m in range(4):
                            ins = e.transpose(aux[:, 2, m * P:(m + 1) * P], o_rows[:, m * P:(m + 1) * P], ident)
                        ins.then_inc(ready(("oT", j)), 1)

            layers(e, body)
            for t in range(NTILE):
                if t >= 2:
                    e.wait_ge(y_ready, 2 * (t - 1))
                n = tile_rows(t)
                for kt in range(KD):
                    ins = e.transpose(aux[0:n, 2 * (t % 2) + kt // 4, kt % 4 * P:(kt % 4 + 1) * P],
                                      x_t[:, kt, token_slice(t)], ident)
                ins.then_inc(y_turned, 1)

        @block.gpsimd
        def _(e):
            def body(layer):
                for p in range(N_PANELS):
                    n = FF_PARTS[PANELS[p][1][0]] * P if PANELS[p][0] == "down" else KD * P
                    e.wait_ge(w_hi_done, p + 1)
                    if p >= 2:
                        g = ("g", plan.groups[p - 2][-1])
                        e.wait_ge(ready(g), filled(g))
                    e.tensor_tensor(w_lo[:, p % 2, 0:n], w_raw[:, p % RAW_RING, 0:n],
                                    w_hi[:, p % 2, 0:n].bitcast(F32), ALU.subtract).then_inc(w_lo_done, 1)
                e.wait_ge(w_lo_done, N_PANELS)

            layers(e, body)

        @block.scalar
        def _(e):
            e.wait_ge(x_filled, KD)

            def body(layer):
                def copy_w(p):
                    e.wait_ge(raw_ready[p % RAW_RING], 16 * RAW_READY[p])
                    if p >= 2:
                        e.wait_ge(ready(("g", plan.groups[p - 2][-1])), filled(("g", plan.groups[p - 2][-1])))
                    n = sum(part[2] for part in PANELS[p][2]) * P if PANELS[p][0] != "misc" else KD * P
                    e.activation(w_hi[:, p % 2, 0:n], w_raw[:, p % RAW_RING, 0:n], ACT.Copy).then_inc(w_hi_done, 1)

                def exp_head(n):
                    j, h = ORDER[n]
                    L = (j + 1) * P
                    key = ("log", j, h)
                    e.wait_ge(max_done, 4 + n + 1)
                    if n >= 2:
                        e.wait_ge(ready(("pT",) + ORDER[n - 2]), filled(("pT",) + ORDER[n - 2]))
                    e.activation(p_t[:, n % 2, 0:L], aux[:, uses[key][0], 0:L], ACT.Exp, bias=neg_max[:, j % 2, h:h + 1], accum_out=p_sum[:, j % 2, h:h + 1]).then_inc(free(key), 1)

                def stage_slot(key):
                    use = plan.stage_use[key]
                    if use >= 2:
                        e.wait_ge(*release(*plan.stage_release[use - 2]))
                    return stage[:, use % 2, :]

                def gate_slot(key):
                    use = plan.gate_tmp_use[key]
                    if use >= 2:
                        e.wait_ge(*release(*plan.gate_tmp_release[use - 2]))
                    return gate_tmp[:, use % 2, :]

                copy_w(0)
                for step in plan.steps:
                    kind = step[0]
                    if kind == "panel":
                        if step[1] + 1 < N_PANELS:
                            copy_w(step[1] + 1)
                        kind_p, idx, _ = PANELS[step[1]]
                        if kind_p == "oab":
                            for gate, gates in ((gate_a, "gta"), (gate_b, "gtb")):
                                e.wait_ge(free(gate_group[gates, idx]), emptied(gate_group[gates, idx]))
                                e.activation(gate[:, idx, :], gate[:, idx, :], ACT.Sigmoid).then_inc(gates_done, 1)
                    elif kind == "post":
                        p = step[1]
                        kind_p, idx, _ = PANELS[p]
                        g = plan.groups[p][0]
                        key = ("g", g)
                        src = slot(g)
                        if kind_p in STAGED:
                            dst = stage_slot(("row", p))
                            e.wait_ge(ready(key), filled(key))
                            if kind_p == "misc":
                                e.activation(halves(ga_t[:]), src[0:RANK], ACT.Copy).then_inc(ga_done, 1)
                            e.activation(halves(dst), src, ACT.Copy).then_inc(staged, 1)
                        elif kind_p == "gq":
                            e.wait_ge(ready(key), filled(key))
                            e.activation(halves(gq[:, idx, :]), src, ACT.Copy, scale=DK ** -0.5).then_inc(free(key), 1)
                        elif kind_p == "gk":
                            e.wait_ge(ready(key), filled(key))
                            e.activation(halves(gk[:, idx, :]), src, ACT.Copy).then_inc(free(key), 1)
                        elif kind_p == "gr":
                            dst = gate_slot(("gr", idx))
                            e.wait_ge(ready(key), filled(key))
                            e.activation(halves(dst), src, ACT.Sigmoid).then_inc(gated, 1)
                        elif kind_p in ("gta", "gtb"):
                            e.wait_ge(ready(key), filled(key))
                            gate = gate_a if kind_p == "gta" else gate_b
                            e.activation(halves(gate[:, idx, :]), src, ACT.Copy).then_inc(free(key), 1)
                        elif kind_p == "oab":
                            e.wait_ge(split_src, plan_src["merge", idx])
                            e.activation(mid_hi[:, idx, :], tmp[:, plan.split_use["merge", idx] % 2, :], ACT.Copy).then_inc(split_hi, 1)
                        elif kind_p == "gate":
                            dst = gate_slot(("gate", idx))
                            e.wait_ge(ready(key), filled(key))
                            e.activation(halves(dst), src, ACT.Sigmoid).then_inc(gated, 1)
                        elif kind_p == "up":
                            e.wait_ge(free(key), emptied(key))
                            part, i = idx
                            u = plan.split_use["ff", idx]
                            e.activation(mid_hi[:, i - sum(FF_PARTS[:part]), :], tmp[:, u % 2, :], ACT.Copy).then_inc(split_hi, 1)
                    elif kind == "stat":
                        _, norm, kt = step
                        dst = stage_slot(("stat", norm, kt))
                        if norm == 2:
                            e.wait_ge(x_added, kt + 1)
                        e.activation(dst, x_t[:, kt, :], ACT.Square).then_inc(staged, 1)
                    elif kind == "norm":
                        norm = step[1]
                        for h in range(2):
                            key = ("stat", norm, h)
                            e.wait_ge(ready(key), filled(key))
                            e.activation(rstd[:, h * HALF:(h + 1) * HALF], aux[:, h, 0:HALF], ACT.Ln, bias=eps_t[:],
                                         scale=1.0 / D_MODEL).then_inc(free(key), 1)
                        e.wait_ge(free(("stat", norm, 1)), emptied(("stat", norm, 1)))
                        e.activation(rstd[:], rstd[:], ACT.Exp, scale=-0.5).then_inc(rstd_done, 1)
                        for kt in range(KD):
                            e.wait_ge(split_src, plan_src["norm", norm, kt])
                            e.activation(in_hi[:, kt, :], tmp[:, plan.split_use["norm", norm, kt] % 2, :], ACT.Copy).then_inc(split_hi, 1)
                    elif kind == "qknorm":
                        t = step[1]
                        n = tile_rows(t)
                        e.wait_ge(free(("rowX", misc_panel)), emptied(("rowX", misc_panel)))
                        e.wait_ge(free(("rowY", misc_panel)), emptied(("rowY", misc_panel)))
                        if t > 0:
                            e.wait_ge(rows_ss, t)
                        q3 = q_rows[0:n, t, :].rearrange("p (h d) -> p h d", d=HD)
                        e.activation(sq_rows[0:n, 0:8, :], q3[:, 0:8, :], ACT.Square)
                        e.activation(sq_rows[0:n, 8:12, :], kv_rows[0:n, t, 0:KV_W].rearrange("p (h d) -> p h d", d=HD), ACT.Square)
                        e.activation(sq_rows[0:n, 12, :], q3[:, 12, :], ACT.Square).then_inc(rows_sq, 1)
                        e.wait_ge(rows_ss, t + 1)
                        e.activation(sums[0:n, 0:13], sums[0:n, 0:13], ACT.Ln, bias=eps_t[0:n, :], scale=1.0 / HD).then_inc(rows_ln, 1)
                        e.wait_ge(rows_ln, t + 1)
                        e.activation(sums[0:n, 0:13], sums[0:n, 0:13], ACT.Exp, scale=-0.5).then_inc(rows_std, 1)
                    elif kind == "qkT":
                        t = step[1]
                        n = tile_rows(t)
                        e.wait_ge(ready(("q", t)), filled(("q", t)))
                        e.activation(q_t[:, :, token_slice(t)], aux[:, 0, :].rearrange("p (m n) -> p m n", m=4)[:, :, 0:n], ACT.Copy, scale=HD ** -0.5).then_inc(free(("q", t)), 1)
                        e.wait_ge(ready(("ki", t)), filled(("ki", t)))
                        e.activation(ki_t[:, token_slice(t)], aux[:, 3, 0:n], ACT.Copy).then_inc(free(("ki", t)), 1)
                    elif kind == "z":
                        def la_rows(i):
                            n = tile_rows(2 * i)
                            tiles = min(2, NTILE - 2 * i)
                            return la[0:n, 2 * i:2 * i + tiles, :].rearrange("p t n -> p (t n)"), n, tiles
                        for i in range(3):
                            dst, n, tiles = la_rows(i)
                            e.wait_ge(ready(("z", i)), filled(("z", i)))
                            e.activation(dst, aux[0:n, uses["z", i][0], 0:tiles * GK_W], ACT.Abs).then_inc(z_abs, 1)
                        e.wait_ge(z_abs, 3)
                        for i in range(3):
                            dst = la_rows(i)[0]
                            e.activation(dst, dst, ACT.Exp, scale=-1.0).then_inc(z_exp, 1)
                        e.wait_ge(z_exp, 3)
                        for i in range(3):
                            dst = la_rows(i)[0]
                            e.activation(dst, dst, ACT.Ln, bias=1.0).then_inc(ln_done, 1)
                    elif kind == "decay":
                        e.wait_ge(decay_done, 1)
                        e.activation(e_t[:], d_t[:], ACT.Exp)
                        e.activation(d_t[:], d_t[:], ACT.Exp, scale=-1.0)
                        e.activation(e_ref[:], b_ref[:], ACT.Exp)
                        e.activation(e_end[:], b_end[:], ACT.Exp)
                        e.activation(e_add[:], e_add[:], ACT.Exp).then_inc(exps_done, 1)
                    elif kind == "index":
                        j = step[1]
                        L = (j + 1) * P
                        for h in range(IDX_HEADS):
                            key = ("index", j, h)
                            dst = gate_slot(key)
                            e.wait_ge(ready(key), filled(key))
                            e.activation(dst[:, 0:L], aux[:, uses[key][0], 0:L], ACT.Relu, scale=IDX_SCALE).then_inc(free(key), 1)
                    elif kind == "kidx":
                        g = step[1]
                        if g:
                            e.wait_ge(ready(("sscore", g - 1)), filled(("sscore", g - 1)))
                        for u in range(2):
                            key = ("kidxT", 2 * g + u)
                            e.wait_ge(ready(key), filled(key))
                            e.activation(kidx_t[:, u, :], aux[0:ID, 3, :], ACT.Copy).then_inc(free(key), 1)
                    if kind == "chunk" and step[1] < N_CHUNK - 1:
                        c = step[1]
                        e.wait_ge(free(("kv", c)), emptied(("kv", c)))
                        for hp in range(2):
                            ins = e.activation(state_in[:, hp, :], state[:, hp, :], ACT.Copy,
                                               scale=e_ref[:, hp, c + 1:c + 2])
                        ins.then_inc(state_in_done, 1)
                        for hp in range(2):
                            ins = e.activation(state_add[:, hp, :], state[:, hp, :], ACT.Copy,
                                               scale=e_end[:, hp, c + 1:c + 2])
                        ins.then_inc(decayed, 1)
                    if (kind == "chunk" and step[1] % 4 == 3) or kind == "sgla_out":
                        t = step[1] // 4 if kind == "chunk" else 4
                        n = tile_rows(t)
                        for par, key in enumerate((("oE", t), ("oO", t))):
                            e.wait_ge(ready(key), filled(key))
                            e.activation(gla_o[:, par::2, token_slice(t)], aux[:, par, 0:2 * P].rearrange("p (g n) -> p g n", g=2)[:, :, 0:n], ACT.Copy).then_inc(free(key), 1)
                    elif kind == "gnorm":
                        h = step[1]
                        dst = stage_slot(("gn", h))
                        for par in range(2):
                            e.wait_ge(free((("oE", 4), ("oO", 4))[par]), emptied((("oE", 4), ("oO", 4))[par]))
                        e.activation(dst, gla_o[:, h, :], ACT.Square).then_inc(staged, 1)
                        root = gate_slot(("gn", h))
                        for k in range(2):
                            key = ("gn", h, k)
                            e.wait_ge(ready(key), filled(key))
                            e.activation(root[:, k * HALF:(k + 1) * HALF], aux[:, k, 0:HALF], ACT.Ln, bias=eps_t[:],
                                         scale=1.0 / DV).then_inc(free(key), 1)
                        e.wait_ge(free(("gn", h, 1)), emptied(("gn", h, 1)))
                        e.activation(root, root, ACT.Exp, scale=-0.5).then_inc(gn_root, 1)
                    elif kind == "mix":
                        e.wait_ge(ready(("g", last_gtb)), filled(("g", last_gtb)))
                        e.wait_ge(free(("so",)), emptied(("so",)))
                        e.wait_ge(free(("oT", 3)), emptied(("oT", 3)))
                        for kt in range(KD):
                            if kt >= 4:
                                e.wait_ge(gnorm_done, kt - 3)
                            src = attn_t[:, kt, :] if kt < 4 else gla_o[:, kt - 4, :]
                            e.activation(in_hi[:, kt, :], src, ACT.Copy).then_inc(split_hi, 1)
                    elif kind == "kcT":
                        b = step[1]
                        if b == 0:
                            e.wait_ge(masks_done, 4)
                        if b >= 2:
                            if b % 2 == 0:
                                e.wait_ge(k_past_used, b // 2)
                            else:
                                e.wait_ge(ready(("slog", b // 2 - 1)), filled(("slog", b // 2 - 1)))
                        e.wait_ge(ready(("kcT", b)), filled(("kcT", b)))
                        e.activation(k_past[:, b % 2, :, :].rearrange("p a n -> p (a n)"), aux[:, 1 + b % 2, :], ACT.Copy).then_inc(free(("kcT", b)), 1)
                    elif kind == "slog" and step[1] % 2 == 1:
                        i = step[1] // 2
                        e.wait_ge(max_done, i + 1)
                        if i >= 2:
                            e.wait_ge(ready(("spT", i - 2)), filled(("spT", i - 2)))
                        e.activation(p_t[:, i % 2, 0:NEW_KEYS], aux[:, uses["slog", i][0], 0:NEW_KEYS], ACT.Exp,
                                     bias=neg_max_s[:, i:i + 1], accum_out=p_sum_s[:, i:i + 1]).then_inc(free(("slog", i)), 1)
                    elif kind == "sample_out":
                        e.wait_ge(ready(("so",)), filled(("so",)))
                        e.wait_ge(gnorm_done, GH)
                        for jj in range(4):
                            src = slice(64 * (jj // 2), 64 * (jj // 2) + 64)
                            dst = slice(64 * (jj % 2), 64 * (jj % 2) + 64)
                            for pair in range(2):
                                ins = e.activation(
                                    attn_t[dst, jj // 2 + 2 * pair, SEQ:NT].rearrange("p (b t) -> p b t", t=DEC_SEQ),
                                    aux[src, 3, :].rearrange("p (b a q t) -> p b a q t", b=8, a=2, q=4)[:, :, pair, jj, :],
                                    ACT.Copy)
                        ins.then_inc(free(("so",)), 1)
                    elif kind == "attn":
                        _, j, h = step
                        n = j * N_HEADS + h
                        L = (j + 1) * P
                        if n == 0:
                            e.wait_ge(ready(("spT", 3)), filled(("spT", 3)))
                            exp_head(0)
                        e.wait_ge(ready(("pT", j, h)), filled(("pT", j, h)))
                        if n >= 2:
                            e.wait_ge(*pv_used(n - 2))
                        e.activation(pT_t[:, n % 2, 0:j + 1, :].rearrange("p s n -> p (s n)"), aux[:, 2, 0:L], ACT.Copy).then_inc(free(("pT", j, h)), 1)
                        if n + 1 < len(ORDER):
                            exp_head(n + 1)
                    elif kind == "attn_t":
                        j = step[1]
                        e.wait_ge(ready(("oT", j)), filled(("oT", j)))
                        e.activation(attn_t[:, :, j * P:(j + 1) * P], aux[:, 2, :].rearrange("p (m n) -> p m n", m=4),
                                     ACT.Copy).then_inc(free(("oT", j)), 1)

            layers(e, body)

        @block.vector
        def _(e):
            e.memset(ones[:], 1.0).then_inc(once, 1)
            e.memset(eps_t[:], EPS).then_inc(once, 1)
            e.wait_ge(x_loaded, 16 * (3 + NTILE))
            e.tensor_copy(ident_b[:], ident).then_inc(once, 1)
            e.tensor_copy(tri_b[:], const("tri")).then_inc(once, 1)
            e.tensor_copy(repeat_b[:].rearrange("p b n -> p (b n)"), repeat_f[0:NS, :]).then_inc(once, 1)
            for kt in range(KD):
                e.wait_ge(x_turned, kt + 1)
                b0 = 2 * (kt % 2)
                e.tensor_copy(x_t[:, kt, 0:SEQ], aux[:, b0, :])
                e.tensor_copy(x_t[:, kt, SEQ:NT], aux[:, b0 + 1, 0:NS]).then_inc(x_filled, 1)

            def body(layer):
                turn = counter()

                def low_part(key, dst, src, hi):
                    e.wait_ge(split_hi, plan.split_use[key] + 1)
                    e.tensor_tensor(dst, src, hi.bitcast(F32), ALU.subtract).then_inc(split_lo, 1)
                    e.wait_ge(split_lo, turn(split_lo))

                def max_head(n):
                    j, h = ORDER[n]
                    L = (j + 1) * P
                    key = ("log", j, h)
                    e.wait_ge(ready(key), filled(key))
                    e.tensor_reduce(neg_max[:, j % 2, h:h + 1], aux[:, uses[key][0], 0:L], AX_X, ALU.max,
                                        negate=True).then_inc(max_done, 1)
                    e.wait_ge(max_done, turn(max_done))

                for step in plan.steps:
                    kind = step[0]
                    if kind == "post":
                        p = step[1]
                        kind_p, idx, _ = PANELS[p]
                        g = plan.groups[p][0]
                        key = ("g", g)
                        src = slot(g)
                        if kind_p in STAGED:
                            pass
                        elif kind_p == "gr":
                            u = plan.gate_tmp_use["gr", idx]
                            e.wait_ge(gated, gated_no["gr", idx])
                            e.tensor_tensor(halves(gla_r[:, idx, :]), src, halves(gate_tmp[:, u % 2, :]), ALU.mult).then_inc(free(key), 1)
                            e.wait_ge(free(key), emptied(key))
                        elif kind_p == "oab":
                            for gate, gg in ((gate_a, g), (gate_b, g + 1)):
                                k2 = ("g", gg)
                                e.wait_ge(gates_done, 2 * idx + 1 + (gate is gate_b))
                                e.wait_ge(ready(k2), filled(k2))
                                e.tensor_tensor(halves(gate[:, idx, :]), slot(gg), halves(gate[:, idx, :]),
                                                    ALU.mult).then_inc(free(k2), 1)
                                e.wait_ge(free(k2), emptied(k2))
                            u = plan.split_use["merge", idx] % 2
                            e.wait_ge(free(("g", g)), emptied(("g", g)))
                            e.tensor_tensor(tmp[:, u, :], gate_a[:, idx, :], gate_b[:, idx, :], ALU.add).then_inc(split_src, 1)
                            e.wait_ge(split_src, turn(split_src))
                            low_part(("merge", idx), mid_lo[:, idx, :], tmp[:, u, :], mid_hi[:, idx, :])
                        elif kind_p in ("o", "down"):
                            m = idx if kind_p == "o" else idx[1]
                            e.wait_ge(ready(key), filled(key))
                            e.tensor_tensor(halves(x_t[:, m, :]), src, halves(x_t[:, m, :]), ALU.add).then_inc(free(key), 1)
                            e.wait_ge(free(key), emptied(key))
                        elif kind_p == "gate":
                            u = plan.gate_tmp_use["gate", idx]
                            v = plan.split_use["ff", idx] % 2
                            e.wait_ge(gated, gated_no["gate", idx])
                            e.tensor_tensor(halves(tmp[:, v, :]), src, halves(gate_tmp[:, u % 2, :]), ALU.mult).then_inc(free(key), 1)
                            e.wait_ge(free(key), emptied(key))
                        elif kind_p == "up":
                            part, i = idx
                            v = plan.split_use["ff", idx] % 2
                            e.wait_ge(ready(key), filled(key))
                            e.wait_ge(free(("g", g - 1)), emptied(("g", g - 1)))
                            e.tensor_tensor(halves(tmp[:, v, :]), src, halves(tmp[:, v, :]), ALU.mult).then_inc(free(key), 1)
                            e.wait_ge(free(key), emptied(key))
                            k = i - sum(FF_PARTS[:part])
                            low_part(("ff", idx), mid_lo[:, k, :], tmp[:, v, :], mid_hi[:, k, :])
                    elif kind == "gains":
                        e.wait_ge(ready(("gains",)), filled(("gains",)))
                        e.tensor_copy(gains[:], aux[:, 2, 0:2 * KD + 1]).then_inc(free(("gains",)), 1)
                        e.wait_ge(free(("gains",)), emptied(("gains",)))
                    elif kind == "norm":
                        norm = step[1]
                        e.wait_ge(rstd_done, norm)
                        e.wait_ge(small_ready, 16 * SMALL_LOADS)
                        for kt in range(KD + 1):
                            if kt < KD:
                                u = plan.split_use["norm", norm, kt] % 2
                                e.scalar_tensor_tensor(out=tmp[:, u, :], in0=x_t[:, kt, :],
                                                           scalar=gains[:, (norm - 1) * KD + kt:(norm - 1) * KD + kt + 1], in1=rstd[:],
                                                           op0=ALU.mult, op1=ALU.mult).then_inc(split_src, 1)
                                e.wait_ge(split_src, turn(split_src))
                            if kt > 0:
                                key = ("norm", norm, kt - 1)
                                low_part(key, in_lo[:, kt - 1, :], tmp[:, plan.split_use[key] % 2, :],
                                         in_hi[:, kt - 1, :])
                    elif kind == "row":
                        p = step[1]
                        kind_p, idx, _ = PANELS[p]
                        bx, by = uses["rowX", p][0], uses["rowY", p][0]
                        if kind_p == "gv":
                            buf, lo, w, src0 = gv_rows, idx * P, P, 0
                        elif kind_p == "q":
                            buf, lo, w, src0 = q_rows, idx * P, P, 0
                        elif kind_p in ("k", "v"):
                            buf, lo, w, src0 = kv_rows, idx * P + (KV_W if kind_p == "v" else 0), P, 0
                        elif kind_p == "qi":
                            buf, lo, w, src0 = q_rows, ATTN_W + idx * P, P, 0
                        else:
                            buf, lo, w, src0 = q_rows, ATTN_W + IDX_W, ID, MISC_KI
                        x3 = aux[:, bx, :].rearrange("p (t n) -> p t n", t=4)
                        if kind_p == "q":
                            at0 = HEAD_TILE[2 * idx][0] * 2 + HEAD_TILE[2 * idx][1]
                            heads = q_rows[:, :, 0:ATTN_W].rearrange("p t (h d) -> p t h d", d=HD)
                            e.wait_ge(ready(("rowX", p)), filled(("rowX", p)))
                            e.tensor_copy(heads[:, 0:4, at0:at0 + 3:2, :],
                                              x3.rearrange("p t (h d) -> p t h d", d=HD)).then_inc(free(("rowX", p)), 1)
                            e.wait_ge(free(("rowX", p)), emptied(("rowX", p)))
                            e.wait_ge(ready(("rowY", p)), filled(("rowY", p)))
                            e.tensor_copy(heads[0:NS, 4, at0:at0 + 3:2, :],
                                              aux[0:NS, by, 0:P].rearrange("p (h d) -> p h d", d=HD)).then_inc(free(("rowY", p)), 1)
                            e.wait_ge(free(("rowY", p)), emptied(("rowY", p)))
                            continue
                        e.wait_ge(ready(("rowX", p)), filled(("rowX", p)))
                        if kind_p == "misc":
                            e.tensor_copy(wi_rows[:, 0:4, :], x3[:, :, MISC_WI:MISC_WI + IDX_HEADS]).then_inc(dve_step, 1)
                            e.wait_ge(dve_step, turn(dve_step))
                        e.tensor_copy(buf[:, 0:4, lo:lo + w], x3[:, :, src0:src0 + w]).then_inc(free(("rowX", p)), 1)
                        e.wait_ge(free(("rowX", p)), emptied(("rowX", p)))
                        e.wait_ge(ready(("rowY", p)), filled(("rowY", p)))
                        if kind_p == "misc":
                            e.tensor_copy(wi_rows[0:NS, 4, :], aux[0:NS, by, MISC_WI:MISC_WI + IDX_HEADS]).then_inc(dve_step, 1)
                            e.wait_ge(dve_step, turn(dve_step))
                        e.tensor_copy(buf[0:NS, 4, lo:lo + w], aux[0:NS, by, src0:src0 + w]).then_inc(free(("rowY", p)), 1)
                        e.wait_ge(free(("rowY", p)), emptied(("rowY", p)))
                    elif kind == "qknorm":
                        t = step[1]
                        n = tile_rows(t)
                        q3 = q_rows[0:n, t, :].rearrange("p (h d) -> p h d", d=HD)
                        k3 = kv_rows[0:n, t, 0:KV_W].rearrange("p (h d) -> p h d", d=HD)
                        e.wait_ge(rows_sq, t + 1)
                        e.tensor_reduce(sums[0:n, 0:13], sq_rows[0:n, :, :], AX_X, ALU.add).then_inc(rows_ss, 1)
                        e.wait_ge(rows_ss, turn(rows_ss))
                        e.wait_ge(rows_std, t + 1)
                        parts = ((q3[:, 0:8, :], 0, 8, 0), (k3, 8, 4, 1), (q3[:, 12:13, :], 12, 1, 2))
                        for x3, s0, nh, gi in parts:
                            e.tensor_tensor(x3, x3, bcast(sums[0:n, s0:s0 + nh], 2, HD), ALU.mult).then_inc(dve_step, 1)
                            e.wait_ge(dve_step, turn(dve_step))
                        for x3, s0, nh, gi in parts:
                            e.tensor_tensor(x3, x3, bcast(qk_g[0:n, gi, :], 1, nh), ALU.mult).then_inc(dve_step, 1)
                            e.wait_ge(dve_step, turn(dve_step))
                        cos = const("cos")[0:n, t * ROT:(t + 1) * ROT]
                        sin = const("sin")[0:n, t * ROT:(t + 1) * ROT]
                        for last, x3, nh in ((False, q3, 13), (True, k3, 4)):
                            e.tensor_tensor(rope1[0:n, 0:nh, :], x3[:, :, 0:ROT], bcast(cos, 1, nh), ALU.mult).then_inc(dve_step, 1)
                            e.wait_ge(dve_step, turn(dve_step))
                            e.tensor_tensor(rope2[0:n, 0:nh, 0:HALF_ROT], x3[:, :, HALF_ROT:ROT],
                                                bcast(sin[:, 0:HALF_ROT], 1, nh), ALU.mult).then_inc(dve_step, 1)
                            e.wait_ge(dve_step, turn(dve_step))
                            e.tensor_tensor(rope2[0:n, 0:nh, HALF_ROT:ROT], x3[:, :, 0:HALF_ROT],
                                                bcast(sin[:, HALF_ROT:ROT], 1, nh), ALU.mult).then_inc(dve_step, 1)
                            e.wait_ge(dve_step, turn(dve_step))
                            raised = rows_done if last else dve_step
                            e.tensor_tensor(x3[:, :, 0:ROT], rope1[0:n, 0:nh, :], rope2[0:n, 0:nh, :], ALU.add).then_inc(raised, 1)
                            e.wait_ge(raised, turn(raised))
                    elif kind == "qkT":
                        t = step[1]
                        n = tile_rows(t)
                        key = ("ik", t)
                        e.wait_ge(ready(key), filled(key))
                        v = aux[:, 1, :].rearrange("p (m n) -> p m n", m=4)
                        e.tensor_copy(qi_t[:, :, token_slice(t)], v[:, 0:2, 0:n]).then_inc(dve_step, 1)
                        e.wait_ge(dve_step, turn(dve_step))
                        e.tensor_copy(k_t[:, :, token_slice(t)], v[:, 2:4, 0:n]).then_inc(free(key), 1)
                        e.wait_ge(free(key), emptied(key))
                    elif kind == "z":
                        for i in range(3):
                            n = tile_rows(2 * i)
                            tiles = min(2, NTILE - 2 * i)
                            dst = la[0:n, 2 * i:2 * i + tiles, :].rearrange("p t n -> p (t n)")
                            e.wait_ge(ln_done, i + 1)
                            e.scalar_tensor_tensor(out=dst, in0=aux[0:n, uses["z", i][0], 0:tiles * GK_W],
                                                       scalar=0.0, in1=dst, op0=ALU.min, op1=ALU.subtract).then_inc(free(("z", i)), 1)
                            e.wait_ge(free(("z", i)), emptied(("z", i)))
                    elif kind == "decay":
                        for i in range(3):
                            if i < 2:
                                v = aux[:, i, :].rearrange("p (c s) -> p c s", s=CHUNK)
                                ref, end = b_ref[:, i, 0:16], b_end[:, i, 0:16]
                                mid, last = CHUNK // 2 - 1, CHUNK - 1
                                dst = d_t[:, i, 0:SEQ].rearrange("p (c s) -> p c s", s=CHUNK)
                                rb = bcast(ref, 2, CHUNK)
                                e.wait_ge(ready(("b", i)), filled(("b", i)))
                                e.tensor_copy(ref, v[:, :, mid]).then_inc(dve_step, 1)
                                e.wait_ge(dve_step, turn(dve_step))
                                e.tensor_copy(end, v[:, :, last]).then_inc(dve_step, 1)
                                e.wait_ge(dve_step, turn(dve_step))
                                e.tensor_tensor(dst, v, rb, ALU.subtract).then_inc(free(("b", i)), 1)
                                e.wait_ge(free(("b", i)), emptied(("b", i)))
                            else:
                                e.wait_ge(ready(("b", 2)), filled(("b", 2)))
                                for hp in range(2):
                                    v = aux[:, 2, hp * NS:(hp + 1) * NS].rearrange("p (c s) -> p c s", s=DEC_SEQ)
                                    e.tensor_copy(b_ref[:, hp, 16:24], v[:, :, DEC_SEQ // 2 - 1]).then_inc(dve_step, 1)
                                    e.wait_ge(dve_step, turn(dve_step))
                                    e.tensor_copy(b_end[:, hp, 16:24], v[:, :, DEC_SEQ - 1]).then_inc(dve_step, 1)
                                    e.wait_ge(dve_step, turn(dve_step))
                                for hp in range(2):
                                    v = aux[:, 2, hp * NS:(hp + 1) * NS].rearrange("p (c s) -> p c s", s=DEC_SEQ)
                                    dst = d_t[:, hp, SEQ:NT].rearrange("p (c s) -> p c s", s=DEC_SEQ)
                                    rb = bcast(b_ref[:, hp, 16:24], 2, DEC_SEQ)
                                    if hp == 0:
                                        e.tensor_tensor(dst, v, rb, ALU.subtract).then_inc(dve_step, 1)
                                        e.wait_ge(dve_step, turn(dve_step))
                                    else:
                                        e.tensor_tensor(dst, v, rb, ALU.subtract).then_inc(free(("b", 2)), 1)
                                        e.wait_ge(free(("b", 2)), emptied(("b", 2)))
                        e.tensor_tensor(e_add[:], b_end[:], b_ref[:], ALU.subtract).then_inc(decay_done, 1)
                        e.wait_ge(decay_done, turn(decay_done))
                    elif kind == "gexp":
                        e.memset(g_attn[:], 0.0).then_inc(dve_step, 1)
                        e.wait_ge(dve_step, turn(dve_step))
                        e.wait_ge(exps_done, 1)
                        for x, y in ((gq, "gq"), (gk, "gk")):
                            for i in range(2):
                                e.wait_ge(free(("g", gqk_group[y, i])), emptied(("g", gqk_group[y, i])))
                        e.tensor_tensor(gq[:], gq[:], e_t[:], ALU.mult).then_inc(dve_step, 1)
                        e.wait_ge(dve_step, turn(dve_step))
                        e.tensor_tensor(gk[:], gk[:], d_t[:], ALU.mult).then_inc(gqk_done, 1)
                        e.wait_ge(gqk_done, turn(gqk_done))
                    elif kind == "qiz":
                        e.wait_ge(free(("ik", 4)), emptied(("ik", 4)))
                        for h in range(IDX_HEADS):
                            src = qi_t[64 * (h % 2):64 * (h % 2) + 64, h // 2, SEQ:NT]
                            raised = qiz_done if h == IDX_HEADS - 1 else dve_step
                            e.tensor_copy(qiz[:, :, h * DEC_SEQ:(h + 1) * DEC_SEQ],
                                              src.rearrange("p (b t) -> p b t", t=DEC_SEQ)).then_inc(raised, 1)
                            e.wait_ge(raised, turn(raised))
                        for g in range(2):
                            e.wait_ge(ready(("wi", g)), filled(("wi", g)))
                            e.tensor_tensor_reduce(out=wi_tmp[:, g, :], in0=aux[:, uses["wi", g][0], 0:IDX_HEADS],
                                                       in1=const("head_rows"), scale=IDX_SCALE, scalar=0.0,
                                                       op0=ALU.mult, op1=ALU.add, accum_out=wi_s[:, g:g + 1]).then_inc(free(("wi", g)), 1)
                            e.wait_ge(free(("wi", g)), emptied(("wi", g)))
                    elif kind == "kidx":
                        g = step[1]
                        e.wait_ge(ready(("sscore", g)), filled(("sscore", g)))
                        e.wait_ge(free(("wi", g)), emptied(("wi", g)))
                        e.tensor_scalar(s_heads[:, g, :], aux[:, 2, 0:NEW_KEYS], 0.0, wi_s[:, g:g + 1],
                                            ALU.max, ALU.mult).then_inc(free(("sscore", g)), 1)
                        e.wait_ge(free(("sscore", g)), emptied(("sscore", g)))
                    elif kind == "sindex":
                        e.memset(scores_s[:, NEW_KEYS:SAMPLE_W], -MASKED).then_inc(dve_step, 1)
                        e.wait_ge(dve_step, turn(dve_step))
                        e.wait_ge(ready(("ssum",)), filled(("ssum",)))
                        e.tensor_copy(scores_s[:, 0:PAST], aux[0:NS, 3, 0:PAST]).then_inc(dve_step, 1)
                        e.wait_ge(dve_step, turn(dve_step))
                        e.tensor_tensor(scores_s[:, PAST:NEW_KEYS], aux[0:NS, 3, PAST:NEW_KEYS],
                                            const("own_new", NS), ALU.add).then_inc(free(("ssum",)), 1)
                        e.wait_ge(free(("ssum",)), emptied(("ssum",)))
                    elif kind == "index":
                        j = step[1]
                        L = (j + 1) * P
                        lo, hi = score_cols[j]
                        acc = scores[:, lo:hi]
                        for h in range(IDX_HEADS):
                            key = ("index", j, h)
                            src = gate_tmp[:, plan.gate_tmp_use[key] % 2, 0:L]
                            e.wait_ge(free(key), emptied(key))
                            if h == 0:
                                e.tensor_scalar(acc, src, wi_rows[:, j, 0:1], None, ALU.mult).then_inc(index_added, 1)
                                e.wait_ge(index_added, turn(index_added))
                            else:
                                e.scalar_tensor_tensor(out=acc, in0=src, scalar=wi_rows[:, j, h:h + 1], in1=acc,
                                                           op0=ALU.mult, op1=ALU.add).then_inc(index_added, 1)
                                e.wait_ge(index_added, turn(index_added))
                        e.tensor_tensor(acc[:, L - P:L], acc[:, L - P:L], const("tri"), ALU.add).then_inc(dve_step, 1)
                        e.wait_ge(dve_step, turn(dve_step))
                    elif kind == "topk":
                        _, w, r = step
                        if w == "s":
                            buf, t8, out, last = scores_s[:], top8s, mask_s[:], (TOPK_SAMPLE + PAD_TOP) // 8 - 1
                            width = NEW_KEYS
                        else:
                            lo, hi = score_cols[w]
                            buf, t8, last, width = scores[:, lo:hi], top8, TOPK_PROMPT // 8 - 1, (w + 1) * P
                            out = mask_b[:, w - 1, 0:width]
                        e.max(out=t8[0:buf.shape[0], :], in_=buf).then_inc(dve_step, 1)
                        e.wait_ge(dve_step, turn(dve_step))
                        e.match_replace(out=buf, in_to_replace=t8[0:buf.shape[0], :], in_values=buf,
                                            imm_value=TAKEN).then_inc(dve_step, 1)
                        e.wait_ge(dve_step, turn(dve_step))
                        if r == last:
                            e.tensor_scalar(out, buf[:, 0:width], TAKEN / 1.5, MASKED, ALU.is_gt, ALU.mult).then_inc(masks_done, 1)
                            e.wait_ge(masks_done, turn(masks_done))
                    elif kind == "intra":
                        t = step[1]
                        n = tile_rows(t)
                        e.wait_ge(ready(("kT", t)), filled(("kT", t)))
                        e.tensor_copy(gk_rows[0:n, t % 2, :], aux[0:n, 3, 0:GK_W]).then_inc(free(("kT", t)), 1)
                        e.wait_ge(free(("kT", t)), emptied(("kT", t)))
                        if t == 4:
                            e.wait_ge(ready(("inE", t)), filled(("inE", t)))
                            e.memset(g_attn[0:NS, :, :], 0.0).then_inc(dve_step, 1)
                            e.wait_ge(dve_step, turn(dve_step))
                        for par, key in enumerate((("inE", t), ("inO", t))):
                            causal = const("chunk_sum") if t < 4 else const("sample_sum", NS)
                            src = aux[0:n, uses[key][0], 0:2 * P].rearrange("p (g n) -> p g n", g=2)[:, :, 0:n]
                            e.wait_ge(ready(key), filled(key))
                            e.copy_predicated(out=g_attn[0:n, par::2, 0:n], mask=bcast(causal, 1, 2).bitcast(U32),
                                                  data=src).then_inc(free(key), 1)
                            e.wait_ge(free(key), emptied(key))
                    elif kind == "chunk":
                        c = step[1]
                        key = ("kv", c)
                        ps = aux[:, 2, 0:2 * DV].rearrange("p (g n) -> p g n", g=2)
                        e.wait_ge(ready(key), filled(key))
                        for hp in range(2):
                            if c == 0:
                                ins = e.tensor_scalar(state[:, hp, :], ps[:, hp, :], e_add[:, hp, c:c + 1], None, ALU.mult)
                            else:
                                if hp == 0:
                                    e.wait_ge(decayed, c)
                                ins = e.scalar_tensor_tensor(out=state[:, hp, :], in0=ps[:, hp, :],
                                                             scalar=e_add[:, hp, c:c + 1], in1=state_add[:, hp, :],
                                                             op0=ALU.mult, op1=ALU.add)
                            if hp == 0:
                                ins.then_inc(dve_step, 1)
                                e.wait_ge(dve_step, turn(dve_step))
                            else:
                                ins.then_inc(free(key), 1)
                                e.wait_ge(free(key), emptied(key))
                    elif kind == "sround":
                        r = step[1]

                        def per_batch(x):
                            return bcast(x[:, :, 16 + 2 * r:18 + 2 * r].rearrange("p g b -> p b g"), 3, DV)
                        e.wait_ge(s_state_ready[r % 2], 16 * 4 * (r // 2 + 1))
                        if r:
                            e.wait_ge(ready(("skv", r - 1)), filled(("skv", r - 1)))
                        st = s_state[:, r % 2, :, :, :]
                        e.tensor_tensor(s_state_in[:], st, per_batch(e_ref), ALU.mult).then_inc(dve_step, 1)
                        e.wait_ge(dve_step, turn(dve_step))
                        e.tensor_tensor(gk_one[:], bcast(gk_rows[0:NS, 0, :], 1, 2),
                                            bcast(const("batch_rows", NS)[:, 2 * r:2 * r + 2], 2, GK_W), ALU.mult).then_inc(s_in_done, 1)
                        e.wait_ge(s_in_done, turn(s_in_done))
                        e.tensor_tensor(st, st, per_batch(e_end), ALU.mult).then_inc(dve_step, 1)
                        e.wait_ge(dve_step, turn(dve_step))
                        e.wait_ge(ready(("skv", r)), filled(("skv", r)))
                        ps = aux[:, 2, :].rearrange("p (b g n) -> p b g n", b=2, g=2)
                        e.tensor_tensor(s_state_add[:], ps, per_batch(e_add), ALU.mult).then_inc(free(("skv", r)), 1)
                        e.wait_ge(free(("skv", r)), emptied(("skv", r)))
                        e.tensor_tensor(st, st, s_state_add[:], ALU.add).then_inc(s_out_done, 1)
                        e.wait_ge(s_out_done, turn(s_out_done))
                    elif kind == "gnorm":
                        h = step[1]
                        root = gate_tmp[:, plan.gate_tmp_use["gn", h] % 2, :]
                        e.wait_ge(gn_root, h + 1)
                        e.scalar_tensor_tensor(out=gla_o[:, h, :], in0=gla_o[:, h, :], scalar=gains[:, 2 * KD:2 * KD + 1],
                                                   in1=root, op0=ALU.mult, op1=ALU.mult).then_inc(dve_step, 1)
                        e.wait_ge(dve_step, turn(dve_step))
                        e.tensor_tensor(gla_o[:, h, :], gla_o[:, h, :], gla_r[:, h, :], ALU.mult).then_inc(gnorm_done, 1)
                        e.wait_ge(gnorm_done, turn(gnorm_done))
                    elif kind == "mix":
                        for kt in range(KD):
                            src = attn_t[:, kt, :] if kt < 4 else gla_o[:, kt - 4, :]
                            low_part(("mix", kt), in_lo[:, kt, :], src, in_hi[:, kt, :])
                    elif kind == "qz":
                        e.wait_ge(state_stored, 16 * 2)
                        e.wait_ge(s_stored, 16 * 2 * DEC_BATCH)
                        e.wait_ge(ready(("oO", 4)), filled(("oO", 4)))
                        e.memset(qz[:], 0.0).then_inc(dve_step, 1)
                        e.wait_ge(dve_step, turn(dve_step))
                        for h in range(N_HEADS):
                            tile, half = HEAD_TILE[h]
                            rows = slice(64 * half, 64 * half + 64)
                            if h == 0:
                                e.wait_ge(free(("q", 4)), emptied(("q", 4)))
                            raised = qz_done if h == N_HEADS - 1 else dve_step
                            e.tensor_copy(qz[rows, :, h // 4, h * DEC_SEQ:(h + 1) * DEC_SEQ],
                                              q_t[rows, tile, SEQ:NT].rearrange("p (b t) -> p b t", t=DEC_SEQ)).then_inc(raised, 1)
                            e.wait_ge(raised, turn(raised))
                    elif kind == "slog" and step[1] % 2 == 1:
                        i = step[1] // 2
                        e.wait_ge(ready(("slog", i)), filled(("slog", i)))
                        e.tensor_reduce(neg_max_s[:, i:i + 1], aux[:, uses["slog", i][0], 0:NEW_KEYS], AX_X,
                                            ALU.max, negate=True).then_inc(max_done, 1)
                        e.wait_ge(max_done, turn(max_done))
                        e.wait_ge(free(("slog", i)), emptied(("slog", i)))
                        e.reciprocal(p_inv_s[:, i:i + 1], p_sum_s[:, i:i + 1]).then_inc(dve_step, 1)
                        e.wait_ge(dve_step, turn(dve_step))
                        e.tensor_scalar(p_t[:, i % 2, 0:NEW_KEYS], p_t[:, i % 2, 0:NEW_KEYS],
                                            p_inv_s[:, i:i + 1], None, ALU.mult).then_inc(p_scaled, 1)
                        e.wait_ge(p_scaled, turn(p_scaled))
                    elif kind == "spT":
                        i = step[1]
                        if i >= 2:
                            e.wait_ge(kc_free, 2 * i - 2)
                        e.wait_ge(ready(("spT", i)), filled(("spT", i)))
                        e.tensor_copy(pT_t[:, i % 2, 0:2, :], aux[:, 2, 0:2 * P].rearrange("p (s n) -> p s n", s=2)).then_inc(dve_step, 1)
                        e.wait_ge(dve_step, turn(dve_step))
                        e.tensor_copy(pT_t[0:NS, i % 2, 2, :], aux[0:NS, 2, 2 * P:3 * P]).then_inc(free(("spT", i)), 1)
                        e.wait_ge(free(("spT", i)), emptied(("spT", i)))
                    elif kind == "attn":
                        _, j, h = step
                        n = j * N_HEADS + h
                        L = (j + 1) * P
                        if n == 0:
                            max_head(0)
                        if n + 1 < len(ORDER):
                            max_head(n + 1)
                    elif kind == "attn_out":
                        j = step[1]
                        e.wait_ge(ready(("o", j)), filled(("o", j)))
                        e.reciprocal(p_inv[:], p_sum[:, j % 2, :]).then_inc(dve_step, 1)
                        e.wait_ge(dve_step, turn(dve_step))
                        e.tensor_tensor(o_rows[:].rearrange("p (h d) -> p h d", d=HD),
                                            aux[:, 3, :].rearrange("p (h d) -> p h d", d=HD), bcast(p_inv[:], 2, HD),
                                            ALU.mult).then_inc(free(("o", j)), 1)
                        e.wait_ge(free(("o", j)), emptied(("o", j)))

            layers(e, body)
            for t in range(NTILE):
                e.wait_ge(y_turned, t + 1)
                n = tile_rows(t)
                for k in range(2):
                    e.tensor_copy(x_rows[0:n, t, k * 512:(k + 1) * 512],
                                  aux[0:n, 2 * (t % 2) + k, :]).then_inc(y_ready, 1)



_INS = ["x_prompt", "x_sample", "cache_k", "cache_v", "cache_kidx", "state_gla", "page_table", "norm1_g", "w_in",
        "q_norm_g", "k_norm_g", "kidx_norm_g", "gla_wa2", "gla_ba", "gla_onorm_g", "w_oa", "w_ob", "w_o", "norm2_g",
        "w_ffn_gu", "w_ffn_down"]
_OUTS = {
    "y_prompt": (1, SEQ, D_MODEL), "y_sample": (DEC_BATCH, DEC_SEQ, D_MODEL),
    "new_k_prompt": (DEPTH, 1, SEQ, N_KV, HD), "new_v_prompt": (DEPTH, 1, SEQ, N_KV, HD),
    "new_kidx_prompt": (DEPTH, 1, SEQ, ID), "new_gla_prompt": (DEPTH, 1, GH, DK, DV),
    "new_k_sample": (DEPTH, DEC_BATCH, DEC_SEQ, N_KV, HD), "new_v_sample": (DEPTH, DEC_BATCH, DEC_SEQ, N_KV, HD),
    "new_kidx_sample": (DEPTH, DEC_BATCH, DEC_SEQ, ID), "new_gla_sample": (DEPTH, DEC_BATCH, GH, DK, DV),
}

def kernel(**inputs):
    import concourse.bacc as bacc
    from concourse.bass_utils import run_bass_kernel_spmd

    nc = bacc.Bacc("TRN2", target_bir_lowering=False, num_devices=1, dynamic_dma_scratch_size=64)
    arrays, args = {}, {}
    for name in _INS:
        a = np.ascontiguousarray(inputs[name])
        arrays[f"in_{name}"] = a
        args[name] = nc.dram_tensor(f"in_{name}", a.shape, mybir.dt.from_np(a.dtype), kind="ExternalInput").ap()
    consts = const_array()
    arrays["in_consts"] = consts
    args["consts"] = nc.dram_tensor("in_consts", consts.shape, F32, kind="ExternalInput").ap()
    for name, shape in _OUTS.items():
        args[name] = nc.dram_tensor(f"out_{name}", shape, F32, kind="ExternalOutput").ap()
    build(nc, args)
    r = run_bass_kernel_spmd(nc, [arrays], core_ids=[0])
    return tuple(r.results[0][f"out_{name}"] for name in _OUTS)
```

```python
from contextlib import ExitStack

import numpy as np

import concourse.bass as bass
from concourse import mybir

F32 = mybir.dt.float32
F32R = mybir.dt.float32r
BF16 = mybir.dt.bfloat16
I32 = mybir.dt.int32
U32 = mybir.dt.uint32
ALU = mybir.AluOpType
ACT = mybir.ActivationFunctionType
AX_X = mybir.AxisListType.X

P = 128
DEPTH = 2
D_MODEL = 1024
SEQ = 512
DEC_BATCH = 8
DEC_SEQ = 8
NS = DEC_BATCH * DEC_SEQ
NT = SEQ + NS
NTILE = 5
PAGE = 128
N_PAGES = 2
PAST = PAGE * N_PAGES
N_POOL = 20
N_HEADS = 8
N_KV = 4
HD = 64
ROT = HD // 4
HALF_ROT = ROT // 2
THETA = 500000.0
IDX_HEADS = 4
ID = 64
TOPK_PROMPT = SEQ // 4
TOPK_SAMPLE = (PAST + DEC_SEQ) // 4
GH = 4
DK = 64
DV = 128
RANK = 16
TAU = 16.0
CHUNK = 32
D_FF = 2816
EPS = 1e-6
KD = D_MODEL // P
HALF = NT // 2
ATTN_W, KV_W, IDX_W = N_HEADS * HD, N_KV * HD, IDX_HEADS * ID
GK_W, GV_W = GH * DK, GH * DV
SPLITS = (ATTN_W, KV_W, KV_W, IDX_W, ID, IDX_HEADS, GK_W, GK_W, GV_W, RANK, GV_W, D_MODEL, D_MODEL)
OFFS = [sum(SPLITS[:i]) for i in range(len(SPLITS))]
O_Q, O_K, O_V, O_QI, O_KI, O_WI, O_GQ, O_GK, O_GV, O_GA, O_GR, O_GTA, O_GTB = OFFS
N_IN = sum(SPLITS)
MISC_KI = 32
MISC_WI = MISC_KI + ID
NEW_KEYS = PAST + NS
PAD_TOP = -TOPK_SAMPLE % 8
SAMPLE_W = NEW_KEYS + PAD_TOP
MASKED = -1e30
TAKEN = -3e38
IDX_SCALE = IDX_HEADS ** -0.5 * ID ** -0.5
FF_TILES = D_FF // P
FF_PARTS = (8, 8, 6)
N_CHUNK = SEQ // CHUNK
RAW_RING = 3
GLA_PANELS = 10
QZ_AT = 2
TOPK_EACH = 2
FILL = {"intra": 1.5, "intra_out": 0.5, "chunk": 1.0, "sround": 2.0, "attn": 1.0, "attn_pv": 0.2, "attn_t": 0.2,
        "topk": 0.5, "kcT": 1.0, "slog": 1.6, "gnorm": 2.0}


def tile_rows(t):
    return P if t < 4 else NS


def token_slice(t):
    return slice(t * P, t * P + tile_rows(t))


def bcast(ap, axis, n):
    dims = [list(d) for d in ap.ap]
    dims.insert(axis, [0, n])
    return bass.AP(ap.tensor, ap.offset, dims)


CONSTS = {}


def const_layout():
    at = 0
    for name, w in (("ident", P), ("chunk_sum", P), ("sample_sum", NS), ("tri", P), ("own_new", NS),
                    ("cos", NTILE * ROT), ("sin", NTILE * ROT), ("batch_rows", DEC_BATCH),
                    ("head_rows", IDX_HEADS), ("spread", 2 * P), ("gather", 2 * NS), ("repeat", 8 * NS)):
        CONSTS[name] = (at, at + w)
        at += w
    return at


CONST_W = const_layout()
KEPT_W = CONSTS["repeat"][0]


def const_array():
    c = np.zeros((P, CONST_W), np.float32)

    def put(name, a):
        lo, hi = CONSTS[name]
        a = a.reshape(a.shape[0], -1)
        assert a.shape[1] == hi - lo
        c[:a.shape[0], lo:hi] = a

    i = np.arange(P)
    put("ident", np.eye(P, dtype=np.float32))
    put("chunk_sum", ((i[:, None] // CHUNK == i[None] // CHUNK) & (i[:, None] <= i[None])) / np.float32(TAU))
    s = np.arange(NS)
    put("sample_sum", ((s[:, None] // DEC_SEQ == s[None] // DEC_SEQ) & (s[:, None] <= s[None])) / np.float32(TAU))
    put("tri", np.where(i[None] <= i[:, None], 0, MASKED).astype(np.float32))
    put("own_new", np.where((s[:, None] // DEC_SEQ == s[None] // DEC_SEQ) & (s[None] <= s[:, None]), 0,
                            MASKED).astype(np.float32))
    inv = np.power(np.float32(THETA), -np.arange(HALF_ROT, dtype=np.float32) * np.float32(2.0) / np.float32(ROT))
    pos = np.zeros((P, NTILE), np.float32)
    pos[:, :4] = i[:, None] + P * np.arange(4)[None]
    pos[:NS, 4] = PAST + s % DEC_SEQ
    ang = pos[:, :, None] * inv.astype(np.float32)[None, None]
    cos, sin = np.cos(ang).astype(np.float32), np.sin(ang).astype(np.float32)
    put("cos", np.concatenate([cos, cos], -1))
    put("sin", np.concatenate([-sin, sin], -1))
    put("batch_rows", (s[:, None] // DEC_SEQ == np.arange(DEC_BATCH)[None]).astype(np.float32))
    rb, rh, rt = i // 32, i // 8 % 4, i % 8
    put("head_rows", (rh[:, None] == np.arange(IDX_HEADS)[None]).astype(np.float32))
    sp = np.stack([(s[:, None] == (g * 4 + rb) * 8 + rt) for g in range(2)], 1).astype(np.float32)
    put("spread", sp)
    put("gather", np.ascontiguousarray(sp.transpose(2, 1, 0)))
    put("repeat", np.stack([(s[:, None] == b * 8 + s[None] % 8) for b in range(DEC_BATCH)], 1).astype(np.float32))
    return c


def make_panels():
    out = []
    for kind, off, n in (("q", O_Q, 4), ("k", O_K, 2), ("v", O_V, 2), ("qi", O_QI, 2)):
        out += [(kind, i, [("w_in", 0, KD, off + i * P, P, 0)]) for i in range(n)]
    out.append(("misc", 0, [("w_in", 0, KD, O_GA, MISC_KI, 0), ("w_in", 0, KD, O_KI, P - MISC_KI, MISC_KI)]))
    for kind, off, n in (("gq", O_GQ, 2), ("gk", O_GK, 2), ("gv", O_GV, 4), ("gr", O_GR, 4),
                         ("gta", O_GTA, 8), ("gtb", O_GTB, 8)):
        out += [(kind, i, [("w_in", 0, KD, off + i * P, P, 0)]) for i in range(n)]
    for j in range(KD):
        out.append(("oab", j, [("w_ob", 0, 4, j * P, P, 0), ("w_oa", 0, 4, j * P, P, 4 * P)]))
    for j in range(KD):
        out.append(("o", j, [("w_o", 0, KD, j * P, P, 0)]))
    first = 0
    for part, n in enumerate(FF_PARTS):
        for i in range(first, first + n):
            out.append(("gate", (part, i), [("w_ffn_gu", 0, KD, i * P, P, 0)]))
            out.append(("up", (part, i), [("w_ffn_gu", 0, KD, D_FF + i * P, P, 0)]))
        for m in range(KD):
            out.append(("down", (part, m), [("w_ffn_down", first * P, n, m * P, P, 0)]))
        first += n
    return out


PANELS = make_panels()
N_PANELS = len(PANELS)
assert N_PANELS % RAW_RING == 0
STAGED = ("q", "k", "v", "qi", "misc", "gv")
RAW_READY = []
_count = [0] * RAW_RING
for _p, (_, _, _parts) in enumerate(PANELS):
    _count[_p % RAW_RING] += len(_parts)
    RAW_READY.append(_count[_p % RAW_RING])
SMALL_LOADS = 8


class Plan:

    def __init__(self):
        self.steps = []
        self.uses = {}
        self.per_bank = [0] * 6
        self.slot_keys = []
        self.groups = {}
        n = 0
        for p, (kind, idx, parts) in enumerate(PANELS):
            self.groups[p] = list(range(n, n + (2 if kind == "oab" else 1)))
            n += len(self.groups[p])
        self.n_groups = n
        self.stage_use = {}
        self.stage_release = []
        self.gate_tmp_use = {}
        self.gate_tmp_release = []
        self.split_use = {}
        self.build()

    def open(self, key, bank):
        self.uses[key] = (bank, self.per_bank[bank])
        self.per_bank[bank] += 1

    def stage(self, key, release):
        self.stage_use[key] = len(self.stage_release)
        self.stage_release.append(release)

    def gate_tmp(self, key, release):
        self.gate_tmp_use[key] = len(self.gate_tmp_release)
        self.gate_tmp_release.append(release)

    def split(self, key):
        self.split_use[key] = len(self.split_use)

    def add(self, *step):
        self.steps.append(step)

    def start(self, p):
        for g in self.groups[p]:
            self.open(("g", g), 4 + g % 2)
        self.weights(p + 1)
        self.add("panel", p)

    def weights(self, p):
        if p < N_PANELS and p not in self.split_panels:
            self.split_panels.add(p)
            self.add("weights", p)

    def finish(self, p):
        kind, idx, _ = PANELS[p]
        g = self.groups[p][0]
        if kind in ("gr", "gate"):
            self.gate_tmp((kind, idx), ("bank_free", ("g", g)))
        if kind in STAGED:
            self.stage(("row", p), ("bank_ready", ("rowY", p)))
        if kind == "oab":
            self.split(("merge", idx))
        if kind == "up":
            self.split(("ff", idx))
        self.add("post", p)

    def panel(self, p):
        self.start(p)
        for i in range(KD):
            self.add("part", p, i)
        self.finish(p)

    def woven(self, panels, items):
        weights = [FILL.get(item[0][0], 1.0) if item else 1.0 for item in items]
        done, due, total = 0, 0.0, len(panels) * KD
        for n in range(len(items) + 1):
            while done < (total if n == len(items) else round(due)):
                p, i = panels[done // KD], done % KD
                if i == 0:
                    self.start(p)
                self.add("part", p, i)
                if i == 0 and PANELS[p - 1][0] in STAGED:
                    self.row(p - 1)
                if i == KD - 1:
                    self.finish(p)
                done += 1
            if n < len(items):
                due += weights[n] * total / sum(weights)
            if n < len(items):
                for step in items[n]:
                    self.extra_step(step)

    def stat(self, norm, kt):
        if kt == 0:
            self.gate_tmp(("squares", norm), ("bank_ready", ("stat", norm, 1)))
        else:
            self.n_stat += 1
            self.stage(("stat", norm, kt), ("squares_added", self.n_stat))
        if kt == KD - 1:
            self.open(("stat", norm, 0), 0)
            self.open(("stat", norm, 1), 1)
        self.add("stat", norm, kt)

    def norm(self, norm, p):
        self.weights(p)
        self.add("weights_upper", p + 1)
        self.add("norm", norm)
        self.split_panels.add(p + 1)
        self.add("weights_lower", p + 1)
        for kt in range(KD):
            self.split(("norm", norm, kt))

    def row(self, p):
        m = self.n_row
        self.n_row += 1
        self.open(("rowX", p), 2 * (m % 2))
        self.open(("rowY", p), 2 * (m % 2) + 1)
        self.add("row", p)

    def build(self):
        self.n_stat = 0
        self.split_panels = set()
        for kt in range(KD):
            self.stat(1, kt)
        self.open(("gains",), 2)
        self.add("gains")
        self.norm(1, 0)
        self.n_row = 0
        first = {}
        for p, (kind, _, _) in enumerate(PANELS):
            first.setdefault(kind, p)
        normed = [[("qn", part, t)] for part in ("q", "k", "x") for t in range(NTILE)]
        self.norm_order = [step[0][1:] for step in normed]
        for p in range(first["gq"]):
            self.start(p)
            for i in range(KD):
                self.add("part", p, i)
                if i == 0 and p:
                    self.row(p - 1)
                if first["k"] <= p < first["qi"] + 1 and i in (3, 6) and len(normed) > NTILE:
                    self.extra_step(normed.pop(0)[0])
            self.finish(p)
        assert len(normed) == NTILE
        items = [[], normed[0], [("z",)], normed[1], normed[2] + [("qkT", 0)], [("decay",)], normed[3] + [("qkT", 1)],
                 normed[4] + [("qkT", 2), ("decay_exp",)], [("qn_end",)], [("qkT", 3)], [("qkT", 4)]]
        self.woven(range(first["gq"], first["gv"]), items)
        rounds = [(1, r) for r in range(TOPK_PROMPT // 8)]
        rounds += [("s", r) for r in range((TOPK_SAMPLE + PAD_TOP) // 8)]
        rounds += [(j, r) for j in (2, 3) for r in range(TOPK_PROMPT // 8)]

        def topk(n):
            out = []
            for _ in range(n):
                if rounds:
                    out.append(("topk", *rounds.pop(0)))
            return out
        items = [[("gexp",)], [("qiz",)], [("index", 1)], [("index", 2)], topk(2), [("index", 3)], topk(2),
                 [("kidx", 0)], topk(2), [("kidx", 1)], topk(2), [("sindex",)], topk(2)]
        self.woven(range(first["gv"], first["gr"]), items)
        items = [[], [("kT", 0)], [("intra", 0)], [("intra_out", 0)]]
        for c in range(N_CHUNK):
            items.append([("chunk", c)] + ([("kT", c // 4 + 1)] if c % 4 == 1 else []) + topk(TOPK_EACH))
            if c % 4 == 2:
                items.append([("intra", c // 4 + 1)] + topk(1))
            if c % 4 == 3:
                items.append([("intra_out", c // 4 + 1)] + ([("sin", 0)] if c == N_CHUNK - 1 else []))
        for r in range(4):
            items.append([("sround", r)] + ([("sin", r + 1)] if r < 3 else []) + topk(1))
            items.append(topk(1))
        items.append([("sgla_out",)])
        split = first["gr"] + GLA_PANELS
        self.woven(range(first["gr"], split), items)
        items = [[("gnorm", h)] + topk(TOPK_EACH) for h in range(GH)]
        while rounds:
            items.append(topk(2))
        items[QZ_AT].append(("qz",))
        items += [[("kcT", 0)], [("kcT", 1)]]
        for i in range(5):
            for b in (2 * i, 2 * i + 1):
                if i < 4:
                    items.append([("slog", b)] + ([("kcT", b + 2)] if b + 2 < DEC_BATCH else []))
                if i > 0:
                    items.append([("spT", i - 1)] if b == 2 * i else [("spv", i - 1)])
        items[-1].append(("sample_out",))
        order = [(j, h) for j in range(4) for h in range(N_HEADS)]
        self.attn_order = order
        for j, h in order:
            if h == 1 and j > 0:
                items.append([("attn_t", j - 1)])
            items.append([("attn", j, h)])
            items.append([("attn_pv", j, h)])
            if h == N_HEADS - 1:
                items[-1].append(("attn_out", j))
        self.woven(range(split, first["oab"]), items)
        for kt in range(KD):
            self.split(("mix", kt))
        self.add("mix", "gla")
        self.extra_step(("attn_t", 3))
        self.add("mix", "attention")
        for p in range(first["oab"], N_PANELS):
            self.panel(p)
            kind, idx, _ = PANELS[p]
            if kind == "o" and idx > 0:
                self.stat(2, idx - 1)
            if kind == "o" and idx == KD - 1:
                self.stat(2, idx)
                self.norm(2, p + 1)

    def extra_step(self, step):
        kind = step[0]
        if kind == "z":
            for i, b in ((0, 2), (1, 3), (2, 1)):
                self.open(("z", i), b)
        if kind == "decay":
            for i, b in ((0, 0), (1, 1), (2, 2)):
                self.open(("b", i), b)
        if kind == "qkT":
            for i, b in (("q", 0), ("ik", 1), ("ki", 3)):
                self.open((i, step[1]), b)
        if kind == "index":
            for h in range(IDX_HEADS):
                self.open(("index", step[1], h), 2 + h % 2)
                self.gate_tmp(("index", step[1], h), ("index_added", 4 * (step[1] - 1) + h + 1))
        if kind == "kidx":
            g = step[1]
            self.open(("kidxT", 2 * g), 3)
            self.open(("kidxT", 2 * g + 1), 3)
            self.open(("sscore", g), 2)
        if kind == "qiz":
            self.open(("wi", 0), 3)
            self.open(("wi", 1), 2)
        if kind == "sindex":
            self.open(("ssum",), 3)
        if kind == "intra":
            t = step[1]
            self.open(("inE", t), 3)
            self.open(("inO", t), 2)
        if kind == "kT":
            self.open(("kT", step[1]), 2)
        if kind == "intra_out":
            self.open(("oE", step[1]), 0)
            self.open(("oO", step[1]), 1)
        if kind == "chunk":
            self.open(("kv", step[1]), 2)
        if kind == "sround":
            self.open(("skv", step[1]), 2)
        if kind == "kcT":
            self.open(("kcT", step[1]), 1 + step[1] % 2)
        if kind == "slog" and step[1] % 2 == 0:
            self.open(("slog", step[1] // 2), 0)
        if kind == "spT":
            self.open(("spT", step[1]), 2)
        if kind == "spv" and step[1] == 0:
            self.open(("so",), 3)
        if kind == "attn":
            _, j, h = step
            order = self.attn_order
            n = order.index((j, h))
            if n == 0:
                self.open(("log", j, h), 0)
            if n + 1 < len(order):
                self.open(("log",) + order[n + 1], (n + 1) % 2)
            self.open(("pT", j, h), 2)
        if kind == "attn_pv" and step[2] == 0:
            self.open(("o", step[1]), 3)
        if kind == "attn_t":
            self.open(("oT", step[1]), 2)
        if kind == "gnorm":
            self.open(("gn", step[1], 0), 0)
            self.open(("gn", step[1], 1), 1)
            self.stage(("gn", step[1]), ("bank_ready", ("gn", step[1], 1)))
            self.gate_tmp(("gn", step[1]), ("gnorm_done", step[1] + 1))
        self.add(*step)


def build(nc, A, depth=DEPTH):
    plan = Plan()
    uses = plan.uses

    ctx = ExitStack()
    with ctx:
        base = 192
        cursor = [base]

        def region(nbytes):
            at = cursor[0]
            cursor[0] += (nbytes + 31) // 32 * 32
            return at

        def at(name, shape, dt, offset):
            return nc.alloc_sbuf_tensor_at(name, shape, dt, offset=offset)

        def sb(name, shape, dt=F32):
            n = int(np.prod(shape[1:])) * (2 if dt == BF16 else 4)
            return at(name, shape, dt, region(n))

        cst = sb("cst", [P, KEPT_W])
        x_t = sb("x_t", [P, KD, NT])
        in_hi = sb("in_hi", [P, KD, NT], F32R)
        in_lo = sb("in_lo", [P, KD, NT], F32R)
        w_raw = sb("w_raw", [P, RAW_RING, KD * P])
        w_hi = sb("w_hi", [P, 2, KD * P], F32R)
        w_lo = sb("w_lo", [P, 2, KD * P], F32R)
        tmp = sb("tmp", [P, 2, NT])
        stage = sb("stage", [P, 2, NT])
        gate_tmp = sb("gate_tmp", [P, 2, NT])
        ones = sb("ones", [P, P])
        ident_b = sb("ident_b", [P, P], BF16)
        tri_b = sb("tri_b", [P, P], BF16)
        repeat_b = sb("repeat_b", [NS, DEC_BATCH, NS], BF16)
        eps_t = sb("eps_t", [P, 1])
        pages = sb("pages", [1, DEC_BATCH * N_PAGES], I32)
        gain_rows = sb("gain_rows", [2 * KD + 1, P])
        gains = sb("gains", [P, 2 * KD + 1])
        qk_g = sb("qk_g", [P, 3, HD])
        wa2 = sb("wa2", [RANK, GK_W])
        ba = sb("ba", [1, GK_W])
        ff = region(2 * KD * NT * 4)
        mid_hi = at("mid_hi", [P, KD, NT], F32R, ff)
        mid_lo = at("mid_lo", [P, KD, NT], F32R, ff + KD * NT * 4)
        normed = at("normed", [P, KD, NT], F32, ff)
        gate_a = at("gate_a", [P, KD, NT], F32, ff)
        gla_r = at("gla_r", [P, GH, NT], F32, ff + KD * NT * 4)
        attn_t = at("attn_t", [P, 4, NT], F32, ff + KD * NT * 4)
        gla_o = at("gla_o", [P, GH, NT], F32, ff + (KD + GH) * NT * 4)
        x_rows = at("x_rows", [P, NTILE, D_MODEL], F32, ff)
        repeat_f = at("repeat_f", [P, CONST_W - KEPT_W], F32, ff + NTILE * D_MODEL * 4)
        q_rows = at("q_rows", [P, NTILE, 13 * HD], F32, ff)
        la = at("la", [P, NTILE, GK_W], F32, ff + 16640)
        ga_t = at("ga_t", [RANK, NT], F32, ff + 21760)
        d_t = at("d_t", [P, 2, NT], F32, ff + 24064)
        e_t = at("e_t", [P, 2, NT], F32, ff + 28672)
        sq_rows = at("sq_rows", [P, 13, HD], F32, ff + 33280)
        kidx = at("kidx", [P, DEC_BATCH, N_PAGES, ID], F32, ff)
        kidx_t = at("kidx_t", [ID, 2, 2 * PAST], F32, ff + 4096)
        qiz = at("qiz", [ID, DEC_BATCH, 32], F32, ff + 8192)
        s_heads = at("s_heads", [P, 2, NEW_KEYS], F32, ff + 9216)
        kv_rows = sb("kv_rows", [P, NTILE, 2 * KV_W])
        q_t = sb("q_t", [P, 4, NT])
        k_t = sb("k_t", [P, 2, NT])
        mask_b = sb("mask_b", [P, 3, SEQ], BF16)
        mask_s = sb("mask_s", [NS, NEW_KEYS], BF16)
        wi_rows = sb("wi_rows", [P, NTILE, IDX_HEADS])
        ar = region(0)
        off = [ar]

        def sub(name, shape, dt=F32):
            t = at(name, shape, dt, off[0])
            off[0] += (int(np.prod(shape[1:])) * (2 if dt == BF16 else 4) + 31) // 32 * 32
            return t

        gq = sub("gq", [P, 2, NT])
        gk = sub("gk", [P, 2, NT])
        gk_rows = sub("gk_rows", [P, 2, GK_W])
        gv_rows = sub("gv_rows", [P, NTILE, GV_W])
        state = sub("state", [P, 2, DV])
        state_in = sub("state_in", [P, 2, DV])
        state_add = sub("state_add", [P, 2, DV])
        s_state = sub("s_state", [P, 2, 2, 2, DV])
        s_state_in = sub("s_state_in", [P, 2, 2, DV])
        s_state_add = sub("s_state_add", [P, 2, 2, DV])
        gk_one = sub("gk_one", [NS, 2, GK_W])
        g_attn = sub("g_attn", [P, GH, P])
        qi_t = sub("qi_t", [P, 2, NT])
        ki_t = sub("ki_t", [P, NT])
        scores = sub("scores", [P, 2 * P + 3 * P + 4 * P])
        rstd = at("rstd", [P, NT], F32, off[0] - 4608)
        scores_s = sub("scores_s", [NS, SAMPLE_W])
        end1 = off[0]
        off[0] = ar
        gate_b = sub("gate_b", [P, KD, NT])
        qz = sub("qz", [P, DEC_BATCH, 2, NS])
        k_pages = sub("k_pages", [P, 4, N_PAGES, KV_W])
        v_pages = sub("v_pages", [P, 4, N_PAGES, KV_W])
        p_t = sub("p_t", [P, 2, SEQ])
        pT_t = sub("pT_t", [P, 2, 4, P])
        k_past = sub("k_past", [P, 2, 2, PAST])
        o_rows = sub("o_rows", [P, ATTN_W])
        cursor[0] = max(off[0], end1)
        small = lambda name, w, rows=P: sb(name, [rows, w])
        sums = sb("sums", [P, 2, 16])
        top8 = small("top8", 8)
        top8s = small("top8s", 8)
        b_ref = sb("b_ref", [P, 2, 24])
        b_end = sb("b_end", [P, 2, 24])
        e_ref = sb("e_ref", [P, 2, 24])
        e_end = sb("e_end", [P, 2, 24])
        e_add = sb("e_add", [P, 2, 24])
        wi_s = sb("wi_s", [P, 2])
        wi_tmp = sb("wi_tmp", [P, 2, IDX_HEADS])
        rope1 = sb("rope1", [P, 8, ROT])
        rope2 = sb("rope2", [P, 8, ROT])
        neg_max = sb("neg_max", [P, 2, N_HEADS])
        p_sum = sb("p_sum", [P, 2, N_HEADS])
        p_inv = sb("p_inv", [P, N_HEADS])
        neg_max_s = sb("neg_max_s", [P, 4])
        p_sum_s = sb("p_sum_s", [P, 4])
        p_inv_s = sb("p_inv_s", [P, 4])
        assert cursor[0] <= nc.sbuf_usable_end, cursor[0]

        aux = nc.alloc_psum_tensor("aux", [P, 4, 512], F32)
        prod = nc.alloc_psum_tensor("prod", [P, 4, 512], F32)

        def const(name, rows=P):
            lo, hi = CONSTS[name]
            return cst[0:rows, lo:hi]

        def slot(g):
            s = g % 2
            return prod[:, 2 * s:2 * s + 2, 0:HALF]

        def halves(ap):
            return ap.rearrange("p (h n) -> p h n", h=2)

        def semaphore(name):
            return ctx.enter_context(nc.semaphore(name))

        x_loaded = semaphore("x_loaded")
        x_turned = semaphore("x_turned")
        once = semaphore("once")
        y_turned = semaphore("y_turned")
        y_ready = semaphore("y_ready")
        y_stored = semaphore("y_stored")
        x_filled = semaphore("x_filled")
        opened_layer = semaphore("opened_layer")
        passed = semaphore("passed")
        bank_ready = [semaphore(f"bank{i}_ready") for i in range(6)]
        bank_free = [semaphore(f"bank{i}_free") for i in range(6)]
        raw_ready = [semaphore(f"raw{i}_ready") for i in range(RAW_RING)]
        w_hi_done = semaphore("w_hi_done")
        w_lo_done = semaphore("w_lo_done")
        staged = semaphore("staged")
        squares_added = semaphore("squares_added")
        squares_ready = semaphore("squares_ready")
        pool_src = semaphore("pool_src")
        gated = semaphore("gated")
        index_added = semaphore("index_added")
        split_src = semaphore("split_src")
        split_hi = semaphore("split_hi")
        split_lo = semaphore("split_lo")
        x_added = semaphore("x_added")
        dve_step = semaphore("dve_step")
        rows_sq = semaphore("rows_sq")
        rows_ss = semaphore("rows_ss")
        rows_std = semaphore("rows_std")
        rows_done = semaphore("rows_done")
        ln_done = semaphore("ln_done")
        ga_done = semaphore("ga_done")
        decay_done = semaphore("decay_done")
        exps_done = semaphore("exps_done")
        gqk_done = semaphore("gqk_done")
        qiz_done = semaphore("qiz_done")
        s_in_done = semaphore("s_in_done")
        s_out_done = semaphore("s_out_done")
        gnorm_done = semaphore("gnorm_done")
        masks_done = semaphore("masks_done")
        qz_done = semaphore("qz_done")
        max_done = semaphore("max_done")
        pv_done = semaphore("pv_done")
        p_scaled = semaphore("p_scaled")
        kc_free = semaphore("kc_free")
        small_ready = semaphore("small_ready")
        kidx_ready = semaphore("kidx_ready")
        s_state_ready = [semaphore(f"s_state{i}_ready") for i in range(2)]
        k_ready = [semaphore(f"k_pages{i}_ready") for i in range(4)]
        v_ready = [semaphore(f"v_pages{i}_ready") for i in range(4)]
        stored = semaphore("stored")
        s_stored = semaphore("s_stored")
        state_stored = semaphore("state_stored")
        sample_intra = semaphore("sample_intra")
        gates_done = semaphore("gates_done")
        rstd_done = semaphore("rstd_done")
        gn_root = semaphore("gn_root")
        rows_ln = semaphore("rows_ln")
        state_in_done = semaphore("state_in_done")
        decayed = semaphore("decayed")
        s_decayed = semaphore("s_decayed")
        k_past_used = semaphore("k_past_used")
        z_abs = semaphore("z_abs")
        z_exp = semaphore("z_exp")
        arrived = semaphore("arrived")
        layer_sems = range(bank_ready[0].num, arrived.num + 1)

        free_of, of_bank = {}, [0, 0]
        for p, (kind, idx, _) in enumerate(PANELS):
            for g in plan.groups[p]:
                if kind == "o":
                    free_of["g", g] = (x_added, idx + 1)
                elif kind in STAGED:
                    free_of["g", g] = (staged, plan.stage_use["row", p] + 1)
                elif kind == "down":
                    free_of["g", g] = (x_added, KD + idx[0] * KD + idx[1] + 1)
                else:
                    of_bank[g % 2] += 1
                    free_of["g", g] = (bank_free[4 + g % 2], of_bank[g % 2])
        for key, (bank, use) in uses.items():
            if bank < 4:
                free_of[key] = (bank_free[bank], use + 1)

        def ready(key):
            return bank_ready[uses[key][0]]

        def filled(key):
            return uses[key][1] + 1

        def free(key):
            return free_of[key][0]

        def emptied(key):
            return free_of[key][1]

        def opened(key):
            return uses[key][1]

        def pv_used(n):
            j, h = ORDER[n]
            return (pv_done, j * (N_HEADS - 1) + h + 1) if h < N_HEADS - 1 else (ready(("o", j)), filled(("o", j)))

        def norm_rows(part, t):
            n = tile_rows(t)
            q3 = q_rows[0:n, t, :].rearrange("p (h d) -> p h d", d=HD)
            if part == "q":
                return q3[:, 0:8, :], 0, 8, 0, q3[:, 0:8, :]
            if part == "k":
                k3 = kv_rows[0:n, t, 0:KV_W].rearrange("p (h d) -> p h d", d=HD)
                return k3, 8, 4, 1, k3
            return q3[:, 12:13, :], 12, 1, 2, q3[:, 8:13, :]

        def per_batch(x, r):
            return bcast(x[:, :, 16 + 2 * r:18 + 2 * r].rearrange("p g b -> p b g"), 3, DV)

        def counter():
            counts = {}

            def turn(sem):
                counts[sem.num] = counts.get(sem.num, 0) + 1
                return counts[sem.num]
            return turn

        def release(what, key):
            if what == "bank_ready":
                return ready(key), filled(key)
            if what == "bank_free":
                return free(key), emptied(key)
            return {"squares_added": squares_added, "index_added": index_added, "gnorm_done": gnorm_done}[what], key

        def layers(e, body):
            with e.Fori(0, depth) as layer:
                body(layer)
                if e is not nc.sync:
                    e.sem_inc(arrived, 1)
                    e.wait_ge(opened_layer, 1)
                    e.sem_inc(passed, 1)

        def of_layer(name, layer):
            return A[name][bass.ds(layer, 1)]

        HEAD_TILE = [(h // 4 * 2 + h % 2, h % 4 // 2) for h in range(N_HEADS)]
        ORDER = plan.attn_order
        last_gtb = max(plan.groups[max(p for p, x in enumerate(PANELS) if x[0] == "gtb")])
        misc_panel = next(p for p, x in enumerate(PANELS) if x[0] == "misc")
        q_panels = [p for p, x in enumerate(PANELS) if x[0] == "q"]
        k_panels = [p for p, x in enumerate(PANELS) if x[0] == "k"]
        gv_panels = [p for p, x in enumerate(PANELS) if x[0] == "gv"]
        gtb_panels = [p for p, x in enumerate(PANELS) if x[0] == "gtb"]
        gate_panel = [min(p for p, x in enumerate(PANELS) if x[0] == k) for k in ("gta", "gtb")]
        gate_group = {(x[0], x[1]): ("g", plan.groups[p][0]) for p, x in enumerate(PANELS) if x[0] in ("gta", "gtb")}
        gqk_group = {(x[0], x[1]): plan.groups[p][0] for p, x in enumerate(PANELS) if x[0] in ("gq", "gk")}
        plan_src, pool_no, gated_no = {}, {}, {}
        for key in plan.split_use:
            if key[0] == "norm" and key[2] % 2:
                pool_no[key] = len(pool_no) + 1
            elif key[0] in ("norm", "merge"):
                plan_src[key] = len(plan_src) + 1
        for key in plan.gate_tmp_use:
            if key[0] in ("gr", "gate"):
                gated_no[key] = len(gated_no) + 1
        score_cols = {1: (0, 2 * P), 2: (2 * P, 5 * P), 3: (5 * P, 9 * P)}
        ident = const("ident")

        block = ctx.enter_context(nc.Block())

        @block.sync
        def _(e):
            e.dma_start(cst[:], A["consts"][:, 0:KEPT_W]).then_inc(x_loaded, 16)
            e.dma_start(repeat_f[:], A["consts"][:, KEPT_W:CONST_W]).then_inc(x_loaded, 16)
            for t in range(NTILE):
                src = A["x_prompt"][0, t * P:(t + 1) * P, :] if t < 4 else A["x_sample"].rearrange("b s d -> (b s) d")
                e.dma_start(x_rows[0:tile_rows(t), t, :], src).then_inc(x_loaded, 16)
            e.dma_start(pages[:], A["page_table"].rearrange("b n -> (b n)").unsqueeze(0)).then_inc(x_loaded, 16)
            e.wait_ge(x_loaded, 16 * (3 + NTILE))

            def load_state(layer, r):
                for b2 in range(2):
                    for h2 in range(2):
                        src = of_layer("state_gla", layer)[:, 2 * r + b2, h2:GH:2].rearrange("a g k v -> k (a g) v")
                        e.dma_start(s_state[h2 * DK:(h2 + 1) * DK, r % 2, b2, :, :],
                                    src).then_inc(s_state_ready[r % 2], 16)

            def body(layer):
                def store(dst, src, sig):
                    e.dma_start(dst, src).then_inc(sig, 16)

                def load_panel(p):
                    if p >= RAW_RING:
                        e.wait_ge(w_lo_done, p - RAW_RING + 1)
                    for name, row, nk, col, w, place in PANELS[p][2]:
                        src = of_layer(name, layer)[:, row:row + nk * P, col:col + w].rearrange(
                            "a (k p) n -> p (a k) n", p=P)
                        if w == P:
                            dst = w_raw[:, p % RAW_RING, place:place + nk * P].rearrange("p (k n) -> p k n", n=P)
                        else:
                            dst = w_raw[:, p % RAW_RING, :].rearrange("p (k n) -> p k n", n=P)[:, :, place:place + w]
                        e.dma_start(dst, src).then_inc(raw_ready[p % RAW_RING], 16)

                def page(b, n):
                    i = b * N_PAGES + n
                    return e.value_load(pages[0:1, i:i + 1], min_val=0, max_val=N_POOL - 1)

                def load_pages(b, name, dst, sem):
                    for n in range(N_PAGES):
                        r = page(b, n)
                        src = A[name].rearrange("l n s h d -> (l n) s (h d)")[bass.ds(layer * N_POOL + r, 1)]
                        e.dma_start(dst[:, b % 4, n, :], src.rearrange("a s f -> (a s) f")).then_inc(sem[b % 4], 16)

                for n, name in ((0, "norm1_g"), (1, "norm2_g")):
                    e.dma_start(gain_rows[n * KD:(n + 1) * KD, :],
                                of_layer(name, layer).rearrange("a (k p) -> (a k) p", p=P)).then_inc(small_ready, 16)
                e.dma_start(gain_rows[2 * KD:2 * KD + 1, :], of_layer("gla_onorm_g", layer)).then_inc(small_ready, 16)
                for n, name in enumerate(("q_norm_g", "k_norm_g", "kidx_norm_g")):
                    row = of_layer(name, layer)
                    e.dma_start(qk_g[:, n, :],
                                row.partition_broadcast(P).rearrange("p a n -> p (a n)")).then_inc(small_ready, 16)
                e.dma_start(wa2[:],
                            of_layer("gla_wa2", layer).rearrange("a r n -> (a r) n")).then_inc(small_ready, 16)
                e.dma_start(ba[:], of_layer("gla_ba", layer)).then_inc(small_ready, 16)
                for p in range(RAW_RING):
                    load_panel(p)
                for step in plan.steps:
                    kind = step[0]
                    if kind == "panel" and step[1] + RAW_RING < N_PANELS:
                        load_panel(step[1] + RAW_RING)
                    if kind == "qkT":
                        t = step[1]
                        n = tile_rows(t)
                        e.wait_ge(rows_done, t + 1)
                        for name, src in (("k", kv_rows[0:n, t, 0:KV_W]), ("v", kv_rows[0:n, t, KV_W:2 * KV_W]),
                                          ("kidx", q_rows[0:n, t, 12 * HD:13 * HD])):
                            if t < 4:
                                dst = of_layer(f"new_{name}_prompt", layer)[:, 0, t * P:(t + 1) * P]
                                dst = dst.rearrange("a s h d -> (a s) (h d)") if name != "kidx" else \
                                    dst.rearrange("a s d -> (a s) d")
                            else:
                                dst = of_layer(f"new_{name}_sample", layer)
                                dst = dst.rearrange("a b s h d -> (a b s) (h d)") if name != "kidx" else \
                                    dst.rearrange("a b s d -> (a b s) d")
                            e.dma_start(dst, src).then_inc(stored, 16)
                    if kind == "qkT" and step[1] == NTILE - 1:
                        e.wait_ge(stored, 16 * 3 * NTILE)
                        e.wait_ge(ready(("ki", 4)), filled(("ki", 4)))
                        for b in range(DEC_BATCH):
                            for n in range(N_PAGES):
                                r = page(b, n)
                                src = A["cache_kidx"].rearrange("l n s d -> (l n) s d")[
                                    bass.ds(layer * N_POOL + r, 1)].rearrange("a s d -> (a s) d")
                                e.dma_start(kidx[:, b, n, :], src).then_inc(kidx_ready, 16)
                    if kind == "intra" and step[1] == 3:
                        for r in range(2):
                            load_state(layer, r)
                    if kind == "intra" and step[1] == 4:
                        e.wait_ge(free(("kv", N_CHUNK - 1)), emptied(("kv", N_CHUNK - 1)))
                        for h2 in range(2):
                            dst = of_layer("new_gla_prompt", layer)[:, 0, h2:GH:2].rearrange("a g k v -> k (a g) v")
                            e.dma_start(dst, state[h2 * DK:(h2 + 1) * DK, :, :]).then_inc(state_stored, 16)
                    if kind == "sround":
                        r = step[1]
                        e.wait_ge(s_out_done, r + 1)
                        for b2 in range(2):
                            for h2 in range(2):
                                dst = of_layer("new_gla_sample", layer)[:, 2 * r + b2, h2:GH:2].rearrange(
                                    "a g k v -> k (a g) v")
                                e.dma_start(dst,
                                            s_state[h2 * DK:(h2 + 1) * DK, r % 2, b2, :, :]).then_inc(s_stored, 16)
                        if r < 2:
                            e.wait_ge(s_stored, 16 * 4 * (r + 1))
                            load_state(layer, r + 2)
                    if kind == "sgla_out":
                        e.wait_ge(ready(("oO", 4)), filled(("oO", 4)))
                        e.wait_ge(state_stored, 16 * 2)
                        e.wait_ge(s_stored, 16 * 2 * DEC_BATCH)
                        for b in range(4):
                            load_pages(b, "cache_k", k_pages, k_ready)
                            load_pages(b, "cache_v", v_pages, v_ready)
                    if kind == "kcT" and step[1] < 4:
                        b = step[1]
                        e.wait_ge(ready(("kcT", b)), filled(("kcT", b)))
                        load_pages(b + 4, "cache_k", k_pages, k_ready)
                    if kind == "spv" and step[1] < 2:
                        i = step[1]
                        e.wait_ge(kc_free, 2 * i + 2)
                        for b in (2 * i + 4, 2 * i + 5):
                            load_pages(b, "cache_v", v_pages, v_ready)

                e.wait_ge(stored, 16 * 3 * NTILE)
                e.wait_ge(s_stored, 16 * 2 * DEC_BATCH)
                e.wait_ge(state_stored, 16 * 2)
                e.wait_ge(arrived, 4)
                e.sem_clear(layer_sems)
                e.sem_inc(opened_layer, 1)
                e.wait_ge(passed, 4)
                e.sem_clear(range(opened_layer.num, passed.num + 1))

            layers(e, body)
            for t in range(NTILE):
                e.wait_ge(y_ready, 2 * (t + 1))
                dst = A["y_prompt"][0, t * P:(t + 1) * P, :] if t < 4 else A["y_sample"].rearrange("b s d -> (b s) d")
                e.dma_start(dst, x_rows[0:tile_rows(t), t, :]).then_inc(y_stored, 16)
            e.wait_ge(y_stored, 16 * NTILE)

        @block.tensor
        def _(e):
            e.wait_ge(x_loaded, 16 * (3 + NTILE))
            for kt in range(KD):
                if kt >= 2:
                    e.wait_ge(x_filled, kt - 1)
                for t in range(NTILE):
                    n = tile_rows(t)
                    out = aux[:, 2 * (kt % 2) + t // 4, (t % 4) * P:(t % 4) * P + n]
                    ins = e.transpose(out, x_rows[0:n, t, kt * P:(kt + 1) * P], ident[0:n, 0:n])
                ins.then_inc(x_turned, 1)
            e.wait_ge(x_filled, KD)

            def body(layer):
                def part(p, i):
                    kind, idx, parts = PANELS[p]
                    slot_w = p % 2
                    if i == 0:
                        e.wait_ge(w_lo_done, p + 1)
                    n, first_k, last_k = 0, 0, KD - 1
                    if kind == "oab":
                        n, first_k, last_k = i // 4, i // 4 * 4, i // 4 * 4 + 3
                    elif kind == "down":
                        last_k = FF_PARTS[idx[0]] - 1
                        if i > last_k:
                            return
                    g = plan.groups[p][n]
                    hi, lo = (mid_hi, mid_lo) if kind in ("o", "down") else (in_hi, in_lo)
                    if i == first_k and g >= 2:
                        e.wait_ge(free(("g", g - 2)), emptied(("g", g - 2)))
                    if kind == "q" and idx == 0:
                        e.wait_ge(split_lo, plan.split_use["norm", 1, i] + 1)
                    if kind == "oab" and idx == 0:
                        e.wait_ge(split_lo, plan.split_use["mix", i] + 1)
                    if kind == "o" and idx == 0:
                        e.wait_ge(split_lo, plan.split_use["merge", i] + 1)
                    if kind == "gate" and idx == (0, 0):
                        e.wait_ge(split_lo, plan.split_use["norm", 2, i] + 1)
                    if kind == "down" and idx[1] == 0:
                        e.wait_ge(split_lo, plan.split_use["ff", (idx[0], sum(FF_PARTS[:idx[0]]) + i)] + 1)
                    for w, parts_in in ((w_hi, (hi, lo)), (w_lo, (hi,))):
                        for a in parts_in:
                            for h in range(2):
                                first = i == first_k and w is w_hi and a is hi
                                last = i == last_k and w is w_lo
                                ins = e.matmul(slot(g)[:, h, :], w[:, slot_w, i * P:(i + 1) * P],
                                               a[:, i, h * HALF:(h + 1) * HALF], start=first, stop=last)
                    if i == last_k:
                        ins.then_inc(ready(("g", g)), 1)

                def logits(n):
                    j, h = ORDER[n]
                    L = (j + 1) * P
                    tile, half = HEAD_TILE[h]
                    rows = slice(64 * half, 64 * half + 64)
                    key = ("log", j, h)
                    e.wait_ge(free(key), opened(key))
                    out = aux[:, uses[key][0], 0:L]
                    mask = tri_b[:] if j == 0 else mask_b[:, j - 1, 0:L]
                    if n == 0:
                        e.wait_ge(masks_done, 4)
                    e.matmul(out, ident_b[:], mask, start=True, stop=False)
                    ins = e.matmul(out, q_t[rows, tile, j * P:(j + 1) * P], k_t[rows, h // 4, 0:L],
                                   start=False, stop=True)
                    ins.then_inc(ready(key), 1)

                for step in plan.steps:
                    kind = step[0]
                    if kind == "part":
                        part(step[1], step[2])
                    elif kind == "gains":
                        e.wait_ge(small_ready, 16 * SMALL_LOADS)
                        e.wait_ge(free(("gains",)), opened(("gains",)))
                        ins = e.transpose(aux[:, 2, 0:2 * KD + 1], gain_rows[:], ident[0:2 * KD + 1, 0:2 * KD + 1])
                        ins.then_inc(ready(("gains",)), 1)
                    elif kind == "stat" and step[2] == KD - 1:
                        norm = step[1]
                        squares = gate_tmp[:, plan.gate_tmp_use["squares", norm] % 2, :]
                        e.wait_ge(squares_added, norm * (KD - 1))
                        for h in range(2):
                            e.wait_ge(free(("stat", norm, h)), opened(("stat", norm, h)))
                            e.matmul(aux[:, h, 0:HALF], ones[:], squares[:, h * HALF:(h + 1) * HALF],
                                     start=True, stop=True).then_inc(ready(("stat", norm, h)), 1)
                    elif kind == "row":
                        p = step[1]
                        use = plan.stage_use["row", p]
                        e.wait_ge(staged, use + 1)
                        e.wait_ge(free(("rowX", p)), opened(("rowX", p)))
                        bx, by = uses["rowX", p][0], uses["rowY", p][0]
                        for t in range(4):
                            ins = e.transpose(aux[:, bx, t * P:(t + 1) * P], stage[:, use % 2, t * P:(t + 1) * P], ident)
                        ins.then_inc(ready(("rowX", p)), 1)
                        e.wait_ge(free(("rowY", p)), opened(("rowY", p)))
                        ins = e.transpose(aux[0:NS, by, 0:P], stage[:, use % 2, SEQ:NT], ident)
                        ins.then_inc(ready(("rowY", p)), 1)
                    elif kind == "z":
                        e.wait_ge(small_ready, 16 * SMALL_LOADS)
                        e.wait_ge(ga_done, 1)
                        for i in range(3):
                            e.wait_ge(free(("z", i)), opened(("z", i)))
                            for t in range(2 * i, min(2 * i + 2, NTILE)):
                                n = tile_rows(t)
                                out = aux[0:n, uses["z", i][0], (t % 2) * GK_W:(t % 2 + 1) * GK_W]
                                e.matmul(out, ga_t[:, token_slice(t)], wa2[:], start=True, stop=False)
                                ins = e.matmul(out, ones[0:1, 0:n], ba[:], start=False, stop=True)
                            ins.then_inc(ready(("z", i)), 1)
                    elif kind == "decay":
                        for i in range(3):
                            e.wait_ge(free(("z", i)), emptied(("z", i)))
                        for hp in range(2):
                            e.wait_ge(free(("b", hp)), opened(("b", hp)))
                            for t in range(4):
                                ins = e.matmul(aux[:, hp, t * P:(t + 1) * P], la[:, t, hp * P:(hp + 1) * P],
                                               const("chunk_sum"), start=True, stop=True)
                            ins.then_inc(ready(("b", hp)), 1)
                        e.wait_ge(free(("b", 2)), opened(("b", 2)))
                        for hp in range(2):
                            ins = e.matmul(aux[:, 2, hp * NS:(hp + 1) * NS], la[0:NS, 4, hp * P:(hp + 1) * P],
                                           const("sample_sum", NS), start=True, stop=True)
                        ins.then_inc(ready(("b", 2)), 1)
                    elif kind == "qkT":
                        t = step[1]
                        n = tile_rows(t)
                        idn = ident[0:n, 0:n]
                        e.wait_ge(rows_done, t + 1)
                        e.wait_ge(free(("q", t)), opened(("q", t)))
                        for m in range(4):
                            ins = e.transpose(aux[:, 0, m * P:m * P + n], q_rows[0:n, t, m * P:(m + 1) * P], idn)
                        ins.then_inc(ready(("q", t)), 1)
                        e.wait_ge(free(("ik", t)), opened(("ik", t)))
                        for m in range(2):
                            e.transpose(aux[:, 1, m * P:m * P + n], q_rows[0:n, t, (4 + m) * P:(5 + m) * P], idn)
                        for m in range(2):
                            ins = e.transpose(aux[:, 1, (2 + m) * P:(2 + m) * P + n],
                                              kv_rows[0:n, t, m * P:(m + 1) * P], idn)
                        ins.then_inc(ready(("ik", t)), 1)
                        e.wait_ge(free(("ki", t)), opened(("ki", t)))
                        e.transpose(aux[0:ID, 3, 0:n], q_rows[0:n, t, 12 * HD:13 * HD], idn)
                        ins = e.matmul(aux[ID:2 * ID, 3, 0:n], q_rows[0:n, t, 12 * HD:13 * HD], idn,
                                       start=True, stop=True)
                        ins.then_inc(ready(("ki", t)), 1)
                    elif kind == "index":
                        j = step[1]
                        L = (j + 1) * P
                        e.wait_ge(free(("ik", 4)), emptied(("ik", 4)))
                        e.wait_ge(free(("ki", 4)), emptied(("ki", 4)))
                        for h in range(IDX_HEADS):
                            rows = slice(64 * (h % 2), 64 * (h % 2) + 64)
                            key = ("index", j, h)
                            e.wait_ge(free(key), opened(key))
                            ins = e.matmul(aux[:, uses[key][0], 0:L], qi_t[rows, h // 2, j * P:(j + 1) * P],
                                           ki_t[rows, 0:L], start=True, stop=True)
                            ins.then_inc(ready(key), 1)
                    elif kind == "qiz":
                        for g in range(2):
                            e.wait_ge(free(("wi", g)), opened(("wi", g)))
                            bank = uses["wi", g][0]
                            ins = e.matmul(aux[:, bank, 0:IDX_HEADS],
                                           const("spread", NS)[:, g * P:(g + 1) * P], wi_rows[0:NS, 4, :],
                                           start=True, stop=True)
                            ins.then_inc(ready(("wi", g)), 1)
                    elif kind == "kidx":
                        g = step[1]
                        e.wait_ge(kidx_ready, 16 * DEC_BATCH * N_PAGES)
                        e.wait_ge(qiz_done, 1)
                        for u in range(2):
                            key = ("kidxT", 2 * g + u)
                            e.wait_ge(free(key), opened(key))
                            for k in range(4):
                                b = 4 * g + 2 * u + k // 2
                                ins = e.transpose(aux[0:ID, 3, k * P:(k + 1) * P], kidx[:, b, k % 2, :], ident)
                            ins.then_inc(ready(key), 1)
                        for u in range(2):
                            e.wait_ge(free(("kidxT", 2 * g + u)), emptied(("kidxT", 2 * g + u)))
                            if u == 0:
                                e.wait_ge(free(("sscore", g)), opened(("sscore", g)))
                            for k in range(2):
                                b = 4 * g + 2 * u + k
                                out = aux[32 * (b % 4):32 * (b % 4) + 32, 2, :]
                                e.matmul(out[:, 0:PAST], qiz[:, b, :], kidx_t[:, u, k * PAST:(k + 1) * PAST],
                                         start=True, stop=True)
                                ins = e.matmul(out[:, PAST:NEW_KEYS], qiz[:, b, :], ki_t[0:ID, SEQ:NT],
                                               start=True, stop=True)
                        ins.then_inc(ready(("sscore", g)), 1)
                    elif kind == "sindex":
                        e.wait_ge(free(("ssum",)), opened(("ssum",)))
                        for g in range(2):
                            e.wait_ge(free(("sscore", g)), emptied(("sscore", g)))
                            ins = e.matmul(aux[0:NS, 3, 0:NEW_KEYS], const("gather")[:, g * NS:(g + 1) * NS],
                                           s_heads[:, g, :], start=(g == 0), stop=(g == 1))
                        ins.then_inc(ready(("ssum",)), 1)
                    elif kind == "kT":
                        t = step[1]
                        n = tile_rows(t)
                        tok = token_slice(t)
                        e.wait_ge(gqk_done, 2)
                        e.wait_ge(free(("rowY", gv_panels[-1])), emptied(("rowY", gv_panels[-1])))
                        e.wait_ge(free(("kT", t)), opened(("kT", t)))
                        for hp in range(2):
                            ins = e.transpose(aux[0:n, 2, hp * P:(hp + 1) * P], gk[:, hp, tok], ident)
                        ins.then_inc(ready(("kT", t)), 1)
                    elif kind == "intra":
                        t = step[1]
                        n = tile_rows(t)
                        tok = token_slice(t)
                        for par, key in enumerate((("inE", t), ("inO", t))):
                            e.wait_ge(free(key), opened(key))
                            rows = slice(64 * par, 64 * par + 64)
                            for hp in range(2):
                                ins = e.matmul(aux[0:n, uses[key][0], hp * P:hp * P + n], gk[rows, hp, tok],
                                               gq[rows, hp, tok], start=True, stop=True)
                            ins.then_inc(ready(key), 1)
                    elif kind == "intra_out":
                        t = step[1]
                        n = tile_rows(t)
                        for par, key in enumerate((("oE", t), ("oO", t))):
                            e.wait_ge(free(key), opened(key))
                            e.wait_ge(free((("inE", t), ("inO", t))[par]), emptied((("inE", t), ("inO", t))[par]))
                            for hp in range(2):
                                h = 2 * hp + par
                                ins = e.matmul(aux[:, par, hp * P:hp * P + n], gv_rows[0:n, t, h * DV:(h + 1) * DV],
                                               g_attn[0:n, h, 0:n], start=(hp == 0), stop=False,
                                               skip_group_check=True)
                        if t == 4:
                            ins.then_inc(sample_intra, 1)
                    elif kind == "chunk":
                        c = step[1]
                        t = c // 4
                        if c > 0:
                            e.wait_ge(state_in_done, c)
                            for par in range(2):
                                rows = slice(64 * par, 64 * par + 64)
                                for hp in range(2):
                                    ins = e.matmul(aux[:, par, hp * P + c % 4 * CHUNK:hp * P + (c % 4 + 1) * CHUNK],
                                                   state_in[rows, hp, :], gq[rows, hp, c * CHUNK:(c + 1) * CHUNK],
                                                   start=False, stop=(c % 4 == 3), skip_group_check=True)
                                if c % 4 == 3:
                                    ins.then_inc(ready((("oE", t), ("oO", t))[par]), 1)
                        e.wait_ge(free(("kT", t)), emptied(("kT", t)))
                        e.wait_ge(free(("kv", c)), opened(("kv", c)))
                        rows = slice(c % 4 * CHUNK, (c % 4 + 1) * CHUNK)
                        for h in range(GH):
                            ins = e.matmul(aux[64 * (h % 2):64 * (h % 2) + 64, 2, h // 2 * DV:(h // 2 + 1) * DV],
                                           gk_rows[rows, t % 2, h * DK:(h + 1) * DK],
                                           gv_rows[rows, t, h * DV:(h + 1) * DV], start=True, stop=True,
                                           tile_position=(c % 4 * CHUNK, 64 * (h % 2)))
                        ins.then_inc(ready(("kv", c)), 1)
                    elif kind == "sround":
                        r = step[1]
                        e.wait_ge(s_in_done, r + 1)
                        if r == 0:
                            e.wait_ge(sample_intra, 1)
                        for par in range(2):
                            rows = slice(64 * par, 64 * par + 64)
                            for b2 in range(2):
                                for hp in range(2):
                                    b = 2 * r + b2
                                    cols = slice(hp * P + b * DEC_SEQ, hp * P + (b + 1) * DEC_SEQ)
                                    ins = e.matmul(aux[:, par, cols], s_state_in[rows, b2, hp, :],
                                                   gq[rows, hp, SEQ + b * DEC_SEQ:SEQ + (b + 1) * DEC_SEQ],
                                                   start=False, stop=(r == 3), skip_group_check=True)
                            if r == 3:
                                ins.then_inc(ready((("oE", 4), ("oO", 4))[par]), 1)
                        e.wait_ge(free(("skv", r)), opened(("skv", r)))
                        for b2 in range(2):
                            for h in range(GH):
                                c0 = (b2 * 2 + h // 2) * DV
                                ins = e.matmul(aux[64 * (h % 2):64 * (h % 2) + 64, 2, c0:c0 + DV],
                                               gk_one[:, b2, h * DK:(h + 1) * DK], gv_rows[0:NS, 4, h * DV:(h + 1) * DV],
                                               start=True, stop=True)
                        ins.then_inc(ready(("skv", r)), 1)
                    elif kind == "gnorm":
                        h = step[1]
                        use = plan.stage_use["gn", h]
                        e.wait_ge(staged, use + 1)
                        for k in range(2):
                            e.wait_ge(free(("gn", h, k)), opened(("gn", h, k)))
                            ins = e.matmul(aux[:, k, 0:HALF], ones[:], stage[:, use % 2, k * HALF:(k + 1) * HALF],
                                           start=True, stop=True)
                            ins.then_inc(ready(("gn", h, k)), 1)
                    elif kind == "kcT":
                        b = step[1]
                        e.wait_ge(k_ready[b % 4], 16 * N_PAGES * (b // 4 + 1))
                        e.wait_ge(free(("kcT", b)), opened(("kcT", b)))
                        for pair in range(2):
                            for n in range(N_PAGES):
                                c0 = pair * PAST + n * PAGE
                                ins = e.transpose(aux[:, 1 + b % 2, c0:c0 + PAGE],
                                                  k_pages[:, b % 4, n, pair * P:(pair + 1) * P], ident)
                        ins.then_inc(ready(("kcT", b)), 1)
                    elif kind == "slog":
                        b = step[1]
                        i = b // 2
                        if b == 0:
                            e.wait_ge(masks_done, 4)
                            e.wait_ge(qz_done, 1)
                        if b % 2 == 0:
                            e.wait_ge(free(("slog", i)), opened(("slog", i)))
                        out = aux[64 * (b % 2):64 * (b % 2) + 64, uses["slog", i][0], :]
                        e.matmul(out[:, 0:NEW_KEYS], repeat_b[:, b, :], mask_s[:], start=True, stop=False,
                                 skip_group_check=True)
                        e.wait_ge(free(("kcT", b)), emptied(("kcT", b)))
                        for pair in range(2):
                            e.matmul(out[:, 0:PAST], qz[:, b, pair, :], k_past[:, b % 2, pair, :],
                                     start=False, stop=False, skip_group_check=True)
                            ins = e.matmul(out[:, PAST:NEW_KEYS], qz[:, b, pair, :], k_t[:, pair, SEQ:NT],
                                           start=False, stop=(pair == 1), skip_group_check=True)
                        if b % 2 == 1:
                            ins.then_inc(ready(("slog", i)), 1)
                        else:
                            ins.then_inc(k_past_used, 1)
                    elif kind == "spT":
                        i = step[1]
                        e.wait_ge(p_scaled, i + 1)
                        e.wait_ge(free(("spT", i)), opened(("spT", i)))
                        for s in range(2):
                            e.transpose(aux[:, 2, s * P:(s + 1) * P], p_t[:, i % 2, s * P:(s + 1) * P], ident)
                        ins = e.transpose(aux[0:NS, 2, 2 * P:3 * P], p_t[:, i % 2, PAST:NEW_KEYS], ident)
                        ins.then_inc(ready(("spT", i)), 1)
                    elif kind == "spv":
                        i = step[1]
                        if i == 0:
                            e.wait_ge(free(("so",)), opened(("so",)))
                        e.wait_ge(free(("spT", i)), emptied(("spT", i)))
                        for b in (2 * i, 2 * i + 1):
                            e.wait_ge(v_ready[b % 4], 16 * N_PAGES * (b // 4 + 1))
                            for pair in range(2):
                                out = aux[:, 3, (b * 2 + pair) * 32:(b * 2 + pair + 1) * 32]
                                cols = slice(64 * (b % 2) + 32 * pair, 64 * (b % 2) + 32 * pair + 32)
                                for s in range(2):
                                    e.matmul(out, v_pages[:, b % 4, s, pair * P:(pair + 1) * P],
                                             pT_t[:, i % 2, s, cols], start=(s == 0), stop=False)
                                ins = e.matmul(out, kv_rows[0:NS, 4, KV_W + pair * P:KV_W + (pair + 1) * P],
                                               pT_t[0:NS, i % 2, 2, cols], start=False, stop=True)
                            if b == DEC_BATCH - 1:
                                ins.then_inc(ready(("so",)), 1)
                            else:
                                ins.then_inc(kc_free, 1)
                    elif kind == "attn":
                        _, j, h = step
                        n = j * N_HEADS + h
                        if n == 0:
                            logits(0)
                        if n + 1 < len(ORDER):
                            logits(n + 1)
                        e.wait_ge(free(("log", j, h)), emptied(("log", j, h)))
                        e.wait_ge(free(("pT", j, h)), opened(("pT", j, h)))
                        for s in range(j + 1):
                            ins = e.transpose(aux[:, 2, s * P:(s + 1) * P], p_t[:, n % 2, s * P:(s + 1) * P], ident)
                        ins.then_inc(ready(("pT", j, h)), 1)
                    elif kind == "attn_pv":
                        _, j, h = step
                        n = j * N_HEADS + h
                        if h == 0:
                            e.wait_ge(free(("o", j)), opened(("o", j)))
                        e.wait_ge(free(("pT", j, h)), emptied(("pT", j, h)))
                        kv = h // 2
                        for s in range(j + 1):
                            ins = e.matmul(aux[:, 3, h * HD:(h + 1) * HD], pT_t[:, n % 2, s, :],
                                           kv_rows[:, s, KV_W + kv * HD:KV_W + (kv + 1) * HD],
                                           start=(s == 0), stop=(s == j))
                        if h < N_HEADS - 1:
                            ins.then_inc(pv_done, 1)
                        else:
                            ins.then_inc(ready(("o", j)), 1)
                    elif kind == "attn_t":
                        j = step[1]
                        e.wait_ge(free(("o", j)), emptied(("o", j)))
                        e.wait_ge(free(("oT", j)), opened(("oT", j)))
                        for m in range(4):
                            ins = e.transpose(aux[:, 2, m * P:(m + 1) * P], o_rows[:, m * P:(m + 1) * P], ident)
                        ins.then_inc(ready(("oT", j)), 1)

            layers(e, body)
            for t in range(NTILE):
                if t >= 2:
                    e.wait_ge(y_ready, 2 * (t - 1))
                n = tile_rows(t)
                for kt in range(KD):
                    ins = e.transpose(aux[0:n, 2 * (t % 2) + kt // 4, kt % 4 * P:(kt % 4 + 1) * P],
                                      x_t[:, kt, token_slice(t)], ident)
                ins.then_inc(y_turned, 1)

        @block.gpsimd
        def _(e):
            def body(layer):
                def lower(p):
                    n = FF_PARTS[PANELS[p][1][0]] * P if PANELS[p][0] == "down" else KD * P
                    e.wait_ge(w_hi_done, p + 1)
                    if p >= 2:
                        g = ("g", plan.groups[p - 2][-1])
                        e.wait_ge(ready(g), filled(g))
                    e.tensor_tensor(w_lo[:, p % 2, 0:n], w_raw[:, p % RAW_RING, 0:n],
                                    w_hi[:, p % 2, 0:n].bitcast(F32), ALU.subtract).then_inc(w_lo_done, 1)

                e.memset(g_attn[:], 0.0)
                for step in plan.steps:
                    kind = step[0]
                    if kind in ("weights", "weights_lower"):
                        lower(step[1])
                    elif kind == "norm":
                        norm = step[1]
                        e.wait_ge(rstd_done, norm)
                        for kt in range(1, KD, 2):
                            e.tensor_tensor(normed[:, kt, :], x_t[:, kt, :], rstd[:], ALU.mult).then_inc(pool_src, 1)
                    elif kind == "gexp":
                        e.wait_ge(exps_done, 1)
                        for x, y, decay in ((gk, "gk", d_t), (gq, "gq", e_t)):
                            for i in range(2):
                                e.wait_ge(free(("g", gqk_group[y, i])), emptied(("g", gqk_group[y, i])))
                            e.tensor_tensor(x[:], x[:], decay[:], ALU.mult).then_inc(gqk_done, 1)
                    elif kind == "sin":
                        r = step[1]
                        st = s_state[:, r % 2, :, :, :]
                        e.wait_ge(s_state_ready[r % 2], 16 * 4 * (r // 2 + 1))
                        if r:
                            e.wait_ge(ready(("skv", r - 1)), filled(("skv", r - 1)))
                        e.tensor_tensor(s_state_in[:], st, per_batch(e_ref, r), ALU.mult)
                        if r == 0:
                            e.wait_ge(free(("kT", 4)), emptied(("kT", 4)))
                        e.tensor_tensor(gk_one[:], bcast(gk_rows[0:NS, 0, :], 1, 2),
                                        bcast(const("batch_rows", NS)[:, 2 * r:2 * r + 2], 2, GK_W),
                                        ALU.mult).then_inc(s_in_done, 1)
                        e.tensor_tensor(st, st, per_batch(e_end, r), ALU.mult).then_inc(s_decayed, 1)
                e.wait_ge(w_lo_done, N_PANELS)

            layers(e, body)

        @block.scalar
        def _(e):
            e.wait_ge(x_filled, KD)

            def body(layer):
                def copy_w(p):
                    e.wait_ge(raw_ready[p % RAW_RING], 16 * RAW_READY[p])
                    if p >= 2:
                        e.wait_ge(ready(("g", plan.groups[p - 2][-1])), filled(("g", plan.groups[p - 2][-1])))
                    n = sum(part[2] for part in PANELS[p][2]) * P if PANELS[p][0] != "misc" else KD * P
                    e.activation(w_hi[:, p % 2, 0:n], w_raw[:, p % RAW_RING, 0:n], ACT.Copy).then_inc(w_hi_done, 1)

                def exp_head(n):
                    j, h = ORDER[n]
                    L = (j + 1) * P
                    key = ("log", j, h)
                    e.wait_ge(max_done, 4 + n + 1)
                    if n >= 2:
                        e.wait_ge(ready(("pT",) + ORDER[n - 2]), filled(("pT",) + ORDER[n - 2]))
                    e.activation(p_t[:, n % 2, 0:L], aux[:, uses[key][0], 0:L], ACT.Exp,
                                 bias=neg_max[:, j % 2, h:h + 1], accum_out=p_sum[:, j % 2, h:h + 1]).then_inc(free(key), 1)

                def stage_slot(key):
                    use = plan.stage_use[key]
                    if use >= 2:
                        e.wait_ge(*release(*plan.stage_release[use - 2]))
                    return stage[:, use % 2, :]

                def gate_slot(key):
                    use = plan.gate_tmp_use[key]
                    if use >= 2:
                        e.wait_ge(*release(*plan.gate_tmp_release[use - 2]))
                    return gate_tmp[:, use % 2, :]

                for step in plan.steps:
                    kind = step[0]
                    if step in (("stat", 1, 0), ("gnorm", 0), ("stat", 2, 0)):
                        e.preload_act_table_set("natural_log_exp_and_others")
                    if kind == "panel":
                        kind_p, idx, _ = PANELS[step[1]]
                        if kind_p == "oab":
                            for gate, gates in ((gate_b, "gtb"), (gate_a, "gta")):
                                e.wait_ge(free(gate_group[gates, idx]), emptied(gate_group[gates, idx]))
                                e.activation(gate[:, idx, :], gate[:, idx, :], ACT.Sigmoid).then_inc(gates_done, 1)
                    elif kind in ("weights", "weights_upper"):
                        copy_w(step[1])
                    elif kind == "post":
                        p = step[1]
                        kind_p, idx, _ = PANELS[p]
                        g = plan.groups[p][0]
                        key = ("g", g)
                        src = slot(g)
                        if kind_p in STAGED:
                            dst = stage_slot(("row", p))
                            e.wait_ge(ready(key), filled(key))
                            if kind_p == "misc":
                                e.activation(halves(ga_t[:]), src[0:RANK], ACT.Copy).then_inc(ga_done, 1)
                            e.activation(halves(dst), src, ACT.Copy).then_inc(staged, 1)
                        elif kind_p == "gq":
                            e.wait_ge(ready(key), filled(key))
                            e.activation(halves(gq[:, idx, :]), src, ACT.Copy,
                                         scale=DK ** -0.5).then_inc(free(key), 1)
                        elif kind_p == "gk":
                            e.wait_ge(ready(key), filled(key))
                            e.activation(halves(gk[:, idx, :]), src, ACT.Copy).then_inc(free(key), 1)
                        elif kind_p == "gr":
                            dst = gate_slot(("gr", idx))
                            e.wait_ge(ready(key), filled(key))
                            e.activation(halves(dst), src, ACT.Sigmoid).then_inc(gated, 1)
                        elif kind_p in ("gta", "gtb"):
                            e.wait_ge(ready(key), filled(key))
                            gate = gate_a if kind_p == "gta" else gate_b
                            e.activation(halves(gate[:, idx, :]), src, ACT.Copy).then_inc(free(key), 1)
                        elif kind_p == "oab":
                            e.wait_ge(split_src, plan_src["merge", idx])
                            e.activation(mid_hi[:, idx, :], tmp[:, plan.split_use["merge", idx] % 2, :],
                                         ACT.Copy).then_inc(split_hi, 1)
                        elif kind_p == "gate":
                            dst = gate_slot(("gate", idx))
                            e.wait_ge(ready(key), filled(key))
                            e.activation(halves(dst), src, ACT.Sigmoid).then_inc(gated, 1)
                        elif kind_p == "up":
                            e.wait_ge(free(key), emptied(key))
                            part, i = idx
                            u = plan.split_use["ff", idx]
                            e.activation(mid_hi[:, i - sum(FF_PARTS[:part]), :], tmp[:, u % 2, :],
                                         ACT.Copy).then_inc(split_hi, 1)
                    elif kind == "stat":
                        _, norm, kt = step
                        dst = stage_slot(("stat", norm, kt)) if kt else gate_slot(("squares", norm))
                        if norm == 2:
                            e.wait_ge(x_added, kt + 1)
                        e.activation(dst, x_t[:, kt, :], ACT.Square).then_inc(staged if kt else squares_ready, 1)
                    elif kind == "norm":
                        norm = step[1]
                        for h in range(2):
                            key = ("stat", norm, h)
                            e.wait_ge(ready(key), filled(key))
                            e.activation(rstd[:, h * HALF:(h + 1) * HALF], aux[:, h, 0:HALF], ACT.Ln, bias=eps_t[:],
                                         scale=1.0 / D_MODEL).then_inc(free(key), 1)
                        e.wait_ge(free(("stat", norm, 1)), emptied(("stat", norm, 1)))
                        e.activation(rstd[:], rstd[:], ACT.Exp, scale=-0.5).then_inc(rstd_done, 1)
                        e.wait_ge(free(("gains",)), emptied(("gains",)))
                        for kt in range(KD):
                            src = ("norm", norm, kt)
                            e.wait_ge(*((split_src, plan_src[src]) if kt % 2 == 0 else (pool_src, pool_no[src])))
                            gain = (norm - 1) * KD + kt
                            e.activation(in_hi[:, kt, :], normed[:, kt, :], ACT.Copy,
                                         scale=gains[:, gain:gain + 1]).then_inc(split_hi, 1)
                    elif kind == "qn":
                        _, part, t = step
                        u = plan.norm_order.index((part, t))
                        n = tile_rows(t)
                        rows, first, heads, _, _ = norm_rows(part, t)
                        if t == 0:
                            last = {"q": q_panels[-1], "k": k_panels[-1], "x": misc_panel}[part]
                            for row in ("rowX", "rowY"):
                                e.wait_ge(free((row, last)), emptied((row, last)))
                        if u:
                            e.wait_ge(rows_ss, u)
                        e.activation(sq_rows[0:n, 0:heads, :], rows, ACT.Square).then_inc(rows_sq, 1)
                        e.wait_ge(rows_ss, u + 1)
                        root = sums[0:n, u % 2, 0:heads]
                        e.activation(root, root, ACT.Ln, bias=eps_t[0:n, :], scale=1.0 / HD).then_inc(rows_ln, 1)
                        e.wait_ge(rows_ln, u + 1)
                        e.activation(root, root, ACT.Exp, scale=-0.5).then_inc(rows_std, 1)
                    elif kind == "qkT":
                        t = step[1]
                        n = tile_rows(t)
                        e.wait_ge(ready(("q", t)), filled(("q", t)))
                        e.activation(q_t[:, :, token_slice(t)],
                                     aux[:, 0, :].rearrange("p (m n) -> p m n", m=4)[:, :, 0:n], ACT.Copy, scale=HD ** -0.5).then_inc(free(("q", t)), 1)
                        e.wait_ge(ready(("ki", t)), filled(("ki", t)))
                        e.activation(ki_t[:, token_slice(t)], aux[:, 3, 0:n], ACT.Copy).then_inc(free(("ki", t)), 1)
                    elif kind == "z":
                        def la_rows(i):
                            n = tile_rows(2 * i)
                            tiles = min(2, NTILE - 2 * i)
                            return la[0:n, 2 * i:2 * i + tiles, :].rearrange("p t n -> p (t n)"), n, tiles
                        for i in range(3):
                            dst, n, tiles = la_rows(i)
                            e.wait_ge(ready(("z", i)), filled(("z", i)))
                            e.activation(dst, aux[0:n, uses["z", i][0], 0:tiles * GK_W], ACT.Abs).then_inc(z_abs, 1)
                        e.wait_ge(z_abs, 3)
                        for i in range(3):
                            dst = la_rows(i)[0]
                            e.activation(dst, dst, ACT.Exp, scale=-1.0).then_inc(z_exp, 1)
                        e.wait_ge(z_exp, 3)
                        for i in range(3):
                            dst = la_rows(i)[0]
                            e.activation(dst, dst, ACT.Ln, bias=1.0).then_inc(ln_done, 1)
                    elif kind == "decay_exp":
                        e.wait_ge(decay_done, 1)
                        e.activation(e_t[:], d_t[:], ACT.Exp)
                        e.activation(d_t[:], d_t[:], ACT.Exp, scale=-1.0)
                        e.activation(e_ref[:], b_ref[:], ACT.Exp)
                        e.activation(e_end[:], b_end[:], ACT.Exp)
                        e.activation(e_add[:], e_add[:], ACT.Exp).then_inc(exps_done, 1)
                    elif kind == "index":
                        j = step[1]
                        L = (j + 1) * P
                        for h in range(IDX_HEADS):
                            key = ("index", j, h)
                            dst = gate_slot(key)
                            e.wait_ge(ready(key), filled(key))
                            e.activation(dst[:, 0:L], aux[:, uses[key][0], 0:L], ACT.Relu,
                                         scale=IDX_SCALE).then_inc(free(key), 1)
                    elif kind == "kidx":
                        g = step[1]
                        if g:
                            e.wait_ge(ready(("sscore", g - 1)), filled(("sscore", g - 1)))
                        for u in range(2):
                            key = ("kidxT", 2 * g + u)
                            e.wait_ge(ready(key), filled(key))
                            e.activation(kidx_t[:, u, :], aux[0:ID, 3, :], ACT.Copy).then_inc(free(key), 1)
                    if kind == "chunk" and step[1] < N_CHUNK - 1:
                        c = step[1]
                        e.wait_ge(free(("kv", c)), emptied(("kv", c)))
                        for hp in range(2):
                            ins = e.activation(state_in[:, hp, :], state[:, hp, :], ACT.Copy,
                                               scale=e_ref[:, hp, c + 1:c + 2])
                        ins.then_inc(state_in_done, 1)
                        for hp in range(2):
                            ins = e.activation(state_add[:, hp, :], state[:, hp, :], ACT.Copy,
                                               scale=e_end[:, hp, c + 1:c + 2])
                        ins.then_inc(decayed, 1)
                    if (kind == "chunk" and step[1] % 4 == 3) or kind == "sgla_out":
                        t = step[1] // 4 if kind == "chunk" else 4
                        n = tile_rows(t)
                        for par, key in enumerate((("oE", t), ("oO", t))):
                            e.wait_ge(ready(key), filled(key))
                            e.activation(gla_o[:, par::2, token_slice(t)],
                                         aux[:, par, 0:2 * P].rearrange("p (g n) -> p g n", g=2)[:, :, 0:n], ACT.Copy).then_inc(free(key), 1)
                    elif kind == "gnorm":
                        h = step[1]
                        dst = stage_slot(("gn", h))
                        for par in range(2):
                            e.wait_ge(free((("oE", 4), ("oO", 4))[par]), emptied((("oE", 4), ("oO", 4))[par]))
                        e.activation(dst, gla_o[:, h, :], ACT.Square).then_inc(staged, 1)
                        root = gate_slot(("gn", h))
                        for k in range(2):
                            key = ("gn", h, k)
                            e.wait_ge(ready(key), filled(key))
                            e.activation(root[:, k * HALF:(k + 1) * HALF], aux[:, k, 0:HALF], ACT.Ln, bias=eps_t[:],
                                         scale=1.0 / DV).then_inc(free(key), 1)
                        e.wait_ge(free(("gn", h, 1)), emptied(("gn", h, 1)))
                        e.activation(root, root, ACT.Exp, scale=-0.5).then_inc(gn_root, 1)
                    elif kind == "mix":
                        e.wait_ge(ready(("g", last_gtb)), filled(("g", last_gtb)))
                        if step[1] == "gla":
                            for kt in range(4):
                                e.wait_ge(gnorm_done, kt + 1)
                                e.activation(in_hi[:, kt, :], gla_o[:, kt, :], ACT.Copy).then_inc(split_hi, 1)
                        else:
                            e.wait_ge(free(("so",)), emptied(("so",)))
                            e.wait_ge(free(("oT", 3)), emptied(("oT", 3)))
                            for kt in range(4, KD):
                                e.activation(in_hi[:, kt, :], attn_t[:, kt - 4, :], ACT.Copy).then_inc(split_hi, 1)
                    elif kind == "kcT":
                        b = step[1]
                        if b == 0:
                            e.wait_ge(masks_done, 4)
                        if b >= 2:
                            if b % 2 == 0:
                                e.wait_ge(k_past_used, b // 2)
                            else:
                                e.wait_ge(ready(("slog", b // 2 - 1)), filled(("slog", b // 2 - 1)))
                        e.wait_ge(ready(("kcT", b)), filled(("kcT", b)))
                        e.activation(k_past[:, b % 2, :, :].rearrange("p a n -> p (a n)"),
                                     aux[:, 1 + b % 2, :], ACT.Copy).then_inc(free(("kcT", b)), 1)
                    elif kind == "slog" and step[1] % 2 == 1:
                        i = step[1] // 2
                        e.wait_ge(max_done, i + 1)
                        if i >= 2:
                            e.wait_ge(ready(("spT", i - 2)), filled(("spT", i - 2)))
                        e.activation(p_t[:, i % 2, 0:NEW_KEYS], aux[:, uses["slog", i][0], 0:NEW_KEYS], ACT.Exp,
                                     bias=neg_max_s[:, i:i + 1], accum_out=p_sum_s[:,
                                                                                                         i:i + 1]).then_inc(free(("slog", i)), 1)
                    elif kind == "sample_out":
                        e.wait_ge(ready(("so",)), filled(("so",)))
                        e.wait_ge(gnorm_done, GH)
                        for jj in range(4):
                            src = slice(64 * (jj // 2), 64 * (jj // 2) + 64)
                            dst = slice(64 * (jj % 2), 64 * (jj % 2) + 64)
                            for pair in range(2):
                                ins = e.activation(
                                    attn_t[dst, jj // 2 + 2 * pair, SEQ:NT].rearrange("p (b t) -> p b t", t=DEC_SEQ),
                                    aux[src, 3, :].rearrange("p (b a q t) -> p b a q t", b=8, a=2, q=4)[:, :, pair, jj, :],
                                    ACT.Copy)
                        ins.then_inc(free(("so",)), 1)
                    elif kind == "attn":
                        _, j, h = step
                        n = j * N_HEADS + h
                        L = (j + 1) * P
                        if n == 0:
                            e.wait_ge(ready(("spT", 3)), filled(("spT", 3)))
                            exp_head(0)
                        e.wait_ge(ready(("pT", j, h)), filled(("pT", j, h)))
                        if n >= 2:
                            e.wait_ge(*pv_used(n - 2))
                        e.activation(pT_t[:, n % 2, 0:j + 1, :].rearrange("p s n -> p (s n)"), aux[:, 2, 0:L],
                                     ACT.Copy).then_inc(free(("pT", j, h)), 1)
                        if n + 1 < len(ORDER):
                            exp_head(n + 1)
                    elif kind == "attn_t":
                        j = step[1]
                        e.wait_ge(ready(("oT", j)), filled(("oT", j)))
                        e.activation(attn_t[:, :, j * P:(j + 1) * P], aux[:, 2, :].rearrange("p (m n) -> p m n", m=4),
                                     ACT.Copy).then_inc(free(("oT", j)), 1)

            layers(e, body)

        @block.vector
        def _(e):
            e.memset(ones[:], 1.0).then_inc(once, 1)
            e.memset(eps_t[:], EPS).then_inc(once, 1)
            e.wait_ge(x_loaded, 16 * (3 + NTILE))
            e.tensor_copy(ident_b[:], ident).then_inc(once, 1)
            e.tensor_copy(tri_b[:], const("tri")).then_inc(once, 1)
            e.tensor_copy(repeat_b[:].rearrange("p b n -> p (b n)"), repeat_f[0:NS, :]).then_inc(once, 1)
            for kt in range(KD):
                e.wait_ge(x_turned, kt + 1)
                b0 = 2 * (kt % 2)
                e.tensor_copy(x_t[:, kt, 0:SEQ], aux[:, b0, :])
                e.tensor_copy(x_t[:, kt, SEQ:NT], aux[:, b0 + 1, 0:NS]).then_inc(x_filled, 1)

            def body(layer):
                turn = counter()

                def low_part(key, dst, src, hi):
                    e.wait_ge(split_hi, plan.split_use[key] + 1)
                    e.tensor_tensor(dst, src, hi.bitcast(F32), ALU.subtract).then_inc(split_lo, 1)
                    e.wait_ge(split_lo, plan.split_use[key] + 1)

                def norm_and_turn(u):
                    part, t = plan.norm_order[u]
                    n = tile_rows(t)
                    x3, first, heads, gain, turned = norm_rows(part, t)
                    cos = const("cos")[0:n, t * ROT:(t + 1) * ROT]
                    sin = const("sin")[0:n, t * ROT:(t + 1) * ROT]
                    e.wait_ge(rows_std, u + 1)
                    e.tensor_tensor(x3, x3, bcast(sums[0:n, u % 2, 0:heads], 2, HD), ALU.mult).then_inc(dve_step, 1)
                    e.wait_ge(dve_step, turn(dve_step))
                    e.tensor_tensor(x3, x3, bcast(qk_g[0:n, gain, :], 1, heads), ALU.mult).then_inc(dve_step, 1)
                    e.wait_ge(dve_step, turn(dve_step))
                    nh = turned.shape[1]
                    e.tensor_tensor(rope1[0:n, 0:nh, :], turned[:, :, 0:ROT], bcast(cos, 1, nh), ALU.mult)
                    e.tensor_tensor(rope2[0:n, 0:nh, 0:HALF_ROT], turned[:, :, HALF_ROT:ROT],
                                    bcast(sin[:, 0:HALF_ROT], 1, nh), ALU.mult)
                    e.tensor_tensor(rope2[0:n, 0:nh, HALF_ROT:ROT], turned[:, :, 0:HALF_ROT],
                                    bcast(sin[:, HALF_ROT:ROT], 1, nh), ALU.mult).then_inc(dve_step, 1)
                    e.wait_ge(dve_step, turn(dve_step))
                    raised = rows_done if part == "x" else dve_step
                    e.tensor_tensor(turned[:, :, 0:ROT], rope1[0:n, 0:nh, :], rope2[0:n, 0:nh, :],
                                    ALU.add).then_inc(raised, 1)
                    e.wait_ge(raised, turn(raised))

                def max_head(n):
                    j, h = ORDER[n]
                    L = (j + 1) * P
                    key = ("log", j, h)
                    e.wait_ge(ready(key), filled(key))
                    e.tensor_reduce(neg_max[:, j % 2, h:h + 1], aux[:, uses[key][0], 0:L], AX_X, ALU.max,
                                        negate=True).then_inc(max_done, 1)
                    e.wait_ge(max_done, turn(max_done))

                for step in plan.steps:
                    kind = step[0]
                    if kind == "post":
                        p = step[1]
                        kind_p, idx, _ = PANELS[p]
                        g = plan.groups[p][0]
                        key = ("g", g)
                        src = slot(g)
                        if kind_p in STAGED:
                            pass
                        elif kind_p == "gr":
                            u = plan.gate_tmp_use["gr", idx]
                            e.wait_ge(gated, gated_no["gr", idx])
                            e.tensor_tensor(halves(gla_r[:, idx, :]), src, halves(gate_tmp[:, u % 2, :]),
                                            ALU.mult).then_inc(free(key), 1)
                            e.wait_ge(free(key), emptied(key))
                        elif kind_p == "oab":
                            for gate, gg in ((gate_b, g), (gate_a, g + 1)):
                                k2 = ("g", gg)
                                e.wait_ge(gates_done, 2 * idx + 1 + (gate is gate_a))
                                e.wait_ge(ready(k2), filled(k2))
                                e.tensor_tensor(halves(gate[:, idx, :]), slot(gg), halves(gate[:, idx, :]),
                                                    ALU.mult).then_inc(free(k2), 1)
                                e.wait_ge(free(k2), emptied(k2))
                            u = plan.split_use["merge", idx] % 2
                            e.wait_ge(free(("g", g)), emptied(("g", g)))
                            e.tensor_tensor(tmp[:, u, :], gate_a[:, idx, :], gate_b[:, idx, :],
                                            ALU.add).then_inc(split_src, 1)
                            e.wait_ge(split_src, plan_src["merge", idx])
                            low_part(("merge", idx), mid_lo[:, idx, :], tmp[:, u, :], mid_hi[:, idx, :])
                        elif kind_p in ("o", "down"):
                            m = idx if kind_p == "o" else idx[1]
                            e.wait_ge(ready(key), filled(key))
                            e.tensor_tensor(halves(x_t[:, m, :]), src, halves(x_t[:, m, :]),
                                            ALU.add).then_inc(free(key), 1)
                            e.wait_ge(free(key), emptied(key))
                        elif kind_p == "gate":
                            u = plan.gate_tmp_use["gate", idx]
                            v = plan.split_use["ff", idx] % 2
                            e.wait_ge(gated, gated_no["gate", idx])
                            e.tensor_tensor(halves(tmp[:, v, :]), src, halves(gate_tmp[:, u % 2, :]),
                                            ALU.mult).then_inc(free(key), 1)
                            e.wait_ge(free(key), emptied(key))
                        elif kind_p == "up":
                            part, i = idx
                            v = plan.split_use["ff", idx] % 2
                            e.wait_ge(ready(key), filled(key))
                            e.wait_ge(free(("g", g - 1)), emptied(("g", g - 1)))
                            e.tensor_tensor(halves(tmp[:, v, :]), src, halves(tmp[:, v, :]),
                                            ALU.mult).then_inc(free(key), 1)
                            e.wait_ge(free(key), emptied(key))
                            k = i - sum(FF_PARTS[:part])
                            low_part(("ff", idx), mid_lo[:, k, :], tmp[:, v, :], mid_hi[:, k, :])
                    elif kind == "stat" and step[2] > 0:
                        _, norm, kt = step
                        squares = gate_tmp[:, plan.gate_tmp_use["squares", norm] % 2, :]
                        use = plan.stage_use["stat", norm, kt]
                        if kt == 1:
                            e.wait_ge(squares_ready, norm)
                        e.wait_ge(staged, use + 1)
                        e.tensor_tensor(squares, squares, stage[:, use % 2, :], ALU.add).then_inc(squares_added, 1)
                        e.wait_ge(squares_added, turn(squares_added))
                    elif kind == "gains":
                        e.wait_ge(ready(("gains",)), filled(("gains",)))
                        e.tensor_copy(gains[:], aux[:, 2, 0:2 * KD + 1]).then_inc(free(("gains",)), 1)
                        e.wait_ge(free(("gains",)), emptied(("gains",)))
                    elif kind == "norm":
                        norm = step[1]
                        e.wait_ge(rstd_done, norm)
                        e.wait_ge(small_ready, 16 * SMALL_LOADS)
                        for kt in range(0, KD + 2):
                            if kt < KD and kt % 2 == 0:
                                e.tensor_tensor(normed[:, kt, :], x_t[:, kt, :], rstd[:],
                                                ALU.mult).then_inc(split_src, 1)
                            if kt >= 2:
                                key = ("norm", norm, kt - 2)
                                gain = (norm - 1) * KD + kt - 2
                                e.wait_ge(split_hi, plan.split_use[key] + 1)
                                e.scalar_tensor_tensor(out=in_lo[:, kt - 2, :], in0=normed[:, kt - 2, :],
                                                       scalar=gains[:, gain:gain + 1],
                                                       in1=in_hi[:, kt - 2, :].bitcast(F32), op0=ALU.mult,
                                                       op1=ALU.subtract).then_inc(split_lo, 1)
                        e.wait_ge(split_lo, plan.split_use["norm", norm, KD - 1] + 1)
                    elif kind == "row":
                        p = step[1]
                        kind_p, idx, _ = PANELS[p]
                        bx, by = uses["rowX", p][0], uses["rowY", p][0]
                        if kind_p == "gv":
                            buf, lo, w, src0 = gv_rows, idx * P, P, 0
                        elif kind_p == "q":
                            buf, lo, w, src0 = q_rows, idx * P, P, 0
                        elif kind_p in ("k", "v"):
                            buf, lo, w, src0 = kv_rows, idx * P + (KV_W if kind_p == "v" else 0), P, 0
                        elif kind_p == "qi":
                            buf, lo, w, src0 = q_rows, ATTN_W + idx * P, P, 0
                        else:
                            buf, lo, w, src0 = q_rows, ATTN_W + IDX_W, ID, MISC_KI
                        x3 = aux[:, bx, :].rearrange("p (t n) -> p t n", t=4)
                        if kind_p == "q":
                            at0 = HEAD_TILE[2 * idx][0] * 2 + HEAD_TILE[2 * idx][1]
                            heads = q_rows[:, :, 0:ATTN_W].rearrange("p t (h d) -> p t h d", d=HD)
                            e.wait_ge(ready(("rowX", p)), filled(("rowX", p)))
                            e.tensor_copy(heads[:, 0:4, at0:at0 + 3:2, :],
                                              x3.rearrange("p t (h d) -> p t h d",
                                                           d=HD)).then_inc(free(("rowX", p)), 1)
                            e.wait_ge(free(("rowX", p)), emptied(("rowX", p)))
                            e.wait_ge(ready(("rowY", p)), filled(("rowY", p)))
                            e.tensor_copy(heads[0:NS, 4, at0:at0 + 3:2, :],
                                              aux[0:NS, by, 0:P].rearrange("p (h d) -> p h d",
                                                                           d=HD)).then_inc(free(("rowY", p)), 1)
                            e.wait_ge(free(("rowY", p)), emptied(("rowY", p)))
                            continue
                        e.wait_ge(ready(("rowX", p)), filled(("rowX", p)))
                        if kind_p == "misc":
                            e.tensor_copy(wi_rows[:, 0:4, :],
                                          x3[:, :, MISC_WI:MISC_WI + IDX_HEADS]).then_inc(dve_step, 1)
                            e.wait_ge(dve_step, turn(dve_step))
                        e.tensor_copy(buf[:, 0:4, lo:lo + w], x3[:, :, src0:src0 + w]).then_inc(free(("rowX", p)), 1)
                        e.wait_ge(free(("rowX", p)), emptied(("rowX", p)))
                        e.wait_ge(ready(("rowY", p)), filled(("rowY", p)))
                        if kind_p == "misc":
                            e.tensor_copy(wi_rows[0:NS, 4, :],
                                          aux[0:NS, by, MISC_WI:MISC_WI + IDX_HEADS]).then_inc(dve_step, 1)
                            e.wait_ge(dve_step, turn(dve_step))
                        e.tensor_copy(buf[0:NS, 4, lo:lo + w],
                                      aux[0:NS, by, src0:src0 + w]).then_inc(free(("rowY", p)), 1)
                        e.wait_ge(free(("rowY", p)), emptied(("rowY", p)))
                    elif kind == "qn":
                        _, part, t = step
                        u = plan.norm_order.index((part, t))
                        n = tile_rows(t)
                        heads = norm_rows(part, t)[2]
                        e.wait_ge(rows_sq, u + 1)
                        e.tensor_reduce(sums[0:n, u % 2, 0:heads], sq_rows[0:n, 0:heads, :], AX_X,
                                        ALU.add).then_inc(rows_ss, 1)
                        if u:
                            norm_and_turn(u - 1)
                    elif kind == "qn_end":
                        norm_and_turn(len(plan.norm_order) - 1)
                    elif kind == "qkT":
                        t = step[1]
                        n = tile_rows(t)
                        key = ("ik", t)
                        e.wait_ge(ready(key), filled(key))
                        v = aux[:, 1, :].rearrange("p (m n) -> p m n", m=4)
                        e.tensor_copy(qi_t[:, :, token_slice(t)], v[:, 0:2, 0:n]).then_inc(dve_step, 1)
                        e.wait_ge(dve_step, turn(dve_step))
                        e.tensor_copy(k_t[:, :, token_slice(t)], v[:, 2:4, 0:n]).then_inc(free(key), 1)
                        e.wait_ge(free(key), emptied(key))
                    elif kind == "z":
                        for i in range(3):
                            n = tile_rows(2 * i)
                            tiles = min(2, NTILE - 2 * i)
                            dst = la[0:n, 2 * i:2 * i + tiles, :].rearrange("p t n -> p (t n)")
                            e.wait_ge(ln_done, i + 1)
                            e.scalar_tensor_tensor(out=dst, in0=aux[0:n, uses["z", i][0], 0:tiles * GK_W],
                                                       scalar=0.0, in1=dst, op0=ALU.min, op1=ALU.subtract).then_inc(free(("z", i)), 1)
                            e.wait_ge(free(("z", i)), emptied(("z", i)))
                    elif kind == "decay":
                        for i in range(3):
                            if i < 2:
                                v = aux[:, i, :].rearrange("p (c s) -> p c s", s=CHUNK)
                                ref, end = b_ref[:, i, 0:16], b_end[:, i, 0:16]
                                mid, last = CHUNK // 2 - 1, CHUNK - 1
                                dst = d_t[:, i, 0:SEQ].rearrange("p (c s) -> p c s", s=CHUNK)
                                rb = bcast(ref, 2, CHUNK)
                                e.wait_ge(ready(("b", i)), filled(("b", i)))
                                e.tensor_copy(ref, v[:, :, mid]).then_inc(dve_step, 1)
                                e.wait_ge(dve_step, turn(dve_step))
                                e.tensor_copy(end, v[:, :, last]).then_inc(dve_step, 1)
                                e.wait_ge(dve_step, turn(dve_step))
                                e.tensor_tensor(dst, v, rb, ALU.subtract).then_inc(free(("b", i)), 1)
                                e.wait_ge(free(("b", i)), emptied(("b", i)))
                            else:
                                e.wait_ge(ready(("b", 2)), filled(("b", 2)))
                                for hp in range(2):
                                    v = aux[:, 2, hp * NS:(hp + 1) * NS].rearrange("p (c s) -> p c s", s=DEC_SEQ)
                                    e.tensor_copy(b_ref[:, hp, 16:24],
                                                  v[:, :, DEC_SEQ // 2 - 1]).then_inc(dve_step, 1)
                                    e.wait_ge(dve_step, turn(dve_step))
                                    e.tensor_copy(b_end[:, hp, 16:24], v[:, :, DEC_SEQ - 1]).then_inc(dve_step, 1)
                                    e.wait_ge(dve_step, turn(dve_step))
                                for hp in range(2):
                                    v = aux[:, 2, hp * NS:(hp + 1) * NS].rearrange("p (c s) -> p c s", s=DEC_SEQ)
                                    dst = d_t[:, hp, SEQ:NT].rearrange("p (c s) -> p c s", s=DEC_SEQ)
                                    rb = bcast(b_ref[:, hp, 16:24], 2, DEC_SEQ)
                                    if hp == 0:
                                        e.tensor_tensor(dst, v, rb, ALU.subtract).then_inc(dve_step, 1)
                                        e.wait_ge(dve_step, turn(dve_step))
                                    else:
                                        e.tensor_tensor(dst, v, rb, ALU.subtract).then_inc(free(("b", 2)), 1)
                                        e.wait_ge(free(("b", 2)), emptied(("b", 2)))
                        e.tensor_tensor(e_add[:], b_end[:], b_ref[:], ALU.subtract).then_inc(decay_done, 1)
                        e.wait_ge(decay_done, turn(decay_done))
                    elif kind == "qiz":
                        e.wait_ge(free(("ik", 4)), emptied(("ik", 4)))
                        for h in range(IDX_HEADS):
                            src = qi_t[64 * (h % 2):64 * (h % 2) + 64, h // 2, SEQ:NT]
                            raised = qiz_done if h == IDX_HEADS - 1 else dve_step
                            e.tensor_copy(qiz[:, :, h * DEC_SEQ:(h + 1) * DEC_SEQ],
                                              src.rearrange("p (b t) -> p b t", t=DEC_SEQ)).then_inc(raised, 1)
                            e.wait_ge(raised, turn(raised))
                        for g in range(2):
                            e.wait_ge(ready(("wi", g)), filled(("wi", g)))
                            e.tensor_tensor_reduce(out=wi_tmp[:, g, :], in0=aux[:, uses["wi", g][0], 0:IDX_HEADS],
                                                       in1=const("head_rows"), scale=IDX_SCALE, scalar=0.0,
                                                       op0=ALU.mult, op1=ALU.add, accum_out=wi_s[:,
                                                                                                                       g:g + 1]).then_inc(free(("wi", g)), 1)
                            e.wait_ge(free(("wi", g)), emptied(("wi", g)))
                    elif kind == "kidx":
                        g = step[1]
                        e.wait_ge(ready(("sscore", g)), filled(("sscore", g)))
                        e.wait_ge(free(("wi", g)), emptied(("wi", g)))
                        e.tensor_scalar(s_heads[:, g, :], aux[:, 2, 0:NEW_KEYS], 0.0, wi_s[:, g:g + 1],
                                            ALU.max, ALU.mult).then_inc(free(("sscore", g)), 1)
                        e.wait_ge(free(("sscore", g)), emptied(("sscore", g)))
                    elif kind == "sindex":
                        e.memset(scores_s[:, NEW_KEYS:SAMPLE_W], -MASKED).then_inc(dve_step, 1)
                        e.wait_ge(dve_step, turn(dve_step))
                        e.wait_ge(ready(("ssum",)), filled(("ssum",)))
                        e.tensor_copy(scores_s[:, 0:PAST], aux[0:NS, 3, 0:PAST]).then_inc(dve_step, 1)
                        e.wait_ge(dve_step, turn(dve_step))
                        e.tensor_tensor(scores_s[:, PAST:NEW_KEYS], aux[0:NS, 3, PAST:NEW_KEYS],
                                            const("own_new", NS), ALU.add).then_inc(free(("ssum",)), 1)
                        e.wait_ge(free(("ssum",)), emptied(("ssum",)))
                    elif kind == "index":
                        j = step[1]
                        L = (j + 1) * P
                        lo, hi = score_cols[j]
                        acc = scores[:, lo:hi]
                        for h in range(IDX_HEADS):
                            key = ("index", j, h)
                            src = gate_tmp[:, plan.gate_tmp_use[key] % 2, 0:L]
                            e.wait_ge(free(key), emptied(key))
                            if h == 0:
                                e.tensor_scalar(acc, src, wi_rows[:, j, 0:1], None, ALU.mult).then_inc(index_added, 1)
                                e.wait_ge(index_added, turn(index_added))
                            else:
                                e.scalar_tensor_tensor(out=acc, in0=src, scalar=wi_rows[:, j, h:h + 1], in1=acc,
                                                           op0=ALU.mult, op1=ALU.add).then_inc(index_added, 1)
                                e.wait_ge(index_added, turn(index_added))
                        e.tensor_tensor(acc[:, L - P:L], acc[:, L - P:L], const("tri"), ALU.add).then_inc(dve_step, 1)
                        e.wait_ge(dve_step, turn(dve_step))
                    elif kind == "topk":
                        _, w, r = step
                        if w == "s":
                            buf, t8, out, last = scores_s[:], top8s, mask_s[:], (TOPK_SAMPLE + PAD_TOP) // 8 - 1
                            width = NEW_KEYS
                        else:
                            lo, hi = score_cols[w]
                            buf, t8, last, width = scores[:, lo:hi], top8, TOPK_PROMPT // 8 - 1, (w + 1) * P
                            out = mask_b[:, w - 1, 0:width]
                        e.max(out=t8[0:buf.shape[0], :], in_=buf).then_inc(dve_step, 1)
                        e.wait_ge(dve_step, turn(dve_step))
                        e.match_replace(out=buf, in_to_replace=t8[0:buf.shape[0], :], in_values=buf,
                                            imm_value=TAKEN).then_inc(dve_step, 1)
                        e.wait_ge(dve_step, turn(dve_step))
                        if r == last:
                            e.tensor_scalar(out, buf[:, 0:width], TAKEN / 1.5, MASKED, ALU.is_gt,
                                            ALU.mult).then_inc(masks_done, 1)
                            e.wait_ge(masks_done, turn(masks_done))
                    elif kind == "kT":
                        t = step[1]
                        n = tile_rows(t)
                        e.wait_ge(ready(("kT", t)), filled(("kT", t)))
                        e.tensor_copy(gk_rows[0:n, t % 2, :], aux[0:n, 2, 0:GK_W]).then_inc(free(("kT", t)), 1)
                        e.wait_ge(free(("kT", t)), emptied(("kT", t)))
                    elif kind == "intra":
                        t = step[1]
                        n = tile_rows(t)
                        if t == 4:
                            e.wait_ge(ready(("inE", t)), filled(("inE", t)))
                            e.memset(g_attn[0:NS, :, :], 0.0).then_inc(dve_step, 1)
                            e.wait_ge(dve_step, turn(dve_step))
                        for par, key in enumerate((("inE", t), ("inO", t))):
                            causal = const("chunk_sum") if t < 4 else const("sample_sum", NS)
                            src = aux[0:n, uses[key][0], 0:2 * P].rearrange("p (g n) -> p g n", g=2)[:, :, 0:n]
                            e.wait_ge(ready(key), filled(key))
                            e.copy_predicated(out=g_attn[0:n, par::2, 0:n], mask=bcast(causal, 1, 2).bitcast(U32),
                                                  data=src).then_inc(free(key), 1)
                            e.wait_ge(free(key), emptied(key))
                    elif kind == "chunk":
                        c = step[1]
                        key = ("kv", c)
                        ps = aux[:, 2, 0:2 * DV].rearrange("p (g n) -> p g n", g=2)
                        e.wait_ge(ready(key), filled(key))
                        for hp in range(2):
                            if c == 0:
                                ins = e.tensor_scalar(state[:, hp, :], ps[:, hp, :], e_add[:, hp, c:c + 1], None, ALU.mult)
                            else:
                                if hp == 0:
                                    e.wait_ge(decayed, c)
                                ins = e.scalar_tensor_tensor(out=state[:, hp, :], in0=ps[:, hp, :],
                                                             scalar=e_add[:, hp, c:c + 1], in1=state_add[:, hp, :],
                                                             op0=ALU.mult, op1=ALU.add)
                            if hp == 0:
                                ins.then_inc(dve_step, 1)
                                e.wait_ge(dve_step, turn(dve_step))
                            else:
                                ins.then_inc(free(key), 1)
                                e.wait_ge(free(key), emptied(key))
                    elif kind == "sround":
                        r = step[1]

                        st = s_state[:, r % 2, :, :, :]
                        e.wait_ge(s_decayed, r + 1)
                        e.wait_ge(ready(("skv", r)), filled(("skv", r)))
                        ps = aux[:, 2, :].rearrange("p (b g n) -> p b g n", b=2, g=2)
                        e.tensor_tensor(s_state_add[:], ps, per_batch(e_add, r),
                                        ALU.mult).then_inc(free(("skv", r)), 1)
                        e.wait_ge(free(("skv", r)), emptied(("skv", r)))
                        e.tensor_tensor(st, st, s_state_add[:], ALU.add).then_inc(s_out_done, 1)
                        e.wait_ge(s_out_done, turn(s_out_done))
                    elif kind == "gnorm":
                        h = step[1]
                        root = gate_tmp[:, plan.gate_tmp_use["gn", h] % 2, :]
                        e.wait_ge(gn_root, h + 1)
                        e.scalar_tensor_tensor(out=gla_o[:, h, :], in0=gla_o[:, h, :], scalar=gains[:, 2 * KD:2 * KD + 1],
                                                   in1=root, op0=ALU.mult, op1=ALU.mult).then_inc(dve_step, 1)
                        e.wait_ge(dve_step, turn(dve_step))
                        e.tensor_tensor(gla_o[:, h, :], gla_o[:, h, :], gla_r[:, h, :],
                                        ALU.mult).then_inc(gnorm_done, 1)
                        e.wait_ge(gnorm_done, turn(gnorm_done))
                    elif kind == "mix":
                        for kt in range(4) if step[1] == "gla" else range(4, KD):
                            src = gla_o[:, kt, :] if kt < 4 else attn_t[:, kt - 4, :]
                            low_part(("mix", kt), in_lo[:, kt, :], src, in_hi[:, kt, :])
                    elif kind == "qz":
                        e.wait_ge(state_stored, 16 * 2)
                        e.wait_ge(s_stored, 16 * 2 * DEC_BATCH)
                        e.wait_ge(ready(("oO", 4)), filled(("oO", 4)))
                        e.memset(qz[:], 0.0).then_inc(dve_step, 1)
                        e.wait_ge(dve_step, turn(dve_step))
                        for h in range(N_HEADS):
                            tile, half = HEAD_TILE[h]
                            rows = slice(64 * half, 64 * half + 64)
                            if h == 0:
                                e.wait_ge(free(("q", 4)), emptied(("q", 4)))
                            raised = qz_done if h == N_HEADS - 1 else dve_step
                            e.tensor_copy(qz[rows, :, h // 4, h * DEC_SEQ:(h + 1) * DEC_SEQ],
                                              q_t[rows, tile, SEQ:NT].rearrange("p (b t) -> p b t",
                                                                                t=DEC_SEQ)).then_inc(raised, 1)
                            e.wait_ge(raised, turn(raised))
                    elif kind == "slog" and step[1] % 2 == 1:
                        i = step[1] // 2
                        e.wait_ge(ready(("slog", i)), filled(("slog", i)))
                        e.tensor_reduce(neg_max_s[:, i:i + 1], aux[:, uses["slog", i][0], 0:NEW_KEYS], AX_X,
                                            ALU.max, negate=True).then_inc(max_done, 1)
                        e.wait_ge(max_done, turn(max_done))
                        e.wait_ge(free(("slog", i)), emptied(("slog", i)))
                        e.reciprocal(p_inv_s[:, i:i + 1], p_sum_s[:, i:i + 1]).then_inc(dve_step, 1)
                        e.wait_ge(dve_step, turn(dve_step))
                        e.tensor_scalar(p_t[:, i % 2, 0:NEW_KEYS], p_t[:, i % 2, 0:NEW_KEYS],
                                            p_inv_s[:, i:i + 1], None, ALU.mult).then_inc(p_scaled, 1)
                        e.wait_ge(p_scaled, turn(p_scaled))
                    elif kind == "spT":
                        i = step[1]
                        if i >= 2:
                            e.wait_ge(kc_free, 2 * i - 2)
                        e.wait_ge(ready(("spT", i)), filled(("spT", i)))
                        e.tensor_copy(pT_t[:, i % 2, 0:2, :],
                                      aux[:, 2, 0:2 * P].rearrange("p (s n) -> p s n", s=2)).then_inc(dve_step, 1)
                        e.wait_ge(dve_step, turn(dve_step))
                        e.tensor_copy(pT_t[0:NS, i % 2, 2, :],
                                      aux[0:NS, 2, 2 * P:3 * P]).then_inc(free(("spT", i)), 1)
                        e.wait_ge(free(("spT", i)), emptied(("spT", i)))
                    elif kind == "attn":
                        _, j, h = step
                        n = j * N_HEADS + h
                        L = (j + 1) * P
                        if n == 0:
                            max_head(0)
                        if n + 1 < len(ORDER):
                            max_head(n + 1)
                    elif kind == "attn_out":
                        j = step[1]
                        e.wait_ge(ready(("o", j)), filled(("o", j)))
                        e.reciprocal(p_inv[:], p_sum[:, j % 2, :]).then_inc(dve_step, 1)
                        e.wait_ge(dve_step, turn(dve_step))
                        e.tensor_tensor(o_rows[:].rearrange("p (h d) -> p h d", d=HD),
                                            aux[:, 3, :].rearrange("p (h d) -> p h d", d=HD), bcast(p_inv[:], 2, HD),
                                            ALU.mult).then_inc(free(("o", j)), 1)
                        e.wait_ge(free(("o", j)), emptied(("o", j)))

            layers(e, body)
            for t in range(NTILE):
                e.wait_ge(y_turned, t + 1)
                n = tile_rows(t)
                for k in range(2):
                    e.tensor_copy(x_rows[0:n, t, k * 512:(k + 1) * 512],
                                  aux[0:n, 2 * (t % 2) + k, :]).then_inc(y_ready, 1)



_INS = ["x_prompt", "x_sample", "cache_k", "cache_v", "cache_kidx", "state_gla", "page_table", "norm1_g", "w_in",
        "q_norm_g", "k_norm_g", "kidx_norm_g", "gla_wa2", "gla_ba", "gla_onorm_g", "w_oa", "w_ob", "w_o", "norm2_g",
        "w_ffn_gu", "w_ffn_down"]
_OUTS = {
    "y_prompt": (1, SEQ, D_MODEL), "y_sample": (DEC_BATCH, DEC_SEQ, D_MODEL),
    "new_k_prompt": (DEPTH, 1, SEQ, N_KV, HD), "new_v_prompt": (DEPTH, 1, SEQ, N_KV, HD),
    "new_kidx_prompt": (DEPTH, 1, SEQ, ID), "new_gla_prompt": (DEPTH, 1, GH, DK, DV),
    "new_k_sample": (DEPTH, DEC_BATCH, DEC_SEQ, N_KV, HD), "new_v_sample": (DEPTH, DEC_BATCH, DEC_SEQ, N_KV, HD),
    "new_kidx_sample": (DEPTH, DEC_BATCH, DEC_SEQ, ID), "new_gla_sample": (DEPTH, DEC_BATCH, GH, DK, DV),
}


def kernel(**inputs):
    import concourse.bacc as bacc
    from concourse.bass_utils import run_bass_kernel_spmd

    nc = bacc.Bacc("TRN2", target_bir_lowering=False, num_devices=1, dynamic_dma_scratch_size=64)
    arrays, args = {}, {}
    for name in _INS:
        a = np.ascontiguousarray(inputs[name])
        arrays[f"in_{name}"] = a
        args[name] = nc.dram_tensor(f"in_{name}", a.shape, mybir.dt.from_np(a.dtype), kind="ExternalInput").ap()
    consts = const_array()
    arrays["in_consts"] = consts
    args["consts"] = nc.dram_tensor("in_consts", consts.shape, F32, kind="ExternalInput").ap()
    for name, shape in _OUTS.items():
        args[name] = nc.dram_tensor(f"out_{name}", shape, F32, kind="ExternalOutput").ap()
    build(nc, args)
    r = run_bass_kernel_spmd(nc, [arrays], core_ids=[0])
    return tuple(r.results[0][f"out_{name}"] for name in _OUTS)
```
